# Optimizing a Trainium2 kernel written in Bass

```python
import jax, jax.numpy as jnp
from jax import lax
import numpy as np

D_MODEL = 1024
BATCH = 1
SEQ = 128
DEPTH = 2
DEC_BATCH = 1
DEC_SEQ = 256
PAST_LEN = 128

GRID_W = 64
HEAD_DIM = 64
NA_HEADS = 4
NA_WIN_H = 8
NA_WIN_W = 16
NA_QBLOCK = 16
NA_KBLOCK = NA_QBLOCK + NA_WIN_W
RW_HEADS = 4
RW_DIM = RW_HEADS * HEAD_DIM
DECAY_LORA = 64
ICLR_LORA = 64
GATE_LORA = 128
GN_EPS = 64e-5
MLA_HEADS = 4
Q_LORA = 256
KV_LORA = 128
NOPE_DIM = 64
ROPE_DIM = 32
V_DIM = 64
MLA_SCALE = (NOPE_DIM + ROPE_DIM) ** -0.5
ROPE_BASE = 10000.0
N_BRANCH = 3
BRANCH_DIM = 256
D_FF = 2816
N_MOD = 9
NORM_EPS = 1e-6
ATTN_QBLOCK = 128
NEG_INF = -1e30
IN_SIZES = (NA_HEADS * HEAD_DIM,) * 3 + (RW_DIM,) * 3 + (DECAY_LORA, DECAY_LORA, ICLR_LORA, ICLR_LORA, GATE_LORA, Q_LORA, KV_LORA, ROPE_DIM, N_BRANCH * D_MODEL)
IN_COLS = sum(IN_SIZES)

kernel_name = 'hybrid_na_rwkv7_mla_flow_step'

def _rmsnorm(x, g):
    xf = x.astype(jnp.float32)
    y = xf * lax.rsqrt(jnp.mean(xf * xf, axis=-1, keepdims=True) + NORM_EPS)
    return (y * g.astype(jnp.float32)).astype(x.dtype)

def _swiglu(h, wg, wu, wd):
    return (jax.nn.silu(h @ wg) * (h @ wu)) @ wd

def _heads(z, n):
    b, t, _ = z.shape
    return z.reshape(b, t, n, -1).transpose(0, 2, 1, 3)

def _merge(z):
    b, h, t, d = z.shape
    return z.transpose(0, 2, 1, 3).reshape(b, t, h * d)

def _split_cols(z):
    idx, acc = [], 0
    for s in IN_SIZES[:-1]:
        acc += s
        idx.append(acc)
    return jnp.split(z, idx, axis=-1)

def _axial_rope(t_len, dim):
    n_freq = dim // 4
    inv = 1.0 / (ROPE_BASE ** (np.arange(n_freq) / n_freq))
    pos = np.arange(t_len)
    ang = np.concatenate([(pos // GRID_W)[:, None] * inv, (pos % GRID_W)[:, None] * inv], axis=-1)
    return jnp.asarray(np.cos(ang), jnp.float32), jnp.asarray(np.sin(ang), jnp.float32)

def _rope(x, cos, sin):
    half = x.shape[-1] // 2
    x1, x2 = x[..., :half], x[..., half:]
    cos = cos.astype(x.dtype)
    sin = sin.astype(x.dtype)
    return jnp.concatenate([x1 * cos - x2 * sin, x1 * sin + x2 * cos], axis=-1)

def _block_attention(q, k, v, scale):
    b, h, tq, dk = q.shape
    qbs = min(ATTN_QBLOCK, tq)
    nblk = tq // qbs
    qb = (q * scale).reshape(b, h, nblk, qbs, dk).transpose(2, 0, 1, 3, 4)

    def one(qi):
        s = jnp.einsum('bhqd,bhkd->bhqk', qi, k).astype(jnp.float32)
        p = jax.nn.softmax(s, axis=-1).astype(v.dtype)
        return jnp.einsum('bhqk,bhkd->bhqd', p, v)

    o = lax.map(one, qb)
    return o.transpose(1, 2, 0, 3, 4).reshape(b, h, tq, v.shape[-1])

def _na_latent(q, k, v, k_ctx, v_ctx, rpb):
    b, h, t, d = q.shape
    rows = t // GRID_W
    kh = min(NA_WIN_H, rows)
    nb = GRID_W // NA_QBLOCK
    qcol = np.arange(GRID_W).reshape(nb, NA_QBLOCK)
    col_lo = np.clip(qcol - NA_WIN_W // 2, 0, GRID_W - NA_WIN_W)
    blk_lo = np.clip(np.arange(nb) * NA_QBLOCK - NA_WIN_W // 2, 0, GRID_W - NA_KBLOCK)
    key_col = blk_lo[:, None] + np.arange(NA_KBLOCK)[None, :]
    kc = key_col[:, None, :]
    col_ok = (kc >= col_lo[..., None]) & (kc < col_lo[..., None] + NA_WIN_W)
    col_idx = np.clip(kc - qcol[..., None] + NA_WIN_W - 1, 0, 2 * NA_WIN_W - 2)
    row_lo = np.clip(np.arange(rows) - NA_WIN_H // 2, 0, rows - kh)
    row_idx = row_lo[:, None] + np.arange(kh)[None, :] - np.arange(rows)[:, None] + NA_WIN_H - 1
    mask = jnp.asarray(col_ok)[:, :, None, :]
    kg = k.reshape(b, h, rows, GRID_W, d)
    vg = v.reshape(b, h, rows, GRID_W, d)
    qr = jnp.moveaxis((q * d ** -0.5).reshape(b, h, rows, nb, NA_QBLOCK, d), 2, 0)
    n_loc = kh * NA_KBLOCK

    def one_row(inp):
        qi, lo, ridx = inp
        k_blk = lax.dynamic_slice_in_dim(kg, lo, kh, axis=2)[:, :, :, key_col, :]
        v_blk = lax.dynamic_slice_in_dim(vg, lo, kh, axis=2)[:, :, :, key_col, :]
        bias = rpb[:, ridx[:, None, None, None], col_idx[None]]
        bias = jnp.transpose(bias, (0, 2, 3, 1, 4)).astype(jnp.float32)
        s_loc = jnp.einsum('bhmqd,bhkmcd->bhmqkc', qi, k_blk).astype(jnp.float32) + bias
        s_loc = jnp.where(mask, s_loc, NEG_INF).reshape(b, h, nb, NA_QBLOCK, n_loc)
        s_ctx = jnp.einsum('bhmqd,bhld->bhmql', qi, k_ctx).astype(jnp.float32)
        p = jax.nn.softmax(jnp.concatenate([s_loc, s_ctx], axis=-1), axis=-1).astype(v.dtype)
        p_loc = p[..., :n_loc].reshape(b, h, nb, NA_QBLOCK, kh, NA_KBLOCK)
        return (jnp.einsum('bhmqkc,bhkmcd->bhmqd', p_loc, v_blk)
                + jnp.einsum('bhmql,bhld->bhmqd', p[..., n_loc:], v_ctx))

    o = lax.map(one_row, (qr, jnp.asarray(row_lo, jnp.int32), jnp.asarray(row_idx, jnp.int32)))
    return jnp.moveaxis(o, 0, 2).reshape(b, h, t, d)

def _rwkv_scan(r, w, k, v, kk, a, s0, reverse):
    def step(S, inp):
        r_t, w_t, k_t, v_t, kk_t, a_t = inp
        sa = jnp.einsum('bhvk,bhk->bhv', S, kk_t)
        S = (S * w_t[:, :, None, :] - sa[..., None] * (kk_t * a_t)[:, :, None, :]
             + v_t[..., None] * k_t[:, :, None, :])
        return S, jnp.einsum('bhvk,bhk->bhv', S, r_t)

    xs = tuple(jnp.moveaxis(z, 1, 0) for z in (r, w, k, v, kk, a))
    s_fin, y = lax.scan(step, s0, xs, reverse=reverse)
    return s_fin, jnp.moveaxis(y, 0, 1)

def _rwkv(r, k, v, w1s, a1s, g1, lp, s0s):
    b, t, _ = r.shape
    dt = r.dtype
    f32 = jnp.float32

    def hd(z):
        return z.reshape(b, t, RW_HEADS, HEAD_DIM).astype(f32)

    rh, kh, vh = hd(r), hd(k), hd(v)
    kk = hd(k * lp['rw_kk'])
    kk = kk / jnp.maximum(jnp.sqrt(jnp.sum(kk * kk, axis=-1, keepdims=True)), 1e-12)
    ka = lp['rw_ka'].reshape(RW_HEADS, HEAD_DIM).astype(f32)
    rk = lp['rw_rk'].astype(f32)
    y_sum, bonus, finals = 0.0, 0.0, []
    for dirn in range(2):
        wlog = hd(lp['rw_w0'][dirn] + jnp.tanh(w1s[dirn]) @ lp['rw_w2'][dirn])
        decay = jnp.exp(-jnp.exp(-jax.nn.softplus(-wlog) - 0.5))
        a = jax.nn.sigmoid(hd(lp['rw_a0'][dirn] + a1s[dirn] @ lp['rw_a2'][dirn]))
        kd = kh * (1.0 + (a - 1.0) * ka)
        s_fin, y = _rwkv_scan(rh, decay, kd, vh, kk, a, s0s[dirn].astype(f32), dirn == 1)
        y_sum = y_sum + y
        bonus = bonus + jnp.sum(rh * kd * rk, axis=-1, keepdims=True) * vh
        finals.append(s_fin.astype(dt))
    mu = jnp.mean(y_sum, axis=-1, keepdims=True)
    var = jnp.mean(jnp.square(y_sum - mu), axis=-1, keepdims=True)
    yn = ((y_sum - mu) * lax.rsqrt(var + GN_EPS)).reshape(b, t, RW_DIM)
    yn = yn * lp['rw_gn_w'].astype(f32) + lp['rw_gn_b'].astype(f32)
    g = jax.nn.sigmoid(g1) @ lp['rw_g2']
    out = ((yn + bonus.reshape(b, t, RW_DIM)) * g.astype(f32)).astype(dt)
    return out, finals[0], finals[1]

def _mla(dq, dkv, kr, lp, cache):
    b, t, _ = dq.shape
    cq = _rmsnorm(dq, lp['mla_qn_g'])
    ckv = _rmsnorm(dkv, lp['mla_kvn_g'])
    q = (cq @ lp['mla_w_uq']).reshape(b, t, MLA_HEADS, NOPE_DIM + ROPE_DIM).transpose(0, 2, 1, 3)

    def expand_kv(c_kv, k_pe):
        kv = (c_kv @ lp['mla_w_ukv']).reshape(b, -1, MLA_HEADS, NOPE_DIM + V_DIM).transpose(0, 2, 1, 3)
        k_pe = jnp.broadcast_to(k_pe[:, None], (b, MLA_HEADS) + k_pe.shape[1:])
        return jnp.concatenate([kv[..., :NOPE_DIM], k_pe], axis=-1), kv[..., NOPE_DIM:]

    if cache is None:
        k, v = expand_kv(ckv, kr)
        o = _block_attention(q, k, v, MLA_SCALE)
        new = (ckv, kr)
    else:
        ckv_ctx, kr_ctx = cache
        cos, sin = _axial_rope(t, ROPE_DIM)
        q = jnp.concatenate([q[..., :NOPE_DIM], _rope(q[..., NOPE_DIM:], cos, sin)], axis=-1)
        k_lat, v_lat = expand_kv(ckv, _rope(kr, cos, sin))
        k_ctx, v_ctx = expand_kv(ckv_ctx, kr_ctx)
        o = _block_attention(q, jnp.concatenate([k_ctx, k_lat], axis=2),
                             jnp.concatenate([v_ctx, v_lat], axis=2), MLA_SCALE)
        new = None
    return _merge(o), new

def _mixer(h, lp, cache):
    b, t, _ = h.shape
    (na_q, na_k, na_v, rw_r, rw_k, rw_v, w1f, w1b, a1f, a1b, g1,
     mla_dq, mla_dkv, mla_kr, gate) = _split_cols(h @ lp['w_in'])
    q, k, v = _heads(na_q, NA_HEADS), _heads(na_k, NA_HEADS), _heads(na_v, NA_HEADS)
    if cache is None:
        o_na = _block_attention(q, k, v, HEAD_DIM ** -0.5)
        zero = jnp.zeros((b, RW_HEADS, HEAD_DIM, HEAD_DIM), jnp.float32)
        s0s = (zero, zero)
        mla_cache = None
    else:
        na_kc, na_vc, ckv_c, kr_c, s_f, s_b = cache
        o_na = _na_latent(q, k, v, na_kc, na_vc, lp['na_rpb'])
        s0s = (s_f, s_b)
        mla_cache = (ckv_c, kr_c)
    o_rw, s_f_new, s_b_new = _rwkv(rw_r, rw_k, rw_v, (w1f, w1b), (a1f, a1b), g1, lp, s0s)
    o_mla, mla_new = _mla(mla_dq, mla_dkv, mla_kr, lp, mla_cache)
    o = jnp.stack([_merge(o_na), o_rw, o_mla], axis=2)
    gates = jax.nn.sigmoid(gate.reshape(b, t, N_BRANCH, D_MODEL))
    out = jnp.sum(gates * jnp.einsum('btnc,ncd->btnd', o, lp['w_br']), axis=2) @ lp['w_o']
    if cache is None:
        return out, (k, v, mla_new[0], mla_new[1], s_f_new, s_b_new)
    return out, None

def _layer(x, cond, lp, cache):
    mod = (jax.nn.silu(cond) @ lp['ada_w'] + lp['ada_b'])[:, None, :]
    sh1, sc1, g1, shm, scm, gm, sh2, sc2, g2 = jnp.split(mod, N_MOD, axis=-1)
    h = _rmsnorm(x, lp['norm_g'][0]) * (1 + sc1) + sh1
    x = x + 0.5 * g1 * _swiglu(h, lp['ffn_wg'][0], lp['ffn_wu'][0], lp['ffn_wd'][0])
    h = _rmsnorm(x, lp['norm_g'][1]) * (1 + scm) + shm
    mix, new_cache = _mixer(h, lp, cache)
    x = x + gm * mix
    h = _rmsnorm(x, lp['norm_g'][2]) * (1 + sc2) + sh2
    x = x + 0.5 * g2 * _swiglu(h, lp['ffn_wg'][1], lp['ffn_wu'][1], lp['ffn_wd'][1])
    return x, new_cache

def setup_inputs(seed: int = 0) -> dict:
    key = jax.random.key(seed)
    ks = iter(jax.random.split(key, 48))
    d = D_MODEL

    def nrm(shape, scale):
        return jax.random.normal(next(ks), shape, jnp.float32) * scale

    return {
        'x_prompt': nrm((BATCH, SEQ, d), 1.0),
        'x_sample': nrm((DEC_BATCH, DEC_SEQ, d), 1.0),
        'c': nrm((DEC_BATCH, d), 1.0),
        'cache_na_k': nrm((DEC_BATCH, DEPTH, NA_HEADS, PAST_LEN, HEAD_DIM), 1.0),
        'cache_na_v': nrm((DEC_BATCH, DEPTH, NA_HEADS, PAST_LEN, HEAD_DIM), 1.0),
        'cache_mla_ckv': nrm((DEC_BATCH, DEPTH, PAST_LEN, KV_LORA), 1.0),
        'cache_mla_krope': nrm((DEC_BATCH, DEPTH, PAST_LEN, ROPE_DIM), 1.0),
        'state_rwkv_fwd': nrm((DEC_BATCH, DEPTH, RW_HEADS, HEAD_DIM, HEAD_DIM), 0.5),
        'state_rwkv_bwd': nrm((DEC_BATCH, DEPTH, RW_HEADS, HEAD_DIM, HEAD_DIM), 0.5),
        'c_ctx': nrm((d,), 1.0),
        'ada_w': nrm((DEPTH, d, N_MOD * d), 0.5 * d ** -0.5),
        'ada_b': nrm((DEPTH, N_MOD * d), 0.02),
        'norm_g': 1.0 + nrm((DEPTH, 3, d), 0.02),
        'ffn_wg': nrm((DEPTH, 2, d, D_FF), d ** -0.5),
        'ffn_wu': nrm((DEPTH, 2, d, D_FF), d ** -0.5),
        'ffn_wd': nrm((DEPTH, 2, D_FF, d), D_FF ** -0.5),
        'w_in': nrm((DEPTH, d, IN_COLS), d ** -0.5),
        'na_rpb': nrm((DEPTH, NA_HEADS, 2 * NA_WIN_H - 1, 2 * NA_WIN_W - 1), 0.1),
        'rw_w0': jax.random.uniform(next(ks), (DEPTH, 2, RW_DIM), jnp.float32, -6.0, -1.0),
        'rw_w2': nrm((DEPTH, 2, DECAY_LORA, RW_DIM), 0.1),
        'rw_a0': nrm((DEPTH, 2, RW_DIM), 0.1),
        'rw_a2': nrm((DEPTH, 2, ICLR_LORA, RW_DIM), 0.5 * ICLR_LORA ** -0.5),
        'rw_g2': nrm((DEPTH, GATE_LORA, RW_DIM), GATE_LORA ** -0.5),
        'rw_kk': 1.0 + nrm((DEPTH, RW_DIM), 0.1),
        'rw_ka': 1.0 + nrm((DEPTH, RW_DIM), 0.1),
        'rw_rk': nrm((DEPTH, RW_HEADS, HEAD_DIM), 0.1),
        'rw_gn_w': 1.0 + nrm((DEPTH, RW_DIM), 0.02),
        'rw_gn_b': nrm((DEPTH, RW_DIM), 0.02),
        'mla_qn_g': 1.0 + nrm((DEPTH, Q_LORA), 0.02),
        'mla_kvn_g': 1.0 + nrm((DEPTH, KV_LORA), 0.02),
        'mla_w_uq': nrm((DEPTH, Q_LORA, MLA_HEADS * (NOPE_DIM + ROPE_DIM)), Q_LORA ** -0.5),
        'mla_w_ukv': nrm((DEPTH, KV_LORA, MLA_HEADS * (NOPE_DIM + V_DIM)), KV_LORA ** -0.5),
        'w_br': nrm((DEPTH, N_BRANCH, BRANCH_DIM, d), BRANCH_DIM ** -0.5),
        'w_o': nrm((DEPTH, d, d), d ** -0.5),
        'final_g': 1.0 + nrm((d,), 0.02),
    }

def reference(x_prompt, x_sample, c, cache_na_k, cache_na_v, cache_mla_ckv, cache_mla_krope,
              state_rwkv_fwd, state_rwkv_bwd, c_ctx, ada_w, ada_b, norm_g, ffn_wg, ffn_wu, ffn_wd,
              w_in, na_rpb, rw_w0, rw_w2, rw_a0, rw_a2, rw_g2, rw_kk, rw_ka, rw_rk, rw_gn_w, rw_gn_b,
              mla_qn_g, mla_kvn_g, mla_w_uq, mla_w_ukv, w_br, w_o, final_g):
    xp, xs = x_prompt, x_sample
    ctx_cond = c_ctx[None, :]
    new_caches = []
    for l in range(DEPTH):
        lp = {
            'ada_w': ada_w[l], 'ada_b': ada_b[l], 'norm_g': norm_g[l],
            'ffn_wg': ffn_wg[l], 'ffn_wu': ffn_wu[l], 'ffn_wd': ffn_wd[l],
            'w_in': w_in[l], 'na_rpb': na_rpb[l],
            'rw_w0': rw_w0[l], 'rw_w2': rw_w2[l], 'rw_a0': rw_a0[l], 'rw_a2': rw_a2[l],
            'rw_g2': rw_g2[l], 'rw_kk': rw_kk[l], 'rw_ka': rw_ka[l], 'rw_rk': rw_rk[l],
            'rw_gn_w': rw_gn_w[l], 'rw_gn_b': rw_gn_b[l],
            'mla_qn_g': mla_qn_g[l], 'mla_kvn_g': mla_kvn_g[l],
            'mla_w_uq': mla_w_uq[l], 'mla_w_ukv': mla_w_ukv[l],
            'w_br': w_br[l], 'w_o': w_o[l],
        }
        xp, cache_l = _layer(xp, ctx_cond, lp, None)
        new_caches.append(cache_l)
        cache_in = (cache_na_k[:, l], cache_na_v[:, l], cache_mla_ckv[:, l], cache_mla_krope[:, l],
                    state_rwkv_fwd[:, l], state_rwkv_bwd[:, l])
        xs, _ = _layer(xs, c, lp, cache_in)
    y_prompt = _rmsnorm(xp, final_g)
    y_sample = _rmsnorm(xs, final_g)
    new_na_k = jnp.stack([cl[0] for cl in new_caches], axis=1)
    new_na_v = jnp.stack([cl[1] for cl in new_caches], axis=1)
    new_mla_ckv = jnp.stack([cl[2] for cl in new_caches], axis=1)
    new_mla_krope = jnp.stack([cl[3] for cl in new_caches], axis=1)
    new_rwkv_fwd = jnp.stack([cl[4] for cl in new_caches], axis=1)
    new_rwkv_bwd = jnp.stack([cl[5] for cl in new_caches], axis=1)
    return (y_prompt, y_sample, new_na_k, new_na_v, new_mla_ckv, new_mla_krope, new_rwkv_fwd, new_rwkv_bwd)


_drawn_inputs = setup_inputs


def setup_inputs(seed=0):
    import zlib

    import numpy as np

    out = dict(_drawn_inputs(seed))
    spreads = {}
    factors = {'cache_mla_ckv': 4.598,
     'cache_mla_krope': 8.0,
     'state_rwkv_fwd': 8.0,
     'state_rwkv_bwd': 8.0,
     'na_rpb': 8.0,
     'rw_gn_w': 8.0,
     'rw_gn_b': 8.0,
     'mla_qn_g': 8.0,
     'mla_kvn_g': 3.161,
     'final_g': 2.844}
    for name, (base, spread) in spreads.items():
        noise = np.random.default_rng([zlib.crc32(name.encode()), seed]).standard_normal(out[name].shape)
        drawn = base * np.exp(spread * noise) if base else spread * noise
        out[name] = __import__('jax').numpy.asarray(drawn.astype(out[name].dtype))
    for name, factor in factors.items():
        out[name] = (out[name] * factor).astype(out[name].dtype)
    return out
```

```python
from contextlib import ExitStack

import concourse.bass as bass
from concourse import mybir
import numpy as np

P = 128
DEPTH, D, DFF = 2, 1024, 2816
SEQ, DEC = 128, 256
TOK = SEQ + DEC
KEYS = TOK + 128
KT, FT = D // P, DFF // P
HEADS, HD, ROPE, NOPE = 4, 64, 32, 64
NMOD = 9
CHUNK = 128
LEVELS = 7
SEGS = ((0, 0, SEQ), (1, SEQ, TOK))
DECAY = float(np.exp(-0.5))

WIDE, NARROW = 16 * P, 11 * P
STAGES = [("ada", 36), ("up0", FT), ("down0", 16), ("proj", 7), ("v", 2), ("gate", 12),
          ("branch", 3), ("out", 4), ("up1", FT), ("down1", 16)]
AT, NBLK = {}, 0
for _name, _n in STAGES:
    AT[_name] = NBLK
    NBLK += _n
SLOTS = 4
assert NBLK % SLOTS == 0


def layout(parts):
    at, where = 0, {}
    for name, n in parts:
        where[name] = (at, at + n)
        at += n
    return where, at


CONST, NCONST = layout([
    ("ident", P), ("ones", P), ("block", P), ("cum0", 2 * P), ("cum1", 2 * P),
    ("level0", LEVELS * P), ("level1", LEVELS * P), ("gram0", 4 * P), ("gram1", 4 * P),
    ("heads", 8), ("okcol", 64), ("negcol", 64), ("rope", TOK), ("pick", 2), ("final_g", KT),
    ("cond", KT * 32), ("eps", 4), ("ada_b", DEPTH * 144), ("norm_g", DEPTH * 48)])
SMALL, NSMALL = layout([
    ("kk", 2), ("ka", 2), ("rk", 2), ("a0", 4), ("qn", 2), ("kvn", 1), ("pad", 3),
    ("w2", 256), ("a2", 256), ("g2", 256), ("w0", 512), ("gnw", 256), ("gnb", 256),
    ("uq", 1024), ("ukv_k", 256), ("ukv_v", 256), ("kr", 512), ("na_k", 256), ("na_v", 256),
    ("ckv", P), ("krope", P), ("state", 256), ("bias", 3072)])

JOBS = [(b, h, q) for b in range(2) for h in range(HEADS) for q in range(3)]
ROUNDS = [(0, 0), (1, 2), (2, 1)]
UNITS = [(d, p, hh) for d in range(2) for p in range(2) for hh in range(2)]


def hybrid_step(nc, wstream, small_d, const_d, x_d, y_d, k_d, v_d, ckv_d, kr_d, s_d):
    F32 = mybir.dt.float32
    ALU, ACT, AX = mybir.AluOpType, mybir.ActivationFunctionType, mybir.AxisListType.X

    with ExitStack() as ctx:
        def sb(name, *shape):
            return ctx.enter_context(nc.sbuf_tensor(name, [P, *shape], F32))

        const = sb("const", NCONST)
        small = sb("small", NSMALL)
        ring = sb("ring", SLOTS, WIDE)
        x = sb("x", KT, TOK)
        h = sb("h", KT, TOK)
        big = sb("big", 24 * TOK)
        tmp = sb("tmp", 2560)
        mod = sb("mod", NMOD * KT * 2)
        scale_c = sb("scale_c", 3, KT, 2)
        gate_c = sb("gate_c", 2, KT, 2)
        V = sb("V", 3, 512)
        r = sb("r", 2, TOK)
        k = sb("k", 2, TOK)
        kk = sb("kk", 2, TOK)
        sig = sb("sig", 3, 512)
        b = sb("b", 2, 2, TOK)
        kd = sb("kd", 2, 2, TOK)
        Y = sb("Y", 3, 256)
        g = sb("g", 3, 256)
        oT = [sb(f"oT{i}", 2, TOK) for i in range(3)]
        bonus = sb("bonus", 12)
        s_out = sb("s_out", 4, HD)
        s_mid = sb("s_mid", 4, HD)
        s_in = sb("s_in", 4, HD)
        pmid = sb("pmid", 4)
        stat = sb("stat", 32)
        stat2 = sb("stat2", 32)
        kr_raw = sb("kr_raw", SEQ)
        ps = ctx.enter_context(nc.psum_tensor("ps", [P, 8, 512], F32))

        def C(name, *dims):
            a, e = CONST[name]
            v = const[:, a:e]
            return v.rearrange("p (a b) -> p a b", b=dims[0]) if dims else v

        def S(name, b_=None):
            a, e = SMALL[name]
            v = small[:, a:e]
            return v.rearrange("p (a b) -> p a b", b=b_) if b_ else v

        def bcast(ap, times):
            return ap.unsqueeze(1).broadcast_to([ap.shape[0], times, ap.shape[1]])

        def spread(ap, width):
            return ap.unsqueeze(2).broadcast_to([ap.shape[0], ap.shape[1], width])

        def view(t, at, *dims):
            n = 1
            for d_ in dims:
                n *= d_
            v = t[:, at:at + n]
            if len(dims) == 2:
                return v.rearrange("p (a b) -> p a b", b=dims[1])
            if len(dims) == 3:
                return v.rearrange("p (a b c) -> p a b c", b=dims[1], c=dims[2])
            if len(dims) == 4:
                return v.rearrange("p (a b c d) -> p a b c d", b=dims[1], c=dims[2], d=dims[3])
            return v

        root, rinv = view(tmp, 0, TOK), view(tmp, TOK, TOK)
        silu = view(tmp, 2 * TOK, 2, TOK)
        rows = view(tmp, 4 * TOK, 2, 512)
        root2 = view(tmp, 0, 2, TOK)
        prod = view(tmp, 2 * TOK, 2, TOK)
        ropes = view(tmp, 0, 4, TOK)
        score, prob, probT = (view(tmp, 2 * TOK * i, 2, TOK) for i in range(3))
        KBt = view(tmp, 0, 2, 512)
        Fm, Um = view(tmp, 1024, 8, HD), view(tmp, 1536, 8, HD)
        brtmp = view(tmp, 2048, TOK)
        hidden = big[:, :].rearrange("p (t n) -> p t n", n=TOK)
        KTm = view(big, 0, 4, KEYS)
        kT = view(big, 2048, 2, KEYS)
        qT = view(big, 3072, 2, TOK)
        qm = view(big, 3840, 4, TOK)
        Vm = view(big, 5376, 4, 256)
        ckvT = view(big, 6400, KEYS)
        dq = view(big, 6912, 2, TOK)
        kpe = view(big, 7680, TOK)
        sq3 = view(big, 8064, 3, TOK)
        G = view(big, 0, 8, 4, P)
        T, Tt, X = (view(big, 4096 + 1024 * i, 8, P) for i in range(3))
        Nm = view(big, 7168, 2, 8, P)
        b0 = SMALL["bias"][0]
        E1 = view(small, b0, 2, 2, 2, P)
        E2 = view(small, b0 + 1024, 2, 2, P)
        KR = view(small, b0 + 1536, 2, 2, 2, P)
        KB = view(small, SMALL["uq"][0], 2, 2, 2, P)
        w1t, a1 = oT[2][:, 0, :], oT[2][:, 1, :]
        g1s = view(Y[:, :, :].rearrange("p a b -> p (a b)"), 0, TOK)
        ident, ones, block = C("ident"), C("ones"), C("block")
        eps6, epsgn = C("eps")[:, 0:1], C("eps")[:, 1:2]
        modv = mod[:, :].rearrange("p (m t c) -> p m t c", t=KT, c=2)

        class Signal:
            def __init__(self, name, per_layer, credit=0):
                self.sem = ctx.enter_context(nc.semaphore(name))
                self.n, self.credit = per_layer, credit

            def at(self, layer, count):
                return layer * self.n + (count + self.credit)

        landed = [Signal(f"landed{i}", 16 * NBLK // SLOTS) for i in range(SLOTS)]
        used = Signal("weights_used", NBLK, SLOTS)
        const_landed = Signal("const_landed", 0)
        x_landed = Signal("x_landed", 0)
        small_landed = Signal("small_landed", 16)
        cond_ready = Signal("cond_ready", 0)
        rows_ready = Signal("ada_rows_ready", 18)
        cols_ready = Signal("ada_cols_ready", 18)
        mod_done = Signal("mod_done", 18, 2)
        sq_act, sq_dve = Signal("squares_act", 3), Signal("squares_dve", 3)
        ss_ready, root_ready = Signal("sumsq_ready", 3), Signal("root_ready", 3)
        h_scaled, h_ready = Signal("h_scaled", 24), Signal("h_ready", 24)
        silu_ready = Signal("silu_ready", 2 * FT)
        up_free = Signal("up_banks_free", 2 * FT, 2)
        down_free = Signal("down_banks_free", 16, 2)
        proj_done = Signal("proj_done", 14)
        kr_ready, v_done = Signal("kr_ready", 1), Signal("v_done", 1)
        wlog_ready, wlog_biased, sig_ready = (Signal(n, 1) for n in ("wlog_ready", "wlog_biased", "sig_ready"))
        a_ready, a_done = Signal("a_ready", 1), Signal("a_done", 1)
        g_ready, g_done = Signal("g_ready", 1), Signal("g_done", 1)
        kksq_ready, kkss_ready, kkmax_ready, kkroot_ready = (
            Signal(n, 1) for n in ("kksq_ready", "kkss_ready", "kkmax_ready", "kkroot_ready"))
        prod_ready, bonus_psum, bonus_done = (Signal(n, 1) for n in ("prod_ready", "bonus_psum", "bonus_done"))
        mla_sq, mla_ss, mla_root, mla_normed = (
            Signal(n, 1) for n in ("mla_sq", "mla_ss", "mla_root", "mla_normed"))
        q_psum, q_done, kn_psum, kn_done, vm_psum, vm_done = (
            Signal(n, 1) for n in ("q_psum", "q_done", "kn_psum", "kn_done", "vm_psum", "vm_done"))
        bias_ready = Signal("bias_ready", 1)
        NJ = len(JOBS)
        scored, maxed, exped, normed, pT_psum, pT_ready, o_psum, o_done = (
            Signal(n, NJ) for n in ("scored", "maxed", "exped", "normed", "pT_psum", "pT_ready", "o_psum", "o_done"))
        cum_ready, exps_ready, factors_ready = (Signal(n, 3) for n in ("cum_ready", "exps_ready", "factors_ready"))
        gram_psum, gram_masked = Signal("gram_psum", 24), Signal("gram_masked", 24)
        kbt_psum, kbt_ready = Signal("kbt_psum", 3), Signal("kbt_ready", 3)
        level_masked, x_psum, t_ready = (
            Signal(n, 3 * LEVELS * 2) for n in ("level_masked", "inv_x_psum", "inv_t_ready"))
        x_ready, tt_psum = (Signal(n, 3 * (LEVELS - 1) * 2) for n in ("inv_x_ready", "inv_tt_psum"))
        f_psum, f_ready, u_psum, u_ready, y_psum, round_done = (
            Signal(n, 3) for n in ("f_psum", "f_ready", "u_psum", "u_ready", "y_psum", "round_done"))
        gn_var, gn_root, rw_out, rwT_psum, rwT_ready = (
            Signal(n, 1) for n in ("gn_var", "gn_root", "rw_out", "rwT_psum", "rwT_ready"))
        gate_done, br_psum, br_free = Signal("gate_done", 24), Signal("br_psum", 24), Signal("br_free", 24)
        comb_ready = Signal("comb_ready", 1)
        out_free = Signal("out_free", 8, 8)
        kv_stored, s_stored = Signal("kv_stored", 64), Signal("s_stored", 16)
        y_ready, y_stored = Signal("y_ready", 0), Signal("y_stored", 0)

        def lev(rd, m, grp):
            return (rd * LEVELS + m) * 2 + grp + 1

        def lev1(rd, m, grp):
            return (rd * (LEVELS - 1) + m - 1) * 2 + grp + 1

        blk = ctx.enter_context(nc.Block())

        @blk.sync
        def _(sp):
            sp.dma_start(const[:, :], const_d).then_inc(const_landed.sem, 16)
            sp.dma_start(x[:, :, :], x_d).then_inc(x_landed.sem, 16)

            def load(layer, n, slot, cols):
                row = sp.snap(layer * NBLK + n)
                sp.wait_ge(used.sem, layer * NBLK + (n + 1))
                sp.dma_start(ring[:, slot, 0:cols],
                             wstream[bass.ds(row, 1), :, 0:cols].rearrange("a p n -> (a p) n")
                             ).then_inc(landed[slot].sem, 16)

            with sp.Fori(0, DEPTH) as layer:
                for name, n in STAGES:
                    cols = NARROW if name.startswith("down") else WIDE
                    off = AT[name]
                    if n >= 2 * SLOTS:
                        with sp.Fori(0, n // SLOTS) as i:
                            for j in range(SLOTS):
                                load(layer, i * SLOTS + (off + j), (off + j) % SLOTS, cols)
                    for j in range(n if n < 2 * SLOTS else n % SLOTS):
                        at = off + (0 if n < 2 * SLOTS else n // SLOTS * SLOTS) + j
                        load(layer, at, at % SLOTS, cols)
                    if name == "ada":
                        row = sp.snap(layer + 0)
                        sp.wait_ge(out_free.sem, out_free.at(layer, 0))
                        sp.dma_start(small[:, :], small_d[bass.ds(row, 1)].rearrange("a p n -> (a p) n")
                                     ).then_inc(small_landed.sem, 16)
            sp.wait_ge(y_ready.sem, 1)
            sp.dma_start(y_d, h[:, :, :]).then_inc(y_stored.sem, 16)
            sp.wait_ge(y_stored.sem, 16)

        @blk.tensor
        def _(pe):
            mm = nc.tensor.matmul
            pe.sem_inc(used.sem, SLOTS)
            pe.wait_ge(const_landed.sem, 16)

            def block_of(layer, off, i=0):
                slot = off % SLOTS
                pe.wait_ge(landed[slot].sem,
                           layer * (16 * NBLK // SLOTS) + (i * 16 + 16 * (off // SLOTS + 1)))
                return ring[:, slot, :]

            def norm(layer, n):
                pe.wait_ge(sq_act.sem, sq_act.at(layer, n + 1))
                pe.wait_ge(sq_dve.sem, sq_dve.at(layer, n + 1))
                for t in range(KT):
                    last = mm(ps[:, 6, 0:TOK], ones, h[:, t, :], start=t == 0, stop=t == KT - 1)
                last.then_inc(ss_ready.sem, 1)

            def wait_h(layer, n):
                pe.wait_ge(h_ready.sem, h_ready.at(layer, 8 * n + 8))

            def ffn(layer, f):
                off = AT[f"up{f}"]

                def up(i, j):
                    w = block_of(layer, off + j, i)
                    if j == 0:
                        wait_h(layer, 2 * f)
                    pe.wait_ge(up_free.sem, layer * up_free.n + (i * SLOTS + (f * FT + j + 1)))
                    for z in range(2):
                        for t in range(KT):
                            last = mm(ps[:, (j % 2) * 2 + z, 0:TOK], w[:, (z * KT + t) * P:(z * KT + t + 1) * P],
                                      h[:, t, :], start=t == 0, stop=t == KT - 1)
                    last.then_inc(used.sem, 1)

                with pe.Fori(0, FT // SLOTS) as i:
                    for j in range(SLOTS):
                        up(i, j)
                for j in range(FT // SLOTS * SLOTS, FT):
                    up(0, j)
                off2 = AT[f"down{f}"]
                with pe.Fori(0, 4) as i:
                    for dd in range(2):
                        for half in range(2):
                            w = block_of(layer, off2 + 2 * dd + half, i)
                            if dd == 0 and half == 0:
                                pe.wait_ge(up_free.sem, up_free.at(layer, (f + 1) * FT))
                            if half == 0:
                                pe.wait_ge(down_free.sem, layer * down_free.n + (i * 2 + (f * 8 + dd + 1)))
                            for t in range(11):
                                last = mm(ps[:, 4 + dd, 0:TOK], w[:, t * P:(t + 1) * P],
                                          hidden[:, half * 11 + t, :], start=half == 0 and t == 0,
                                          stop=half == 1 and t == 10)
                            last.then_inc(used.sem, 1)

            with pe.Fori(0, DEPTH) as layer:
                pe.wait_ge(cond_ready.sem, 1)
                cond = C("cond", 32)
                with pe.Fori(0, 9) as i:
                    for c in range(2):
                        for half in range(2):
                            w = block_of(layer, 2 * c + half, i)
                            for q in range(4):
                                last = mm(ps[32 * q:32 * q + 32, c, :], cond[:, half * 4 + q, :],
                                          w[:, q * 512:(q + 1) * 512], start=half == 0, stop=half == 1)
                            last.then_inc(used.sem, 1)
                    for c in range(2):
                        pe.wait_ge(rows_ready.sem, layer * 18 + (i * 2 + (c + 1)))
                        pe.wait_ge(mod_done.sem, layer * 18 + (i * 2 + (c + 1)))
                        for j in range(4):
                            last = mm(ps[:, 2 + c, 2 * j:2 * j + 2], rows[:, c, j * P:(j + 1) * P],
                                      C("pick"), start=True, stop=True)
                        last.then_inc(cols_ready.sem, 1)

                norm(layer, 0)
                ffn(layer, 0)
                norm(layer, 1)
                wait_h(layer, 1)

                for t in range(14):
                    if t % 2 == 0:
                        w = block_of(layer, AT["proj"] + t // 2)
                    if t >= 4:
                        pe.wait_ge(proj_done.sem, proj_done.at(layer, t - 3))
                    for z in range(KT):
                        last = mm(ps[:, t % 4, 0:TOK], w[:, (t % 2 * KT + z) * P:(t % 2 * KT + z + 1) * P],
                                  h[:, z, :], start=z == 0, stop=z == KT - 1)
                    if t % 2:
                        last.then_inc(used.sem, 1)
                pe.wait_ge(small_landed.sem, small_landed.at(layer, 16))
                for z in range(KT):
                    last = mm(ps[64:128, 4, 0:TOK], S("kr", 64)[:, z, :], h[:, z, :],
                              start=z == 0, stop=z == KT - 1)
                last.then_inc(kr_ready.sem, 1)
                for half in range(2):
                    w = block_of(layer, AT["v"] + half)
                    for j in range(3):
                        for z in range(4):
                            last = mm(ps[:, 5 + j, :], h[:, half * 4 + z, j * P:(j + 1) * P],
                                      w[:, z * 512:(z + 1) * 512],
                                      start=half == 0 and z == 0, stop=half == 1 and z == 3)
                    last.then_inc(used.sem, 1)

                pe.wait_ge(proj_done.sem, proj_done.at(layer, 14))
                for d in range(2):
                    for j in range(3):
                        last = mm(ps[:, 2 * d + j // 2, j % 2 * 256:j % 2 * 256 + 256], w1t[64 * d:64 * d + 64, j * P:(j + 1) * P],
                                  S("w2")[64 * d:64 * d + 64, :], start=True, stop=True)
                last.then_inc(wlog_ready.sem, 1)
                pe.wait_ge(v_done.sem, v_done.at(layer, 1))
                for d in range(2):
                    for p in range(2):
                        last = mm(ps[:, 4 + 2 * d + p, 0:TOK], S("a2")[64 * d:64 * d + 64, p * P:(p + 1) * P],
                                  a1[64 * d:64 * d + 64, :], start=True, stop=True)
                last.then_inc(a_ready.sem, 1)
                pe.wait_ge(wlog_biased.sem, wlog_biased.at(layer, 1))
                for j in range(3):
                    last = mm(ps[:, j // 2, j % 2 * 256:j % 2 * 256 + 256],
                              g1s[:, j * P:(j + 1) * P], S("g2"), start=True, stop=True)
                last.then_inc(g_ready.sem, 1)
                pe.wait_ge(kksq_ready.sem, kksq_ready.at(layer, 1))
                for p in range(2):
                    last = mm(ps[:, 2 + p, 0:TOK], block, kd[:, 0, p, :], start=True, stop=True)
                last.then_inc(kkss_ready.sem, 1)
                pe.wait_ge(prod_ready.sem, prod_ready.at(layer, 1))
                for j in range(3):
                    for p in range(2):
                        last = mm(ps[:, 2, 4 * j:4 * j + 4], prod[:, p, j * P:(j + 1) * P],
                                  C("heads", 4)[:, p, :], start=p == 0, stop=p == 1)
                last.then_inc(bonus_psum.sem, 1)

                pe.wait_ge(g_done.sem, g_done.at(layer, 1))
                pe.wait_ge(mla_sq.sem, mla_sq.at(layer, 1))
                for z in range(2):
                    mm(ps[:, 0, 0:TOK], ones, sq3[:, z, :], start=z == 0, stop=z == 1)
                mm(ps[:, 1, 0:TOK], ones, sq3[:, 2, :], start=True, stop=True).then_inc(mla_ss.sem, 1)
                pe.wait_ge(mla_normed.sem, mla_normed.at(layer, 1))
                pe.wait_ge(bonus_done.sem, bonus_done.at(layer, 1))
                for hd in range(HEADS):
                    for z in range(2):
                        last = mm(ps[:, hd, 0:TOK], S("uq")[:, (z * 4 + hd) * P:(z * 4 + hd + 1) * P],
                                  dq[:, z, :], start=z == 0, stop=z == 1)
                last.then_inc(q_psum.sem, 1)
                pe.wait_ge(a_done.sem, a_done.at(layer, 1))
                for hd in range(HEADS):
                    last = mm(ps[0:64, 4 + hd, :], S("ukv_k")[:, hd * 64:(hd + 1) * 64], ckvT,
                              start=True, stop=True)
                last.then_inc(kn_psum.sem, 1)
                pe.wait_ge(q_done.sem, q_done.at(layer, 1))
                for t in range(4):
                    last = mm(ps[:, t // 2, t % 2 * 256:t % 2 * 256 + 256], ckvT[:, t * P:(t + 1) * P],
                              S("ukv_v"), start=True, stop=True)
                last.then_inc(vm_psum.sem, 1)
                pe.wait_ge(kn_done.sem, kn_done.at(layer, 1))
                pe.wait_ge(vm_done.sem, vm_done.at(layer, 1))

                def scores(n):
                    br, hd, q = JOBS[n]
                    k0, k1 = (0, P) if q == 0 else (P, KEYS)
                    if n >= 2:
                        pe.wait_ge(exped.sem, exped.at(layer, n - 1))
                    if br == 0:
                        o, p = 64 * (hd % 2), hd // 2
                        ins = mm(ps[:, 2 + n % 2, 0:k1 - k0], qT[o:o + 64, p, q * P:(q + 1) * P],
                                 kT[o:o + 64, p, k0:k1], start=True, stop=True)
                    else:
                        ins = mm(ps[:, 2 + n % 2, 0:k1 - k0], qm[0:96, hd, q * P:(q + 1) * P],
                                 KTm[0:96, hd, k0:k1], start=True, stop=True)
                    ins.then_inc(scored.sem, 1)

                def turn(n):
                    _, _, q = JOBS[n]
                    pe.wait_ge(normed.sem, normed.at(layer, n + 1))
                    if n >= 2:
                        pe.wait_ge(pT_ready.sem, pT_ready.at(layer, n - 1))
                    for t in range(1 if q == 0 else 3):
                        last = nc.tensor.transpose(ps[:, 4 + n % 2, t * P:(t + 1) * P],
                                                   prob[:, n % 2, t * P:(t + 1) * P], ident)
                    last.then_inc(pT_psum.sem, 1)

                def weigh(n):
                    br, hd, q = JOBS[n]
                    o = 64 * (hd % 2)
                    pe.wait_ge(pT_ready.sem, pT_ready.at(layer, n + 1))
                    if n >= 2:
                        pe.wait_ge(o_done.sem, o_done.at(layer, n - 1))
                    tiles = (0,) if q == 0 else (1, 2, 3)
                    for i_, t in enumerate(tiles):
                        if br == 1:
                            v_ = Vm[:, t, hd * 64:(hd + 1) * 64]
                        elif t == 3:
                            v_ = S("na_v")[:, hd * 64:(hd + 1) * 64]
                        else:
                            v_ = V[:, t, hd * 64:(hd + 1) * 64]
                        last = mm(ps[o:o + 64, 6 + n % 2, 0:P], v_, probT[:, n % 2, i_ * P:(i_ + 1) * P],
                                  start=i_ == 0, stop=i_ == len(tiles) - 1)
                    last.then_inc(o_psum.sem, 1)

                for n in range(NJ + 2):
                    if n < NJ:
                        scores(n)
                    if 1 <= n <= NJ:
                        turn(n - 1)
                    if n >= 2:
                        weigh(n - 2)

                pe.wait_ge(o_done.sem, o_done.at(layer, NJ))
                pe.wait_ge(bonus_done.sem, bonus_done.at(layer, 1))
                pe.wait_ge(sig_ready.sem, sig_ready.at(layer, 1))
                for rd, tiles in enumerate(ROUNDS):
                    if rd:
                        pe.wait_ge(round_done.sem, round_done.at(layer, rd))
                    for d in range(2):
                        for p in range(2):
                            last = mm(ps[:, d, p * 256:(p + 1) * 256],
                                      sig[:, tiles[d], d * 256 + p * P:d * 256 + (p + 1) * P],
                                      C(f"cum{d}"), start=True, stop=True)
                    last.then_inc(cum_ready.sem, 1)
                    pe.wait_ge(factors_ready.sem, factors_ready.at(layer, rd + 1))
                    for u, (d, p, hh) in enumerate(UNITS):
                        o = 64 * hh
                        for z in range(2):
                            last = mm(ps[:, u, z * 256:(z + 1) * 256], KB[o:o + 64, d, p, z, :],
                                      KR[o:o + 64, d, p, :, :], start=True, stop=True)
                        last.then_inc(gram_psum.sem, 1)
                    pe.wait_ge(gram_masked.sem, gram_masked.at(layer, 8 * rd + 8))
                    for d in range(2):
                        for z in range(2):
                            for p in range(2):
                                last = nc.tensor.transpose(ps[:, d, (2 * z + p) * P:(2 * z + p + 1) * P],
                                                           KB[:, d, p, z, :], ident)
                    last.then_inc(kbt_psum.sem, 1)
                    for m in range(LEVELS):
                        for grp in range(2):
                            pe.wait_ge(level_masked.sem, level_masked.at(layer, lev(rd, m, grp)))
                            if m:
                                pe.wait_ge(t_ready.sem, t_ready.at(layer, lev(rd, m - 1, grp)))
                            for q in range(4):
                                u = 4 * grp + q
                                last = mm(ps[:, 2 + grp, q * P:(q + 1) * P], Nm[:, m % 2, u, :],
                                          T[:, u, :] if m else ident, start=True, stop=True)
                            last.then_inc(x_psum.sem, 1)
                        if m == 0:
                            continue
                        for grp in range(2):
                            pe.wait_ge(x_ready.sem, x_ready.at(layer, lev1(rd, m, grp)))
                            for q in range(4):
                                u = 4 * grp + q
                                if m < LEVELS - 1:
                                    mm(ps[:, 4 + grp, q * P:(q + 1) * P], Tt[:, u, :], X[:, u, :],
                                       start=True, stop=True)
                                last = mm(ps[:, 6 + grp, q * P:(q + 1) * P], X[:, u, :], Tt[:, u, :],
                                          start=True, stop=True)
                            last.then_inc(tt_psum.sem, 1)
                    pe.wait_ge(kbt_ready.sem, kbt_ready.at(layer, rd + 1))
                    for u, (d, p, hh) in enumerate(UNITS):
                        o, hd = 64 * hh, 2 * p + hh
                        c0 = (2 * d + p) * 64
                        mm(ps[:, hh, c0:c0 + 64], KR[o:o + 64, d, p, 0, :],
                           s_in[o:o + 64, 2 * d + p, :], start=True, stop=False)
                        last = mm(ps[:, hh, c0:c0 + 64], G[:, u, 0, :],
                                  V[:, tiles[d], 256 + hd * 64:256 + hd * 64 + 64], start=False, stop=True)
                    last.then_inc(f_psum.sem, 1)
                    pe.wait_ge(f_ready.sem, f_ready.at(layer, rd + 1))
                    pe.wait_ge(t_ready.sem, t_ready.at(layer, lev(rd, LEVELS - 1, 1)))
                    for u in range(8):
                        last = mm(ps[:, 2, u * 64:(u + 1) * 64], Tt[:, u, :], Fm[:, u, :],
                                  start=True, stop=True)
                    last.then_inc(u_psum.sem, 1)
                    pe.wait_ge(u_ready.sem, u_ready.at(layer, rd + 1))
                    for u, (d, p, hh) in enumerate(UNITS):
                        o, hd = 64 * hh, 2 * p + hh
                        v_ = V[:, tiles[d], 256 + hd * 64:256 + hd * 64 + 64]
                        if rd < 2:
                            so = ps[o:o + 64, 5, (2 * d + p) * 64:(2 * d + p) * 64 + 64]
                            mm(so, KBt[:, d, p * P + o:p * P + o + 64], v_, start=True, stop=False)
                            mm(so, KBt[:, d, 256 + p * P + o:256 + p * P + o + 64], Um[:, u, :],
                               start=False, stop=True)
                        yo = ps[:, 3 + hh, (2 * d + p) * 64:(2 * d + p) * 64 + 64]
                        mm(yo, KR[o:o + 64, d, p, 1, :], s_in[o:o + 64, 2 * d + p, :], start=True, stop=False)
                        mm(yo, G[:, u, 1, :], v_, start=False, stop=False)
                        last = mm(yo, G[:, u, 3, :], Um[:, u, :], start=False, stop=True)
                    last.then_inc(y_psum.sem, 1)
                pe.wait_ge(rw_out.sem, rw_out.at(layer, 1))
                for p in range(2):
                    for j in range(3):
                        last = nc.tensor.transpose(ps[:, p, j * P:(j + 1) * P], Y[:, j, p * P:(p + 1) * P], ident)
                last.then_inc(rwT_psum.sem, 1)
                pe.wait_ge(rwT_ready.sem, rwT_ready.at(layer, 1))

                for n in range(24):
                    if n % 2 == 0:
                        w = block_of(layer, AT["gate"] + n // 2)
                    if n >= 4:
                        pe.wait_ge(gate_done.sem, gate_done.at(layer, n - 3))
                    for z in range(KT):
                        last = mm(ps[:, n % 4, 0:TOK], w[:, (n % 2 * KT + z) * P:(n % 2 * KT + z + 1) * P],
                                  h[:, z, :], start=z == 0, stop=z == KT - 1)
                    if n % 2:
                        last.then_inc(used.sem, 1)
                for n in range(24):
                    if n % 8 == 0:
                        w = block_of(layer, AT["branch"] + n // 8)
                    if n >= 4:
                        pe.wait_ge(br_free.sem, br_free.at(layer, n - 3))
                    for z in range(2):
                        last = mm(ps[:, 4 + n % 4, 0:TOK], w[:, (n % 8 * 2 + z) * P:(n % 8 * 2 + z + 1) * P],
                                  oT[(0, 2, 1)[n % 3]][:, z, :], start=z == 0, stop=z == 1)
                        if z == 0 and n and n % 8 == 0:
                            last.then_inc(used.sem, 1)
                    last.then_inc(br_psum.sem, 1)
                pe.wait_ge(comb_ready.sem, comb_ready.at(layer, 1))
                for n in range(8):
                    if n % 2 == 0:
                        w = block_of(layer, AT["out"] + n // 2)
                    if n >= 4:
                        pe.wait_ge(out_free.sem, out_free.at(layer, n - 3))
                    for z in range(KT):
                        last = mm(ps[:, n % 4, 0:TOK], w[:, (n % 2 * KT + z) * P:(n % 2 * KT + z + 1) * P],
                                  h[:, z, :], start=z == 0, stop=z == KT - 1)
                        if n == 0 and z == 0:
                            last.then_inc(used.sem, 1)
                    if n % 2:
                        last.then_inc(used.sem, 1)

                norm(layer, 2)
                ffn(layer, 1)
            norm(DEPTH, 0)

        @blk.scalar
        def _(act):
            A = nc.scalar.activation
            act.wait_ge(const_landed.sem, 16)
            A(C("cond"), C("cond"), ACT.Silu).then_inc(cond_ready.sem, 1)

            def norm(layer, n, final=False):
                for t in range(4):
                    last = A(h[:, t, :], x[:, t, :], ACT.Square)
                last.then_inc(sq_act.sem, 1)
                act.wait_ge(ss_ready.sem, ss_ready.at(layer, n + 1))
                A(root, ps[:, 6, 0:TOK], ACT.Sqrt, bias=eps6, scale=1.0 / D).then_inc(root_ready.sem, 1)
                if final:
                    return
                for t in range(KT):
                    act.wait_ge(h_scaled.sem, h_scaled.at(layer, 8 * n + t + 1))
                    for c, s0, s1 in SEGS:
                        last = A(h[:, t, s0:s1], h[:, t, s0:s1], ACT.Identity,
                                 bias=modv[:, 3 * n, t, c:c + 1])
                    last.then_inc(h_ready.sem, 1)

            def ffn(layer, f):
                def one(i, j):
                    act.wait_ge(used.sem, layer * NBLK + (i * SLOTS + (AT[f"up{f}"] + j + 1 + SLOTS)))
                    A(silu[:, j % 2, :], ps[:, (j % 2) * 2, 0:TOK], ACT.Silu).then_inc(silu_ready.sem, 1)
                with act.Fori(0, FT // SLOTS) as i:
                    for j in range(SLOTS):
                        one(i, j)
                for j in range(FT // SLOTS * SLOTS, FT):
                    one(0, j)
                act.wait_ge(down_free.sem, down_free.at(layer, 8 * f + 8))

            act.wait_ge(x_landed.sem, 16)
            with act.Fori(0, DEPTH) as layer:
                with act.Fori(0, 9) as i:
                    for c in range(2):
                        act.wait_ge(used.sem, layer * NBLK + (i * SLOTS + (2 * c + 2 + SLOTS)))
                        A(rows[:, c, :], ps[:, c, :], ACT.Copy).then_inc(rows_ready.sem, 1)
                norm(layer, 0)
                ffn(layer, 0)
                norm(layer, 1)

                dest = ([qT[:, z, :] for z in range(2)] + [kT[:, z, 0:TOK] for z in range(2)]
                        + [r[:, z, :] for z in range(2)] + [k[:, z, :] for z in range(2)]
                        + [w1t, a1, g1s] + [dq[:, z, :] for z in range(2)] + [ckvT[:, 0:TOK]])
                for t in range(14):
                    act.wait_ge(used.sem, used.at(layer, AT["proj"] + t // 2 + 1))
                    A(dest[t], ps[:, t % 4, 0:TOK], {8: ACT.Tanh, 10: ACT.Sigmoid}.get(t, ACT.Copy)
                      ).then_inc(proj_done.sem, 1)
                act.wait_ge(wlog_biased.sem, wlog_biased.at(layer, 1))
                A(sig[:, :, :], sig[:, :, :], ACT.Sigmoid).then_inc(sig_ready.sem, 1)
                act.wait_ge(a_ready.sem, a_ready.at(layer, 1))
                for d in range(2):
                    for p in range(2):
                        last = A(b[:, d, p, :], ps[:, 4 + 2 * d + p, 0:TOK], ACT.Sigmoid,
                                 bias=S("a0")[:, 2 * d + p:2 * d + p + 1])
                last.then_inc(a_done.sem, 1)
                act.wait_ge(g_ready.sem, g_ready.at(layer, 1))
                A(g[:, 0:2, :].rearrange("p a b -> p (a b)"), ps[:, 0, :], ACT.Copy)
                A(g[:, 2, :], ps[:, 1, 0:256], ACT.Copy).then_inc(g_done.sem, 1)
                act.wait_ge(kkmax_ready.sem, kkmax_ready.at(layer, 1))
                A(root2, root2, ACT.Sqrt).then_inc(kkroot_ready.sem, 1)
                act.wait_ge(mla_ss.sem, mla_ss.at(layer, 1))
                act.wait_ge(bonus_psum.sem, bonus_psum.at(layer, 1))
                A(prod[:, 0, :], ps[:, 0, 0:TOK], ACT.Sqrt, bias=eps6, scale=1.0 / 256)
                A(prod[:, 1, :], ps[:, 1, 0:TOK], ACT.Sqrt, bias=eps6, scale=1.0 / P).then_inc(mla_root.sem, 1)
                act.wait_ge(kn_psum.sem, kn_psum.at(layer, 1))
                A(KTm[0:64, :, :], ps[0:64, 4:8, :], ACT.Copy).then_inc(kn_done.sem, 1)
                act.wait_ge(vm_psum.sem, vm_psum.at(layer, 1))
                A(Vm[:, :, :].rearrange("p a b -> p (a b)"), ps[:, 0:2, :].rearrange("p a b -> p (a b)"),
                  ACT.Copy).then_inc(vm_done.sem, 1)
                act.wait_ge(mla_normed.sem, mla_normed.at(layer, 1))
                row = act.snap(layer + 0)
                act.dma_start(k_d[bass.ds(row, 1)].rearrange("a p t n -> (a p) t n"), kT[:, :, 0:SEQ]
                              ).then_inc(kv_stored.sem, 16)
                act.dma_start(v_d[bass.ds(row, 1)].rearrange("a p n -> (a p) n"), V[:, 0, 0:256]
                              ).then_inc(kv_stored.sem, 16)
                act.dma_start(ckv_d[bass.ds(row, 1)].rearrange("a p n -> (a p) n"), ckvT[:, 0:SEQ]
                              ).then_inc(kv_stored.sem, 16)
                act.dma_start(kr_d[bass.ds(row, 1)].rearrange("a p n -> (a p) n"), kr_raw[64:96, :]
                              ).then_inc(kv_stored.sem, 16)

                def exp(n):
                    br, hd, q = JOBS[n]
                    act.wait_ge(maxed.sem, maxed.at(layer, n + 1))
                    if n >= 2:
                        act.wait_ge(pT_psum.sem, pT_psum.at(layer, n - 1))
                    local = br == 0 and q > 0
                    width = P if q == 0 else TOK
                    A(prob[:, n % 2, 0:width], (score[:, n % 2, :] if local else ps[:, 2 + n % 2, 0:width]),
                      ACT.Exp, bias=stat[:, 4 + n % 2:5 + n % 2],
                      scale=1.0 if local else (HD ** -0.5 if br == 0 else (NOPE + ROPE) ** -0.5),
                      accum_out=stat[:, 8 + n % 2:9 + n % 2]).then_inc(exped.sem, 1)

                def copyT(n):
                    _, _, q = JOBS[n]
                    width = P if q == 0 else TOK
                    act.wait_ge(pT_psum.sem, pT_psum.at(layer, n + 1))
                    if n >= 2:
                        act.wait_ge(o_psum.sem, o_psum.at(layer, n - 1))
                    A(probT[:, n % 2, 0:width], ps[:, 4 + n % 2, 0:width], ACT.Copy).then_inc(pT_ready.sem, 1)

                for n in range(NJ + 1):
                    if n < NJ:
                        exp(n)
                    if n:
                        copyT(n - 1)

                act.wait_ge(kv_stored.sem, kv_stored.at(layer, 64))
                for rd, tiles in enumerate(ROUNDS):
                    act.wait_ge(cum_ready.sem, cum_ready.at(layer, rd + 1))
                    for d in range(2):
                        cs = ps[:, d, :].rearrange("p (a b c) -> p a b c", a=2, b=2)
                        A(E1[:, d].rearrange("p a b c -> p (a b c)"), ps[:, d, :], ACT.Exp, scale=-DECAY)
                        A(E2[:, d], cs[:, :, 0, :], ACT.Exp, scale=DECAY)
                        first = 0 if d == 0 else P - 1
                        last = A(pmid[:, 2 * d:2 * d + 2], cs[:, :, 1, first], ACT.Exp, scale=DECAY)
                    last.then_inc(exps_ready.sem, 1)
                    act.wait_ge(kbt_psum.sem, kbt_psum.at(layer, rd + 1))
                    for d in range(2):
                        A(KBt[:, d, 0:256], ps[:, d, 0:256], ACT.Copy)
                        last = A(KBt[:, d, 256:512], ps[:, d, 256:512], ACT.Copy, scale=-1.0)
                    last.then_inc(kbt_ready.sem, 1)
                    for m in range(1, LEVELS):
                        for grp in range(2):
                            act.wait_ge(x_psum.sem, x_psum.at(layer, lev(rd, m, grp)))
                            A(X[:, 4 * grp:4 * grp + 4, :], ps[:, 2 + grp, :].rearrange("p (a b) -> p a b", b=P),
                              ACT.Copy).then_inc(x_ready.sem, 1)
                    if rd == 0:
                        act.wait_ge(round_done.sem, round_done.at(layer, 1))
                        act.dma_start(s_d[bass.ds(row, 1)].rearrange("a p t n -> (a p) t n"), s_out[:, :, :]
                                      ).then_inc(s_stored.sem, 16)
                act.wait_ge(gn_var.sem, gn_var.at(layer, 1))
                A(stat2[:, 0:12], stat[:, 12:24], ACT.Sqrt, bias=epsgn, scale=1.0 / HD).then_inc(gn_root.sem, 1)
                act.wait_ge(rwT_psum.sem, rwT_psum.at(layer, 1))
                A(oT[2][:, :, :], ps[:, 0:2, 0:TOK], ACT.Copy).then_inc(rwT_ready.sem, 1)
                act.wait_ge(s_stored.sem, s_stored.at(layer, 16))
                for n in range(24):
                    act.wait_ge(used.sem, used.at(layer, AT["gate"] + n // 2 + 1))
                    A(hidden[:, n, :], ps[:, n % 4, 0:TOK], ACT.Sigmoid).then_inc(gate_done.sem, 1)
                act.wait_ge(out_free.sem, out_free.at(layer, 8))
                norm(layer, 2)
                ffn(layer, 1)
            norm(DEPTH, 0, final=True)

        @blk.vector
        def _(dve):
            v = nc.vector
            dve.sem_inc(up_free.sem, up_free.credit)
            dve.sem_inc(down_free.sem, down_free.credit)
            dve.sem_inc(mod_done.sem, mod_done.credit)
            dve.sem_inc(out_free.sem, out_free.credit)
            dve.wait_ge(const_landed.sem, 16)
            dve.wait_ge(x_landed.sem, 16)

            def norm(layer, n, final=False):
                dve.drain()
                v.tensor_tensor(h[:, 4:8, :], x[:, 4:8, :], x[:, 4:8, :], ALU.mult).then_inc(sq_dve.sem, 1)
                dve.wait_ge(root_ready.sem, root_ready.at(layer, n + 1))
                v.reciprocal(rinv, root)
                dve.drain()
                for t in range(KT):
                    if final:
                        last = v.scalar_tensor_tensor(out=h[:, t, :], in0=x[:, t, :],
                                                      scalar=C("final_g")[:, t:t + 1], in1=rinv,
                                                      op0=ALU.mult, op1=ALU.mult)
                        continue
                    for c, s0, s1 in SEGS:
                        last = v.scalar_tensor_tensor(out=h[:, t, s0:s1], in0=x[:, t, s0:s1],
                                                      scalar=scale_c[:, n, t, c:c + 1], in1=rinv[:, s0:s1],
                                                      op0=ALU.mult, op1=ALU.mult)
                    last.then_inc(h_scaled.sem, 1)
                if final:
                    last.then_inc(y_ready.sem, 1)

            def ffn(layer, f):
                def one(i, j):
                    dve.wait_ge(silu_ready.sem, layer * silu_ready.n + (i * SLOTS + (f * FT + j + 1)))
                    v.tensor_tensor(hidden[:, bass.ds(i * SLOTS + j, 1), :].rearrange("p a n -> p (a n)"),
                                    silu[:, j % 2, :], ps[:, (j % 2) * 2 + 1, 0:TOK], ALU.mult
                                    ).then_inc(up_free.sem, 1)
                with dve.Fori(0, FT // SLOTS) as i:
                    for j in range(SLOTS):
                        one(i, j)
                for j in range(FT // SLOTS * SLOTS, FT):
                    dve.wait_ge(silu_ready.sem, silu_ready.at(layer, f * FT + j + 1))
                    v.tensor_tensor(hidden[:, j, :], silu[:, j % 2, :], ps[:, (j % 2) * 2 + 1, 0:TOK],
                                    ALU.mult).then_inc(up_free.sem, 1)
                for t in range(KT):
                    dve.wait_ge(used.sem, used.at(layer, AT[f"down{f}"] + 2 * t + 2))
                    for c, s0, s1 in SEGS:
                        last = v.scalar_tensor_tensor(out=x[:, t, s0:s1], in0=ps[:, 4 + t % 2, s0:s1],
                                                      scalar=gate_c[:, f, t, c:c + 1], in1=x[:, t, s0:s1],
                                                      op0=ALU.mult, op1=ALU.add)
                    last.then_inc(down_free.sem, 1)

            with dve.Fori(0, DEPTH) as layer:
                ada_b, norm_g = C("ada_b"), C("norm_g")
                with dve.Fori(0, 9) as i:
                    for c in range(2):
                        dve.wait_ge(cols_ready.sem, layer * 18 + (i * 2 + (c + 1)))
                        at = i * 16 + 8 * c
                        v.tensor_tensor(mod[:, bass.ds(at, 8)], ps[:, 2 + c, 0:8],
                                        ada_b[:, bass.ds(layer * 144 + at, 8)], ALU.add
                                        ).then_inc(mod_done.sem, 1)
                dve.drain()
                for n in range(3):
                    v.scalar_tensor_tensor(out=scale_c[:, n].rearrange("p t c -> p (t c)"),
                                           in0=modv[:, 3 * n + 1].rearrange("p t c -> p (t c)"), scalar=1.0,
                                           in1=norm_g[:, bass.ds(layer * 48 + 16 * n, 16)],
                                           op0=ALU.add, op1=ALU.mult)
                for f in range(2):
                    v.tensor_scalar(gate_c[:, f], modv[:, 6 * f + 2], 0.5, None, ALU.mult)
                norm(layer, 0)
                ffn(layer, 0)
                norm(layer, 1)

                dve.wait_ge(kr_ready.sem, kr_ready.at(layer, 1))
                v.tensor_copy(kr_raw[64:96, :], ps[64:96, 4, 0:SEQ])
                v.tensor_tensor(kpe[64:96, :], ps[64:96, 4, 0:TOK], C("rope")[64:96, :], ALU.mult)
                v.tensor_tensor(ropes[64:96, 0, :], ps[96:128, 4, 0:TOK], C("rope")[96:128, :], ALU.mult)
                dve.drain()
                v.tensor_tensor(kpe[64:96, :], kpe[64:96, :], ropes[64:96, 0, :], ALU.add)
                dve.drain()
                for hd in range(HEADS):
                    v.tensor_copy(KTm[64:96, hd, 0:TOK], kpe[64:96, :])
                    v.tensor_copy(KTm[64:96, hd, TOK:KEYS], S("krope")[64:96, :])
                for z in range(2):
                    v.tensor_copy(kT[:, z, TOK:KEYS], S("na_k", P)[:, z, :])
                v.tensor_copy(ckvT[:, TOK:KEYS], S("ckv"))
                dve.wait_ge(used.sem, used.at(layer, AT["v"] + 2))
                for j in range(3):
                    last = v.tensor_copy(V[:, j, :], ps[:, 5 + j, :])
                last.then_inc(v_done.sem, 1)
                dve.wait_ge(wlog_ready.sem, wlog_ready.at(layer, 1))
                for j in range(3):
                    for d in range(2):
                        last = v.tensor_tensor(sig[:, j, d * 256:(d + 1) * 256],
                                               ps[:, 2 * d + j // 2, j % 2 * 256:j % 2 * 256 + 256],
                                               S("w0")[:, d * 256:(d + 1) * 256], ALU.add)
                last.then_inc(wlog_biased.sem, 1)
                for p in range(2):
                    v.tensor_scalar(kk[:, p, :], k[:, p, :], S("kk")[:, p:p + 1], None, ALU.mult)
                dve.drain()
                v.tensor_tensor(kd[:, 0, :, :], kk[:, :, :], kk[:, :, :], ALU.mult).then_inc(kksq_ready.sem, 1)
                dve.wait_ge(kkss_ready.sem, kkss_ready.at(layer, 1))
                v.tensor_scalar(root2, ps[:, 2:4, 0:TOK], 1e-24, None, ALU.max).then_inc(kkmax_ready.sem, 1)
                v.tensor_tensor(sq3[:, 0:2, :], dq, dq, ALU.mult)
                v.tensor_tensor(sq3[:, 2, :], ckvT[:, 0:TOK], ckvT[:, 0:TOK], ALU.mult).then_inc(mla_sq.sem, 1)
                dve.wait_ge(kkroot_ready.sem, kkroot_ready.at(layer, 1))
                v.reciprocal(root2, root2)
                v.tensor_scalar(stat[:, 0:2], S("ka"), -1.0, 1.0, ALU.mult, ALU.add)
                dve.drain()
                v.tensor_tensor(kk[:, :, :], kk[:, :, :], root2, ALU.mult)
                dve.wait_ge(a_done.sem, a_done.at(layer, 1))
                for d in range(2):
                    for p in range(2):
                        v.tensor_scalar(kd[:, d, p, :], b[:, d, p, :], S("ka")[:, p:p + 1], stat[:, p:p + 1],
                                        ALU.mult, ALU.add)
                dve.drain()
                for d in range(2):
                    v.tensor_tensor(kd[:, d], kd[:, d], k[:, :, :], ALU.mult)
                    v.tensor_tensor(b[:, d], b[:, d], kk[:, :, :], ALU.mult)
                dve.drain()
                v.tensor_tensor(prod, kd[:, 0], kd[:, 1], ALU.add)
                dve.drain()
                for p in range(2):
                    last = v.scalar_tensor_tensor(out=prod[:, p, :], in0=prod[:, p, :],
                                                  scalar=S("rk")[:, p:p + 1], in1=r[:, p, :],
                                                  op0=ALU.mult, op1=ALU.mult)
                last.then_inc(prod_ready.sem, 1)
                dve.wait_ge(bonus_psum.sem, bonus_psum.at(layer, 1))
                v.tensor_copy(bonus[:, :], ps[:, 2, 0:12]).then_inc(bonus_done.sem, 1)
                dve.wait_ge(mla_root.sem, mla_root.at(layer, 1))
                v.reciprocal(prod, prod)
                dve.drain()
                for z in range(2):
                    v.scalar_tensor_tensor(out=dq[:, z, :], in0=dq[:, z, :], scalar=S("qn")[:, z:z + 1],
                                           in1=prod[:, 0, :], op0=ALU.mult, op1=ALU.mult)
                v.scalar_tensor_tensor(out=ckvT[:, 0:TOK], in0=ckvT[:, 0:TOK], scalar=S("kvn"),
                                       in1=prod[:, 1, :], op0=ALU.mult, op1=ALU.mult
                                       ).then_inc(mla_normed.sem, 1)
                dve.wait_ge(q_psum.sem, q_psum.at(layer, 1))
                v.tensor_copy(qm[0:64, :, :], ps[0:64, 0:4, 0:TOK])
                for hd in range(HEADS):
                    v.tensor_tensor(qm[64:96, hd, :], ps[64:96, hd, 0:TOK], C("rope")[64:96, :], ALU.mult)
                    v.tensor_tensor(ropes[64:96, hd, :], ps[96:128, hd, 0:TOK], C("rope")[96:128, :], ALU.mult)
                dve.drain()
                v.tensor_tensor(qm[64:96, :, :], qm[64:96, :, :], ropes[64:96, :, :], ALU.add
                                ).then_inc(q_done.sem, 1)

                def top(n):
                    br, hd, q = JOBS[n]
                    dve.wait_ge(scored.sem, scored.at(layer, n + 1))
                    width = P if q == 0 else TOK
                    src, scale = ps[:, 2 + n % 2, 0:width], HD ** -0.5 if br == 0 else (NOPE + ROPE) ** -0.5
                    if br == 0 and q > 0:
                        if n == 1:
                            dve.wait_ge(bias_ready.sem, bias_ready.at(layer, 1))
                        v.scalar_tensor_tensor(out=score[:, n % 2, :], in0=src, scalar=scale,
                                               in1=S("bias", TOK)[:, (q - 1) * 4 + hd, :],
                                               op0=ALU.mult, op1=ALU.add)
                        dve.drain()
                        src, scale = score[:, n % 2, :], 1.0
                    v.reduce_max(stat[:, 2 + n % 2:3 + n % 2], src, AX)
                    dve.drain()
                    v.tensor_scalar(stat[:, 4 + n % 2:5 + n % 2], stat[:, 2 + n % 2:3 + n % 2], -scale, None,
                                    ALU.mult).then_inc(maxed.sem, 1)

                def share(n):
                    width = P if JOBS[n][2] == 0 else TOK
                    dve.wait_ge(exped.sem, exped.at(layer, n + 1))
                    v.reciprocal(stat[:, 10 + n % 2:11 + n % 2], stat[:, 8 + n % 2:9 + n % 2])
                    dve.drain()
                    v.tensor_scalar(prob[:, n % 2, 0:width], prob[:, n % 2, 0:width],
                                    stat[:, 10 + n % 2:11 + n % 2], None, ALU.mult).then_inc(normed.sem, 1)

                def keep(n):
                    br, hd, q = JOBS[n]
                    o = 64 * (hd % 2)
                    dve.wait_ge(o_psum.sem, o_psum.at(layer, n + 1))
                    v.tensor_copy(oT[br][o:o + 64, hd // 2, q * P:(q + 1) * P], ps[o:o + 64, 6 + n % 2, 0:P]
                                  ).then_inc(o_done.sem, 1)

                for n in range(NJ + 2):
                    if n < NJ:
                        top(n)
                    if 1 <= n <= NJ:
                        share(n - 1)
                    if n >= 2:
                        keep(n - 2)

                for rd, tiles in enumerate(ROUNDS):
                    dve.wait_ge(exps_ready.sem, exps_ready.at(layer, rd + 1))
                    for d in range(2):
                        c0, c1 = tiles[d] * P, (tiles[d] + 1) * P
                        v.tensor_tensor(KR[:, d, :, 0, :], kk[:, :, c0:c1], E1[:, d, :, 1, :], ALU.mult)
                        v.tensor_tensor(KR[:, d, :, 1, :], r[:, :, c0:c1], E1[:, d, :, 0, :], ALU.mult)
                        v.tensor_tensor(KB[:, d, :, 0, :], kd[:, d, :, c0:c1], E2[:, d], ALU.mult)
                        last = v.tensor_tensor(KB[:, d, :, 1, :], b[:, d, :, c0:c1], E2[:, d], ALU.mult)
                    if rd == 0:
                        last = v.memset(s_in[:, :, :], 0.0)
                    else:
                        for z in range(4):
                            src = S("state", HD)[:, z, :] if rd == 1 else s_mid[:, z, :]
                            last = v.tensor_scalar(s_in[:, z, :], src, pmid[:, z:z + 1], None, ALU.mult)
                    last.then_inc(factors_ready.sem, 1)
                    for u, (d, p, hh) in enumerate(UNITS):
                        dve.wait_ge(gram_psum.sem, gram_psum.at(layer, 8 * rd + u + 1))
                        v.tensor_tensor(G[:, u].rearrange("p a b -> p (a b)"), ps[:, u, :], C(f"gram{d}"),
                                        ALU.mult).then_inc(gram_masked.sem, 1)
                    for m in range(LEVELS):
                        for grp in range(2):
                            sl = slice(4 * grp, 4 * grp + 4)
                            pv = lambda bank: ps[:, bank, :].rearrange("p (a b) -> p a b", b=P)
                            if m == 0:
                                eye = bcast(ident, 4)
                                dve.wait_ge(x_psum.sem, x_psum.at(layer, lev(rd, m, grp)))
                                v.tensor_tensor(T[:, sl, :], pv(2 + grp), eye, ALU.add)
                                v.tensor_tensor(Tt[:, sl, :], Nm[:, 0, sl, :], eye, ALU.add
                                                ).then_inc(t_ready.sem, 1)
                                continue
                            dve.wait_ge(tt_psum.sem, tt_psum.at(layer, lev1(rd, m, grp)))
                            if m < LEVELS - 1:
                                v.tensor_tensor(T[:, sl, :], T[:, sl, :], pv(4 + grp), ALU.add)
                            v.tensor_tensor(Tt[:, sl, :], Tt[:, sl, :], pv(6 + grp), ALU.add
                                            ).then_inc(t_ready.sem, 1)
                        if m == 0:
                            dve.drain()
                    dve.wait_ge(f_psum.sem, f_psum.at(layer, rd + 1))
                    for hh in range(2):
                        last = v.tensor_copy(Fm[:, hh::2, :], ps[:, hh, 0:256].rearrange("p (a b) -> p a b", b=HD))
                    last.then_inc(f_ready.sem, 1)
                    dve.wait_ge(u_psum.sem, u_psum.at(layer, rd + 1))
                    v.tensor_copy(Um.rearrange("p a b -> p (a b)"), ps[:, 2, :]).then_inc(u_ready.sem, 1)
                    dve.drain()
                    dve.wait_ge(y_psum.sem, y_psum.at(layer, rd + 1))
                    for d in range(2):
                        if rd == 0 and d == 1:
                            dve.drain()
                        for hh in range(2):
                            src = ps[:, 3 + hh, d * P:(d + 1) * P].rearrange("p (a b) -> p a b", b=HD)
                            dst = Y[:, tiles[d], :].rearrange("p (a c b) -> p a c b", c=2, b=HD)[:, :, hh, :]
                            if rd == 2 or (rd == 0 and d == 1):
                                v.tensor_tensor(dst, dst, src, ALU.add)
                            else:
                                v.tensor_copy(dst, src)
                    if rd < 2:
                        s_new = (s_out, s_mid)[rd]
                        v.tensor_tensor(s_new[:, :, :].rearrange("p a b -> p (a b)"), ps[:, 5, 0:256],
                                        s_in[:, :, :].rearrange("p a b -> p (a b)"), ALU.add)
                        dve.drain()
                        for z in range(4):
                            at_end = P - 1 if z < 2 else 0
                            last = v.tensor_scalar(s_new[:, z, :], s_new[:, z, :],
                                                   E1[:, z // 2, z % 2, 0, at_end:at_end + 1], None, ALU.mult)
                        last.then_inc(round_done.sem, 1)
                    else:
                        dve.drain().then_inc(round_done.sem, 1)

                Yh = Y[:, :, :].rearrange("p a (h c) -> p (a h) c", c=HD)
                sqY = view(big, 4096, 12, HD)
                bv = view(big, 4096 + 768, 3, 256)
                v.tensor_reduce(stat[:, 12:24], Yh, AX, ALU.add)
                dve.drain()
                v.tensor_scalar(stat[:, 12:24], stat[:, 12:24], 1.0 / HD, None, ALU.mult)
                dve.drain()
                v.tensor_tensor(Yh, Yh, spread(stat[:, 12:24], HD), ALU.subtract)
                dve.drain()
                v.tensor_tensor(sqY, Yh, Yh, ALU.mult)
                dve.drain()
                v.tensor_reduce(stat[:, 12:24], sqY, AX, ALU.add).then_inc(gn_var.sem, 1)
                for j in range(3):
                    v.tensor_tensor(bv[:, j, :].rearrange("p (h c) -> p h c", c=HD),
                                    V[:, j, 256:512].rearrange("p (h c) -> p h c", c=HD),
                                    spread(bonus[:, 4 * j:4 * j + 4], HD), ALU.mult)
                dve.wait_ge(gn_root.sem, gn_root.at(layer, 1))
                v.reciprocal(stat2[:, 12:24], stat2[:, 0:12])
                dve.drain()
                v.tensor_tensor(Yh, Yh, spread(stat2[:, 12:24], HD), ALU.mult)
                dve.drain()
                v.tensor_tensor(Y[:, :, :], Y[:, :, :], bcast(S("gnw"), 3), ALU.mult)
                dve.drain()
                v.tensor_tensor(Y[:, :, :], Y[:, :, :], bcast(S("gnb"), 3), ALU.add)
                dve.drain()
                v.tensor_tensor(Y[:, :, :], Y[:, :, :], bv, ALU.add)
                dve.drain()
                v.tensor_tensor(Y[:, :, :], Y[:, :, :], g[:, :, :], ALU.mult).then_inc(rw_out.sem, 1)

                for n in range(24):
                    t, br = n // 3, n % 3
                    dve.drain()
                    if n == 0:
                        dve.wait_ge(gate_done.sem, gate_done.at(layer, 24))
                    dve.wait_ge(br_psum.sem, br_psum.at(layer, n + 1))
                    src = ps[:, 4 + n % 4, 0:TOK]
                    if br == 0:
                        v.tensor_tensor(h[:, t, :], src, hidden[:, n, :], ALU.mult).then_inc(br_free.sem, 1)
                    else:
                        v.tensor_tensor(brtmp, src, hidden[:, n, :], ALU.mult).then_inc(br_free.sem, 1)
                        dve.drain()
                        last = v.tensor_tensor(h[:, t, :], h[:, t, :], brtmp, ALU.add)
                last.then_inc(comb_ready.sem, 1)
                for t in range(KT):
                    dve.wait_ge(used.sem, used.at(layer, AT["out"] + t // 2 + 1))
                    for c, s0, s1 in SEGS:
                        last = v.scalar_tensor_tensor(out=x[:, t, s0:s1], in0=ps[:, t % 4, s0:s1],
                                                      scalar=modv[:, 5, t, c:c + 1], in1=x[:, t, s0:s1],
                                                      op0=ALU.mult, op1=ALU.add)
                    last.then_inc(out_free.sem, 1)
                norm(layer, 2)
                ffn(layer, 1)
            norm(DEPTH, 0, final=True)

        @blk.gpsimd
        def _(pool):
            g_ = nc.gpsimd
            with pool.Fori(0, DEPTH) as layer:
                pool.wait_ge(const_landed.sem, 16)
                pool.wait_ge(small_landed.sem, small_landed.at(layer, 16))
                for n in range(8):
                    tab = S("bias", TOK)[:, n, 0:256].rearrange("p (a b) -> p a b", b=64)
                    last = g_.tensor_tensor(tab, tab, bcast(C("okcol"), 4), ALU.mult)
                pool.drain()
                for n in range(8):
                    tab = S("bias", TOK)[:, n, 0:256].rearrange("p (a b) -> p a b", b=64)
                    last = g_.tensor_tensor(tab, tab, bcast(C("negcol"), 4), ALU.add)
                last.then_inc(bias_ready.sem, 1)
                for rd in range(3):
                    for m in range(LEVELS):
                        for grp in range(2):
                            if m == 0:
                                pool.wait_ge(gram_masked.sem, gram_masked.at(layer, 8 * rd + 4 * grp + 4))
                                if rd == 0:
                                    pool.wait_ge(exps_ready.sem, exps_ready.at(layer, 1))
                            if m >= 2:
                                pool.wait_ge(x_psum.sem, x_psum.at(layer, lev(rd, m - 2, grp)))
                                pool.wait_ge(t_ready.sem, t_ready.at(layer, lev(rd, m - 2, grp)))
                            g_.tensor_tensor(Nm[:, m % 2, 4 * grp:4 * grp + 4, :],
                                             G[:, 4 * grp:4 * grp + 4, 2, :],
                                             bcast(C(f"level{grp}", P)[:, m, :], 4), ALU.mult
                                             ).then_inc(level_masked.sem, 1)


def packed(where, width, lead=()):
    a = np.zeros((*lead, P, width), np.float32)

    def put(name, v):
        lo, hi = where[name]
        v = np.asarray(v)
        v = v.reshape(*v.shape[:len(lead) + 1], -1)
        a[..., lo:lo + v.shape[-1]] = v
        assert v.shape[-1] <= hi - lo
    return a, put


def shape_constants():
    i = np.arange(P)
    s, t = i[:, None], i[None, :]
    out = {"ident": np.eye(P), "ones": np.ones((P, P)), "block": s // 64 == t // 64}
    for d in range(2):
        before = (s < t) if d == 0 else (s > t)
        upto = (s <= t) if d == 0 else (s >= t)
        mid = (s < 64) if d == 0 else (s >= 64)
        out[f"cum{d}"] = np.concatenate([upto * 1.0 - mid, before * 1.0 - mid], 1)
        out[f"gram{d}"] = np.concatenate([before * 1.0, upto * 1.0, before * -1.0, upto * -1.0], 1)
        levels = []
        for lv in range(LEVELS):
            m = 1 << lv
            half_s, half_t = s // m % 2, t // m % 2
            levels.append((s // (2 * m) == t // (2 * m)) & ((half_s == d) & (half_t == 1 - d)))
        out[f"level{d}"] = np.stack(levels, 1)
    heads = np.zeros((P, 2, 4))
    for p in range(2):
        for hh in range(2):
            heads[64 * hh:64 * hh + 64, p, 2 * p + hh] = 1
    out["heads"] = heads
    qc, kc = i % 64, np.arange(64)
    lo = np.clip(qc - 8, 0, 48)[:, None]
    ok = (kc[None] >= lo) & (kc[None] < lo + 16)
    out["okcol"], out["negcol"] = ok, np.where(ok, 0.0, -1e30)
    n_freq = ROPE // 4
    inv = 1.0 / (10000.0 ** (np.arange(n_freq) / n_freq))
    pos = np.arange(DEC)
    ang = np.concatenate([(pos // 64)[:, None] * inv, (pos % 64)[:, None] * inv], -1).T
    rope = np.zeros((P, TOK))
    rope[64:96, 0:SEQ] = 1
    rope[64:96, SEQ:] = np.concatenate([np.cos(ang)] * 2)
    rope[96:112, SEQ:], rope[112:128, SEQ:] = -np.sin(ang), np.sin(ang)
    out["rope"] = rope
    pick = np.zeros((P, 2))
    pick[0::32, 0] = pick[1::32, 1] = 1
    out["pick"] = pick
    out["eps"] = np.tile([1e-6, 64e-5, 0, 0], (P, 1))
    return out


def by_feature(v, lead):
    return np.swapaxes(v.reshape(*v.shape[:lead], -1, P), -1, -2)


def weight_stream(w):
    out = np.zeros((DEPTH * NBLK, P, WIDE), np.float32)
    for layer in range(DEPTH):
        def put(name, i, v):
            v = v.reshape(P, -1)
            out[layer * NBLK + AT[name] + i, :, 0:v.shape[1]] = v

        def tiles(m):
            return m.reshape(m.shape[0] // P, P, m.shape[1] // P, P).transpose(1, 2, 0, 3)

        ada = w["ada_w"][layer].reshape(KT, P, 18, 512)
        for c in range(18):
            for half in range(2):
                put("ada", 2 * c + half, ada[4 * half:4 * half + 4, :, c].transpose(1, 0, 2))
        for f in range(2):
            wg, wu = tiles(w["ffn_wg"][layer, f]), tiles(w["ffn_wu"][layer, f])
            wd = tiles(w["ffn_wd"][layer, f])
            for t in range(FT):
                put(f"up{f}", t, np.stack([wg[:, t], wu[:, t]], 1))
            for t in range(KT):
                for half in range(2):
                    put(f"down{f}", 2 * t + half, wd[:, t, 11 * half:11 * half + 11])
        w_in = w["w_in"][layer]
        feat = tiles(np.concatenate([w_in[:, 0:512], w_in[:, 768:1280], w_in[:, 1536:2304]], 1))
        for i in range(7):
            put("proj", i, feat[:, 2 * i:2 * i + 2])
        vals = np.concatenate([w_in[:, 512:768], w_in[:, 1280:1536]], 1).reshape(KT, P, 512)
        for half in range(2):
            put("v", half, vals[4 * half:4 * half + 4].transpose(1, 0, 2))
        gates = tiles(w_in[:, 2336:])
        order = [br * KT + t for t in range(KT) for br in range(3)]
        for i in range(12):
            put("gate", i, gates[:, order[2 * i:2 * i + 2]])
        br = np.stack([tiles(w["w_br"][layer, n]) for n in range(3)], 2).reshape(P, 24, 2, P)
        for i in range(3):
            put("branch", i, br[:, 8 * i:8 * i + 8])
        wo = tiles(w["w_o"][layer])
        for i in range(4):
            put("out", i, wo[:, 2 * i:2 * i + 2])
    return out


def swap_halves(a):
    return np.concatenate([a[..., ROPE // 2:], a[..., :ROPE // 2]], -1)


def small_weights(w):
    a, put = packed(SMALL, NSMALL, (DEPTH,))
    L = DEPTH
    put("kk", by_feature(w["rw_kk"], 1))
    put("ka", by_feature(w["rw_ka"], 1))
    put("rk", by_feature(w["rw_rk"].reshape(L, 256), 1))
    put("a0", by_feature(w["rw_a0"].reshape(L, 512), 1))
    put("qn", by_feature(w["mla_qn_g"], 1))
    put("kvn", by_feature(w["mla_kvn_g"], 1))
    put("w2", w["rw_w2"].reshape(L, P, 256))
    put("a2", w["rw_a2"].reshape(L, P, 256))
    put("g2", w["rw_g2"])
    for name, v in (("w0", w["rw_w0"].reshape(L, 1, 512)), ("gnw", w["rw_gn_w"][:, None]),
                    ("gnb", w["rw_gn_b"][:, None])):
        put(name, np.broadcast_to(v, (L, P, v.shape[-1])))
    uq = w["mla_w_uq"].reshape(L, 2, P, 4, NOPE + ROPE)
    put("uq", np.concatenate([uq, swap_halves(uq[..., NOPE:])], -1).transpose(0, 2, 1, 3, 4))
    ukv = w["mla_w_ukv"].reshape(L, P, 4, 2, 64)
    put("ukv_k", ukv[:, :, :, 0])
    put("ukv_v", ukv[:, :, :, 1])
    kr = w["w_in"][:, :, 2304:2336]
    kr = np.concatenate([kr, swap_halves(kr)], -1).reshape(L, KT, P, 64)
    put("kr", kr.transpose(0, 2, 1, 3))
    nk = w["cache_na_k"][0].reshape(L, 2, 2, P, HD)
    put("na_k", nk.transpose(0, 2, 4, 1, 3).reshape(L, P, 256))
    put("na_v", w["cache_na_v"][0].transpose(0, 2, 1, 3).reshape(L, P, 256))
    put("ckv", w["cache_mla_ckv"][0].transpose(0, 2, 1))
    lo = SMALL["krope"][0]
    a[:, 64:96, lo:lo + P] = w["cache_mla_krope"][0].transpose(0, 2, 1)
    st = np.stack([w["state_rwkv_fwd"][0], w["state_rwkv_bwd"][0]], 1).reshape(L, 2, 2, 2, HD, HD)
    put("state", st.transpose(0, 3, 5, 1, 2, 4).reshape(L, P, 256))
    q, n = np.arange(DEC), np.arange(DEC)
    row = n[None] // 64 - q[:, None] // 64 + 7
    col = np.clip(n[None] % 64 - q[:, None] % 64 + 15, 0, 30)
    tab = w["na_rpb"][:, :, row, col].reshape(L, 4, 2, P, DEC)
    full = np.zeros((L, P, 2, 4, TOK), np.float32)
    full[..., 0:DEC] = tab.transpose(0, 3, 2, 1, 4)
    put("bias", full)
    return a


def constants(w):
    a, put = packed(CONST, NCONST)
    for name, v in shape_constants().items():
        put(name, v)
    put("final_g", by_feature(w["final_g"], 0))
    cond = np.zeros((P, KT, 32), np.float32)
    cond[:, :, 0], cond[:, :, 1] = by_feature(w["c_ctx"], 0), by_feature(w["c"][0], 0)
    put("cond", cond)
    put("ada_b", np.repeat(by_feature(w["ada_b"], 1).transpose(1, 0, 2)[..., None], 2, -1))
    put("norm_g", np.repeat(by_feature(w["norm_g"], 2).transpose(2, 0, 1, 3)[..., None], 2, -1))
    return a


_OUTS = [("y", (P, KT, TOK)), ("k", (DEPTH, P, 2, SEQ)), ("v", (DEPTH, P, 256)),
         ("ckv", (DEPTH, P, SEQ)), ("kr", (DEPTH, ROPE, SEQ)), ("s", (DEPTH, P, 4, HD))]


def kernel(**inputs):
    import concourse.bacc as _bacc
    from concourse.bass_utils import run_bass_kernel_spmd as _run

    w = {name: np.asarray(a) for name, a in inputs.items()}
    tokens = np.concatenate([w["x_prompt"][0], w["x_sample"][0]], 0)
    arrays = {
        "wstream": weight_stream(w),
        "small_d": small_weights(w),
        "const_d": constants(w),
        "x_d": np.ascontiguousarray(tokens.T.reshape(KT, P, TOK).transpose(1, 0, 2)),
    }
    nc = _bacc.Bacc("TRN2", target_bir_lowering=False, num_devices=1)
    f32 = mybir.dt.float32
    args = [nc.dram_tensor(n, a.shape, f32, kind="ExternalInput").ap() for n, a in arrays.items()]
    args += [nc.dram_tensor(f"out_{n}", s, f32, kind="ExternalOutput").ap() for n, s in _OUTS]
    hybrid_step(nc, *args)
    res = _run(nc, [arrays], core_ids=[0]).results[0]
    y, k, v, ckv, kr, s = (res[f"out_{n}"] for n, _ in _OUTS)
    y = y.transpose(2, 1, 0).reshape(TOK, D)
    k = k.reshape(DEPTH, 2, HD, 2, SEQ).transpose(0, 3, 1, 4, 2).reshape(1, DEPTH, HEADS, SEQ, HD)
    v = v.reshape(DEPTH, SEQ, HEADS, HD).transpose(0, 2, 1, 3)[None]
    s = s.reshape(DEPTH, 2, HD, 2, 2, HD).transpose(3, 0, 4, 1, 5, 2).reshape(2, 1, DEPTH, HEADS, HD, HD)
    return (y[None, 0:SEQ], y[None, SEQ:], k, v, ckv.transpose(0, 2, 1)[None],
            kr.transpose(0, 2, 1)[None], s[0], s[1])
```

```python
from contextlib import ExitStack

import concourse.bass as bass
from concourse import mybir
import numpy as np

P = 128
DEPTH, D, DFF = 2, 1024, 2816
SEQ, DEC = 128, 256
TOK = SEQ + DEC
KEYS = TOK + 128
KT, FT = D // P, DFF // P
HEADS, HD, ROPE, NOPE = 4, 64, 32, 64
NMOD = 9
CHUNK = 128
LEVELS = 7
SEGS = ((0, 0, SEQ), (1, SEQ, TOK))
DECAY = float(np.exp(-0.5))

WIDE, NARROW = 16 * P, 11 * P
ADA, ADA0, HALF = 36, 14, FT // 2
FFN0 = [("up00", 2 * HALF), ("down00", KT), ("up01", 2 * HALF), ("down01", KT)]
FFN1 = [("up10", HALF), ("down10", KT), ("up11", HALF), ("down11", KT)]
MIX = [(name, 1) for q in range(6) for name in (f"gate{2 * q}", f"gate{2 * q + 1}", f"branch{q}")]
STAGES = [("ada", ADA0)] + FFN0 + [("proj", 7), ("kr", 1), ("v", 2)] + MIX + [("out", 4)] + FFN1
AT, NBLK = {}, 0
for _name, _n in STAGES:
    AT[_name] = NBLK
    NBLK += _n
SLOTS = 4
assert NBLK % SLOTS == 0 and ADA - ADA0 == FT

PIECES = []


def _pieces(name, n, step=1, first=0, cols=(0, 8 * P, 16 * P)):
    PA.setdefault(name, len(PIECES))
    for i in range(n):
        for c0, c1 in zip(cols[:-1], cols[1:]):
            PIECES.append((AT[name] + first + step * i, c0, c1))


PA = {}
DOWN_CUT = (0, 6 * P, 11 * P)
for _h in range(2):
    _pieces(f"up0{_h}", HALF, 2, 1)
    _pieces(f"down0{_h}", KT, cols=DOWN_CUT)
_pieces("proj", 7)
_pieces("kr", 1, cols=(0, 4 * P, 8 * P))
_pieces("v", 2)
for _q in range(12):
    _pieces(f"gate{_q}", 1)
_pieces("out", 4)
for _h in range(2):
    _pieces(f"up1{_h}", HALF)
    _pieces(f"down1{_h}", KT, cols=DOWN_CUT)
NPIECE = len(PIECES)
assert NPIECE % 2 == 0 and all(p % 2 == 0 for p in PA.values())


def layout(parts):
    at, where = 0, {}
    for name, n in parts:
        where[name] = (at, at + n)
        at += n
    return where, at


CONST, NCONST = layout([
    ("ident", P), ("ones", P), ("block", P), ("cum0", 2 * P), ("cum1", 2 * P),
    ("level0", LEVELS * P), ("level1", LEVELS * P), ("gram0", 4 * P), ("gram1", 4 * P),
    ("heads", 8), ("okcol", 64), ("negcol", 64), ("rope", TOK), ("pick", 2), ("final_g", KT),
    ("cond", KT * 32), ("eps", 4), ("ada_b", DEPTH * 144), ("norm_g", DEPTH * 48)])
SMALL, NSMALL = layout([
    ("kk", 2), ("ka", 2), ("rk", 2), ("a0", 4), ("qn", 2), ("kvn", 1), ("pad", 3),
    ("w2", 256), ("a2", 256), ("g2", 256), ("w0", 512), ("gnw", 256), ("gnb", 256),
    ("uq", 1024), ("ukv_k", 256), ("ukv_v", 256), ("na_k", 256), ("na_v", 256),
    ("ckv", P), ("krope", P), ("state", 256), ("bias", 3072)])

JOBS = [(b, h, q) for b in range(2) for h in range(HEADS) for q in range(3)]
ROUNDS = [(0, 0), (1, 2), (2, 1)]
UNITS = [(d, p, hh) for d in range(2) for p in range(2) for hh in range(2)]


def hybrid_step(nc, wstream, small_d, const_d, x_d, y_d, k_d, v_d, ckv_d, kr_d, s_d):
    F32, F32R = mybir.dt.float32, mybir.dt.float32r
    ALU, ACT, AX = mybir.AluOpType, mybir.ActivationFunctionType, mybir.AxisListType.X

    with ExitStack() as ctx:
        def sb(name, *shape):
            return ctx.enter_context(nc.sbuf_tensor(name, [P, *shape], F32))

        const = sb("const", NCONST)
        small = sb("small", NSMALL)
        ring = sb("ring", SLOTS, WIDE)
        x = sb("x", KT, TOK)
        w_hi = ctx.enter_context(nc.sbuf_tensor("w_hi", [P, 2, 8 * P], F32R))
        w_lo = ctx.enter_context(nc.sbuf_tensor("w_lo", [P, 2, 8 * P], F32R))
        tmp = sb("tmp", 2432)
        rinv = sb("rinv", TOK)
        mod = sb("mod", NMOD * KT * 2)
        ada_b = sb("ada_b", NMOD * KT * 2)
        scale_c = sb("scale_c", 3, KT, 2)
        gate_c = sb("gate_c", 2, KT, 2)
        bonus = sb("bonus", 12)
        s_out = sb("s_out", 4, HD)
        s_mid = sb("s_mid", 4, HD)
        s_in = sb("s_in", 4, HD)
        pmid = sb("pmid", 4)
        pend = sb("pend", 2, 2, 2)
        stat = sb("stat", 32)
        stat2 = sb("stat2", 32)
        kr_raw = sb("kr_raw", SEQ)
        with ExitStack() as region:
            def mx(name, *shape):
                return region.enter_context(nc.sbuf_tensor(name, [P, *shape], F32))
            sig = mx("sig", 3, 512)
            b = mx("b", 2, 2, TOK)
            kd = mx("kd", 2, 2, TOK)
            g = mx("g", 3, 256)
            kk = mx("kk", 2, TOK)
            V = mx("V", 3, 512)
            r = mx("r", 2, TOK)
            k = mx("k", 2, TOK)
            Y = mx("Y", 3, 256)
            oT = [mx(f"oT{i}", 2, TOK) for i in range(2)] + [k]
            big = mx("big", 24 * TOK)
        with ExitStack() as region:
            def mr(name, *shape):
                return region.enter_context(nc.sbuf_tensor(name, [P, *shape], F32R))
            hA = mr("hA_hi", KT, TOK), mr("hA_lo", KT, TOK)
            mr("gap_a", 5376)
            hid = mr("hid_hi", HALF, TOK), mr("hid_lo", HALF, TOK)
        with ExitStack() as region:
            mr("gap_b", 6144 + 5376)
            hB = mr("hB_hi", KT, TOK), mr("hB_lo", KT, TOK)
        ps = ctx.enter_context(nc.psum_tensor("ps", [P, 8, 512], F32))

        def C(name, *dims):
            a, e = CONST[name]
            v = const[:, a:e]
            return v.rearrange("p (a b) -> p a b", b=dims[0]) if dims else v

        def S(name, b_=None):
            a, e = SMALL[name]
            v = small[:, a:e]
            return v.rearrange("p (a b) -> p a b", b=b_) if b_ else v

        def bcast(ap, times):
            return ap.unsqueeze(1).broadcast_to([ap.shape[0], times, ap.shape[1]])

        def spread(ap, width):
            return ap.unsqueeze(2).broadcast_to([ap.shape[0], ap.shape[1], width])

        def view(t, at, *dims):
            n = 1
            for d_ in dims:
                n *= d_
            v = t[:, at:at + n]
            if len(dims) == 2:
                return v.rearrange("p (a b) -> p a b", b=dims[1])
            if len(dims) == 3:
                return v.rearrange("p (a b c) -> p a b c", b=dims[1], c=dims[2])
            if len(dims) == 4:
                return v.rearrange("p (a b c d) -> p a b c d", b=dims[1], c=dims[2], d=dims[3])
            return v

        root, rows = view(tmp, 0, TOK), view(tmp, TOK, 2, 256)
        htmp = view(tmp, 896, 3, TOK)
        silu, product = view(tmp, 896, 2, TOK), view(tmp, 896 + 2 * TOK, 2, TOK)
        sq = view(tmp, 896, 2, TOK)
        root2 = view(tmp, 0, 2, TOK)
        prod = view(tmp, 2 * TOK, 2, TOK)
        ropes = view(tmp, 0, 4, TOK)
        prob, probT = view(tmp, 0, 3, TOK), view(tmp, 3 * TOK, 2, TOK)
        KBt = view(tmp, 0, 2, 512)
        Fm, Um = view(tmp, 1024, 8, HD), view(tmp, 1536, 8, HD)
        gsig, brtmp, comb = (view(big, 6144, 4, TOK), view(big, 6144 + 4 * TOK, 2, TOK),
                             view(big, 6144 + 6 * TOK, 2, TOK))
        KTm = view(big, 0, 4, KEYS)
        kT = view(big, 2048, 2, KEYS)
        qT = view(big, 3072, 2, TOK)
        qm = view(big, 3840, 4, TOK)
        Vm = view(big, 5376, 4, 256)
        ckvT = view(big, 6400, KEYS)
        dq = view(big, 6912, 2, TOK)
        kpe = view(big, 7680, TOK)
        sq3 = view(big, 8064, 3, TOK)
        G = view(big, 0, 8, 4, P)
        T, Tt, X = (view(big, 4096 + 1024 * i, 8, P) for i in range(3))
        Nm = view(big, 7168, 2, 8, P)
        b0 = SMALL["bias"][0]
        E1 = view(small, b0, 2, 2, 2, P)
        E2 = view(small, b0 + 1024, 2, 2, P)
        KR = view(small, b0 + 1536, 2, 2, 2, P)
        KB = view(small, SMALL["uq"][0], 2, 2, 2, P)
        w1t, a1 = oT[1][:, 0, :], oT[1][:, 1, :]
        g1s = view(Y[:, :, :].rearrange("p a b -> p (a b)"), 0, TOK)
        ident, ones, block = C("ident"), C("ones"), C("block")
        eps6, epsgn = C("eps")[:, 0:1], C("eps")[:, 1:2]
        modv = mod[:, :].rearrange("p (m t c) -> p m t c", t=KT, c=2)

        class Signal:
            def __init__(self, name, per_layer, credit=0):
                self.sem = ctx.enter_context(nc.semaphore(name))
                self.n, self.credit = per_layer, credit

            def at(self, layer, count):
                return layer * self.n + (count + self.credit)

        landed = [Signal(f"landed{i}", 16 * NBLK // SLOTS) for i in range(SLOTS)]
        slot_free = [Signal(f"slot_free{i}", NBLK // SLOTS, 1) for i in range(SLOTS)]
        hi_ready, split_ready = Signal("piece_hi_ready", NPIECE), Signal("piece_split", NPIECE)
        piece_used = Signal("piece_used", NPIECE, 2)
        ada_psum = Signal("ada_psum", ADA)
        hid_hi, hid_ready = Signal("hid_hi_ready", 2 * FT), Signal("hid_ready", 2 * FT)
        const_landed = Signal("const_landed", 0)
        x_landed = Signal("x_landed", 0)
        small_landed = Signal("small_landed", 16)
        cond_ready = Signal("cond_ready", 0)
        rows_ready = Signal("ada_rows_ready", ADA)
        cols_ready = Signal("ada_cols_ready", ADA)
        mod_done = Signal("mod_done", ADA, 1)
        sq_ready, ss_step = Signal("square_ready", 24), Signal("sumsq_step", 24)
        root_ready = Signal("root_ready", 3)
        h_scaled, h_hi, h_ready = (Signal(n, 32) for n in ("h_scaled", "h_hi_ready", "h_ready"))
        silu_ready = Signal("silu_ready", 2 * FT)
        up_free = Signal("up_banks_free", 2 * FT, 2)
        down_free = Signal("down_banks_free", 32, 2)
        proj_done = Signal("proj_done", 14 + 24)
        v_done = Signal("v_done", 1)
        wlog_ready, wlog_biased, sig_ready = (Signal(n, 1) for n in ("wlog_ready", "wlog_biased", "sig_ready"))
        a_ready, a_done = Signal("a_ready", 1), Signal("a_done", 1)
        g_ready, g_done = Signal("g_ready", 1), Signal("g_done", 1)
        kksq_ready, kkss_ready, kkmax_ready, kkroot_ready = (
            Signal(n, 1) for n in ("kksq_ready", "kkss_ready", "kkmax_ready", "kkroot_ready"))
        prod_ready, bonus_psum, bonus_done = (Signal(n, 1) for n in ("prod_ready", "bonus_psum", "bonus_done"))
        mla_sq, mla_ss, mla_root, mla_normed = (
            Signal(n, 1) for n in ("mla_sq", "mla_ss", "mla_root", "mla_normed"))
        q_psum, q_done, kn_psum, kn_done, vm_psum, vm_done = (
            Signal(n, 1) for n in ("q_psum", "q_done", "kn_psum", "kn_done", "vm_psum", "vm_done"))
        bias_ready = Signal("bias_ready", 1)
        NJ = len(JOBS)
        scored, maxed, exped, normed, pT_psum, pT_ready, o_psum, o_done = (
            Signal(n, NJ) for n in ("scored", "maxed", "exped", "normed", "pT_psum", "pT_ready", "o_psum", "o_done"))
        cum_ready, exps_ready, factors_ready = (Signal(n, 3) for n in ("cum_ready", "exps_ready", "factors_ready"))
        gram_psum, gram_masked = Signal("gram_psum", 24), Signal("gram_masked", 24)
        kbt_psum, kbt_ready = Signal("kbt_psum", 3), Signal("kbt_ready", 3)
        level0_masked, level_masked = Signal("level0_masked", 6), Signal("level_masked", 3 * (LEVELS - 1) * 2)
        t_ready = Signal("inv_t_ready", 3 * LEVELS * 2)
        x_ready = Signal("inv_x_ready", 3 * (LEVELS - 1) * 2)
        inv_psum = Signal("inv_psum", 3 * (4 * LEVELS - 2))
        f_psum, f_ready, y_psum, round_done, state_ready = (
            Signal(n, 3) for n in ("f_psum", "f_ready", "y_psum", "round_done", "state_ready"))
        u_psum, u_ready = Signal("u_psum", 6), Signal("u_ready", 6)
        Y_psum, Y_ready, gn_var, gn_root, rw_out, rwT_ready = (
            Signal(n, 1) for n in ("rw_tokens_psum", "rw_tokens_ready", "gn_var", "gn_root", "rw_out", "rwT_ready"))
        br_psum, br_free = Signal("br_psum", 25), Signal("br_free", 24)
        comb_sum, comb_hi, comb_ready = (Signal(n, 8) for n in ("comb_sum", "comb_hi_ready", "comb_ready"))
        out_free = Signal("out_free", 8, 8)
        kv_stored, s_stored = Signal("kv_stored", 64), Signal("s_stored", 16)
        y_ready, y_stored = Signal("y_ready", 0), Signal("y_stored", 0)

        def lev(rd, m, grp):
            return (rd * LEVELS + m) * 2 + grp + 1

        def lev1(rd, m, grp):
            return (rd * (LEVELS - 1) + m - 1) * 2 + grp + 1

        def inv_x(rd, m, grp):
            return rd * (4 * LEVELS - 2) + (4 * m - 2 if m else 0) + grp + 1

        def inv_tt(rd, m, grp):
            return inv_x(rd, m, grp) + 2

        blk = ctx.enter_context(nc.Block())

        @blk.sync
        def _(sp):
            sp.dma_start(const[:, :], const_d).then_inc(const_landed.sem, 16)
            sp.dma_start(x[:, :, :], x_d).then_inc(x_landed.sem, 16)

            def load(layer, n, slot, cols, turn):
                row = sp.snap(layer * NBLK + n)
                freed = sp.snap(layer * (NBLK // SLOTS) + turn)
                sp.wait_ge(slot_free[slot].sem, freed)
                sp.dma_start(ring[:, slot, 0:cols],
                             wstream[bass.ds(row, 1), :, 0:cols].rearrange("a p n -> (a p) n")
                             ).then_inc(landed[slot].sem, 16)

            with sp.Fori(0, DEPTH) as layer:
                for name, n in STAGES:
                    cols = NARROW if name.startswith("down") else WIDE
                    off = AT[name]
                    if n >= 2 * SLOTS:
                        with sp.Fori(0, n // SLOTS) as i:
                            for j in range(SLOTS):
                                load(layer, i * SLOTS + (off + j), (off + j) % SLOTS, cols,
                                     i + ((off + j) // SLOTS + 1))
                    for j in range(n if n < 2 * SLOTS else n % SLOTS):
                        at = off + (0 if n < 2 * SLOTS else n // SLOTS * SLOTS) + j
                        load(layer, at, at % SLOTS, cols, at // SLOTS + 1)
                    if name == "ada":
                        row = sp.snap(layer + 0)
                        sp.wait_ge(out_free.sem, out_free.at(layer, 0))
                        sp.dma_start(small[:, :], small_d[bass.ds(row, 1)].rearrange("a p n -> (a p) n")
                                     ).then_inc(small_landed.sem, 16)
            sp.wait_ge(y_ready.sem, 1)
            sp.dma_start(y_d, x[:, :, :]).then_inc(y_stored.sem, 16)
            sp.wait_ge(y_stored.sem, 16)

        @blk.tensor
        def _(pe):
            mm = nc.tensor.matmul
            for s_ in slot_free:
                pe.sem_inc(s_.sem, 1)
            pe.sem_inc(piece_used.sem, 2)
            pe.wait_ge(const_landed.sem, 16)

            def block_of(layer, off, i=0):
                slot = off % SLOTS
                pe.wait_ge(landed[slot].sem,
                           layer * (16 * NBLK // SLOTS) + (i * 16 + 16 * (off // SLOTS + 1)))
                return ring[:, slot, :]

            def sumsq(layer, n, t, src):
                pe.wait_ge(sq_ready.sem, sq_ready.at(layer, 8 * n + t + 1))
                mm(ps[:, 6, 0:TOK], ones, src, start=t == 0, stop=t == KT - 1).then_inc(ss_step.sem, 1)

            def piece_of(layer, n, shift=0):
                pe.wait_ge(split_ready.sem, layer * NPIECE + (shift + (n + 1)))
                return w_hi[:, n % 2, :], w_lo[:, n % 2, :]

            def mm3(out, stat_, mov, start, stop):
                mm(out, stat_[0], mov[0], start=start, stop=False)
                mm(out, stat_[0], mov[1], start=False, stop=False)
                return mm(out, stat_[1], mov[0], start=False, stop=stop)

            def both(pair, *at):
                return pair[0][at], pair[1][at]

            ALLP = slice(None)

            def tile8(layer, w, c0, n, h, out, hcount=None):
                for t in range(KT):
                    if hcount is not None:
                        pe.wait_ge(h_ready.sem, h_ready.at(layer, hcount + t + 1))
                    last = mm3(out, both(w, ALLP, slice(t * P, (t + 1) * P)), both(h, ALLP, t, ALLP),
                               t == 0, t == KT - 1)
                return last

            def up(layer, f, half, i, tile, parity, off, hcount):
                for z in range(2):
                    w = piece_of(layer, off + z, i * 4)
                    if z == 0:
                        pe.wait_ge(up_free.sem, layer * up_free.n + (tile + (f * FT + half * HALF + 1)))
                    tile8(layer, w, 0, KT, hA, ps[:, parity * 2 + z, 0:TOK],
                          hcount if z == 0 else None).then_inc(piece_used.sem, 1)

            def ada_rows(layer, off, i, parity):
                w = block_of(layer, off, i)
                for t in range(KT):
                    q = t % 4
                    last = mm(ps[32 * q:32 * q + 32, 4 + parity, 0:256], C("cond", 32)[:, t, :],
                              w[:, t * 256:(t + 1) * 256], start=t < 4, stop=t >= 4)
                last.then_inc(ada_psum.sem, 1)

            def ada_cols(layer, chunk, parity, off):
                pe.wait_ge(rows_ready.sem, layer * ADA + (chunk + 1))
                pe.wait_ge(mod_done.sem, layer * ADA + (chunk + 1))
                for j in range(2):
                    last = mm(ps[:, 6 + parity, 2 * j:2 * j + 2], rows[:, parity, j * P:(j + 1) * P],
                              C("pick"), start=True, stop=True)
                    last.then_inc(*((slot_free[off % SLOTS].sem, 1) if j == 0 else (cols_ready.sem, 1)))

            def down_tile(layer, f, half, i, dd, off, poff):
                for z in range(2):
                    w = piece_of(layer, poff + z, i * 8)
                    if z == 0:
                        pe.wait_ge(down_free.sem, layer * down_free.n + (i * 4 + (16 * f + 8 * half + dd + 1)))
                    n0, n1 = DOWN_CUT[z] // P, DOWN_CUT[z + 1] // P
                    for t in range(n0, n1):
                        if dd % 4 == 0:
                            pe.wait_ge(hid_ready.sem, hid_ready.at(layer, f * FT + half * HALF + t + 1))
                        last = mm3(ps[:, 4 + dd % 2, 0:TOK], both(w, ALLP, slice((t - n0) * P, (t - n0 + 1) * P)),
                                   both(hid, ALLP, t, ALLP), t == 0, t == HALF - 1)
                    last.then_inc(piece_used.sem, 1)

            def ffn(layer, f, hcount):
                for half in range(2):
                    name = f"up{f}{half}"
                    off, poff = AT[name], PA[name]

                    def pair(i, c):
                        if f == 0:
                            if half == 1:
                                pe.wait_ge(down_free.sem, down_free.at(layer, 8))
                            ada_rows(layer, off + 2 * c, i, c % 2)
                        up(layer, f, half, i, i * 2 + c, c % 2, poff + 2 * c,
                           hcount if c == 0 and half == 0 else None)
                        if f == 0:
                            ada_cols(layer, i * 2 + (ADA0 + half * HALF + c), c % 2, off + 2 * c)

                    with pe.Fori(0, HALF // 2) as i:
                        pair(i, 0)
                        pair(i, 1)
                    c = HALF - 1
                    if f == 0:
                        ada_rows(layer, off + 2 * c, 0, 0)
                    up(layer, f, half, 0, c, 0, poff + 2 * c, None)
                    if f == 0:
                        ada_cols(layer, ADA0 + half * HALF + c, 0, off + 2 * c)
                    off, poff = AT[f"down{f}{half}"], PA[f"down{f}{half}"]
                    if half == 0:
                        with pe.Fori(0, 2) as i:
                            for dd in range(4):
                                down_tile(layer, f, half, i, dd, off + dd, poff + 2 * dd)
                    else:
                        n = 1 + 2 * f
                        for dd in range(KT):
                            down_tile(layer, f, half, 0, dd, off + dd, poff + 2 * dd)
                            if dd:
                                sumsq(layer, n, dd - 1, sq[:, (dd - 1) % 2, :])
                        sumsq(layer, n, KT - 1, sq[:, (KT - 1) % 2, :])

            for t in range(KT):
                sumsq(0, 0, t, sq[:, t % 2, :])
            pe.wait_ge(cond_ready.sem, 1)
            with pe.Fori(0, DEPTH) as layer:
                with pe.Fori(0, ADA0 // SLOTS) as i:
                    pe.wait_ge(down_free.sem, down_free.at(layer, 0))
                    for pair_ in range(2):
                        for c in range(2):
                            ada_rows(layer, 2 * pair_ + c, i, c)
                        for c in range(2):
                            ada_cols(layer, i * SLOTS + (2 * pair_ + c), c, 2 * pair_ + c)
                for c in range(2):
                    ada_rows(layer, ADA0 // SLOTS * SLOTS + c, 0, c)
                for c in range(2):
                    ada_cols(layer, ADA0 // SLOTS * SLOTS + c, c, ADA0 // SLOTS * SLOTS + c)
                ffn(layer, 0, 0)

                for t in range(14):
                    w = piece_of(layer, PA["proj"] + t)
                    if t >= 4:
                        pe.wait_ge(proj_done.sem, proj_done.at(layer, t - 3))
                    tile8(layer, w, 0, KT, hA, ps[:, t % 4, 0:TOK], 8 if t == 0 else None
                          ).then_inc(piece_used.sem, 1)
                for z in range(2):
                    w = piece_of(layer, PA["kr"] + z)
                    for t in range(4):
                        last = mm3(ps[:, 4, 0:TOK], both(w, ALLP, slice(t * P, (t + 1) * P)),
                                   both(hA, ALLP, 4 * z + t, ALLP), z == 0 and t == 0, z == 1 and t == 3)
                    last.then_inc(piece_used.sem, 1)
                for q in range(4):
                    w = piece_of(layer, PA["v"] + q)
                    for j in range(3):
                        for z in range(2):
                            last = mm3(ps[:, 5 + j, :], both(hA, ALLP, 2 * q + z, slice(j * P, (j + 1) * P)),
                                       both(w, ALLP, slice(z * 512, (z + 1) * 512)),
                                       q == 0 and z == 0, q == 3 and z == 1)
                    last.then_inc(piece_used.sem, 1)
                pe.wait_ge(small_landed.sem, small_landed.at(layer, 16))

                pe.wait_ge(proj_done.sem, proj_done.at(layer, 14))
                for d in range(2):
                    for j in range(3):
                        last = mm(ps[:, 2 * d + j // 2, j % 2 * 256:j % 2 * 256 + 256], w1t[64 * d:64 * d + 64, j * P:(j + 1) * P],
                                  S("w2")[64 * d:64 * d + 64, :], start=True, stop=True)
                last.then_inc(wlog_ready.sem, 1)
                pe.wait_ge(v_done.sem, v_done.at(layer, 1))
                for d in range(2):
                    for p in range(2):
                        last = mm(ps[:, 4 + 2 * d + p, 0:TOK], S("a2")[64 * d:64 * d + 64, p * P:(p + 1) * P],
                                  a1[64 * d:64 * d + 64, :], start=True, stop=True)
                last.then_inc(a_ready.sem, 1)
                pe.wait_ge(wlog_biased.sem, wlog_biased.at(layer, 1))
                for j in range(3):
                    last = mm(ps[:, j // 2, j % 2 * 256:j % 2 * 256 + 256],
                              g1s[:, j * P:(j + 1) * P], S("g2"), start=True, stop=True)
                last.then_inc(g_ready.sem, 1)
                pe.wait_ge(kksq_ready.sem, kksq_ready.at(layer, 1))
                for p in range(2):
                    last = mm(ps[:, 2 + p, 0:TOK], block, kd[:, 0, p, :], start=True, stop=True)
                last.then_inc(kkss_ready.sem, 1)
                pe.wait_ge(prod_ready.sem, prod_ready.at(layer, 1))
                for j in range(3):
                    for p in range(2):
                        last = mm(ps[:, 2, 4 * j:4 * j + 4], prod[:, p, j * P:(j + 1) * P],
                                  C("heads", 4)[:, p, :], start=p == 0, stop=p == 1)
                last.then_inc(bonus_psum.sem, 1)

                pe.wait_ge(g_done.sem, g_done.at(layer, 1))
                pe.wait_ge(mla_sq.sem, mla_sq.at(layer, 1))
                for z in range(2):
                    mm(ps[:, 0, 0:TOK], ones, sq3[:, z, :], start=z == 0, stop=z == 1)
                mm(ps[:, 1, 0:TOK], ones, sq3[:, 2, :], start=True, stop=True).then_inc(mla_ss.sem, 1)
                pe.wait_ge(mla_normed.sem, mla_normed.at(layer, 1))
                pe.wait_ge(bonus_done.sem, bonus_done.at(layer, 1))
                for hd in range(HEADS):
                    for z in range(2):
                        last = mm(ps[:, hd, 0:TOK], S("uq")[:, (z * 4 + hd) * P:(z * 4 + hd + 1) * P],
                                  dq[:, z, :], start=z == 0, stop=z == 1)
                last.then_inc(q_psum.sem, 1)
                pe.wait_ge(a_done.sem, a_done.at(layer, 1))
                for hd in range(HEADS):
                    last = mm(ps[0:64, 4 + hd, :], S("ukv_k")[:, hd * 64:(hd + 1) * 64], ckvT,
                              start=True, stop=True)
                last.then_inc(kn_psum.sem, 1)
                pe.wait_ge(q_done.sem, q_done.at(layer, 1))
                for t in range(4):
                    last = mm(ps[:, t // 2, t % 2 * 256:t % 2 * 256 + 256], ckvT[:, t * P:(t + 1) * P],
                              S("ukv_v"), start=True, stop=True)
                last.then_inc(vm_psum.sem, 1)
                pe.wait_ge(kn_done.sem, kn_done.at(layer, 1))
                pe.wait_ge(vm_done.sem, vm_done.at(layer, 1))

                def scores(n):
                    br, hd, q = JOBS[n]
                    k0, k1 = (0, P) if q == 0 else (P, KEYS)
                    if n >= 3:
                        pe.wait_ge(exped.sem, exped.at(layer, n - 2))
                    if br == 0:
                        o, p = 64 * (hd % 2), hd // 2
                        ins = mm(ps[:, n % 3, 0:k1 - k0], qT[o:o + 64, p, q * P:(q + 1) * P],
                                 kT[o:o + 64, p, k0:k1], start=True, stop=True)
                    else:
                        ins = mm(ps[:, n % 3, 0:k1 - k0], qm[0:96, hd, q * P:(q + 1) * P],
                                 KTm[0:96, hd, k0:k1], start=True, stop=True)
                    ins.then_inc(scored.sem, 1)

                def turn(n):
                    _, _, q = JOBS[n]
                    pe.wait_ge(normed.sem, normed.at(layer, n + 1))
                    if n >= 2:
                        pe.wait_ge(pT_ready.sem, pT_ready.at(layer, n - 1))
                    for t in range(1 if q == 0 else 3):
                        last = nc.tensor.transpose(ps[:, 3 + n % 2, t * P:(t + 1) * P],
                                                   prob[:, n % 3, t * P:(t + 1) * P], ident)
                    last.then_inc(pT_psum.sem, 1)

                def weigh(n):
                    br, hd, q = JOBS[n]
                    o = 64 * (hd % 2)
                    pe.wait_ge(pT_ready.sem, pT_ready.at(layer, n + 1))
                    if n >= 2:
                        pe.wait_ge(o_done.sem, o_done.at(layer, n - 1))
                    tiles = (0,) if q == 0 else (1, 2, 3)
                    for i_, t in enumerate(tiles):
                        if br == 1:
                            v_ = Vm[:, t, hd * 64:(hd + 1) * 64]
                        elif t == 3:
                            v_ = S("na_v")[:, hd * 64:(hd + 1) * 64]
                        else:
                            v_ = V[:, t, hd * 64:(hd + 1) * 64]
                        last = mm(ps[o:o + 64, 5 + n % 2, 0:P], v_, probT[:, n % 2, i_ * P:(i_ + 1) * P],
                                  start=i_ == 0, stop=i_ == len(tiles) - 1)
                    last.then_inc(o_psum.sem, 1)

                for n in range(NJ + 3):
                    if n < NJ:
                        scores(n)
                    if 2 <= n <= NJ + 1:
                        turn(n - 2)
                    if n >= 3:
                        weigh(n - 3)

                pe.wait_ge(o_done.sem, o_done.at(layer, NJ))
                pe.wait_ge(bonus_done.sem, bonus_done.at(layer, 1))
                pe.wait_ge(sig_ready.sem, sig_ready.at(layer, 1))
                def running_sums(rd):
                    for d in range(2):
                        for p in range(2):
                            last = mm(ps[:, 4 + d, p * 256:(p + 1) * 256],
                                      sig[:, ROUNDS[rd][d], d * 256 + p * P:d * 256 + (p + 1) * P],
                                      C(f"cum{d}"), start=True, stop=True)
                    last.then_inc(cum_ready.sem, 1)

                running_sums(0)
                for rd, tiles in enumerate(ROUNDS):
                    pe.wait_ge(factors_ready.sem, factors_ready.at(layer, rd + 1))
                    for u, (d, p, hh) in enumerate(UNITS):
                        o = 64 * hh
                        if rd and u == 5:
                            pe.wait_ge(round_done.sem, round_done.at(layer, rd))
                        for z in range(2):
                            last = mm(ps[:, (u + 2) % 8, z * 256:(z + 1) * 256], KB[o:o + 64, d, p, z, :],
                                      KR[o:o + 64, d, p, :, :], start=True, stop=True)
                        last.then_inc(gram_psum.sem, 1)
                    for m in range(LEVELS):
                        for grp in range(2):
                            if m == 0:
                                pe.wait_ge(level0_masked.sem, level0_masked.at(layer, 2 * rd + grp + 1))
                            else:
                                pe.wait_ge(level_masked.sem, level_masked.at(layer, lev1(rd, m, grp)))
                                pe.wait_ge(t_ready.sem, t_ready.at(layer, lev(rd, m - 1, grp)))
                            for q in range(4):
                                u = 4 * grp + q
                                last = mm(ps[:, 2 + grp, q * P:(q + 1) * P], Nm[:, m % 2, u, :],
                                          T[:, u, :] if m else ident, start=True, stop=True)
                            last.then_inc(inv_psum.sem, 1)
                        if m == 0:
                            pe.wait_ge(gram_masked.sem, gram_masked.at(layer, 8 * rd + 8))
                            for d in range(2):
                                for z in range(2):
                                    for p in range(2):
                                        last = nc.tensor.transpose(
                                            ps[:, d, (2 * z + p) * P:(2 * z + p + 1) * P],
                                            KB[:, d, p, z, :], ident)
                            last.then_inc(kbt_psum.sem, 1)
                            continue
                        if m == 1:
                            pe.wait_ge(kbt_ready.sem, kbt_ready.at(layer, rd + 1))
                            pe.wait_ge(state_ready.sem, state_ready.at(layer, rd + 1))
                            for u, (d, p, hh) in enumerate(UNITS):
                                o, c0 = 64 * hh, (2 * d + p) * 64
                                mm(ps[:, hh, c0:c0 + 64], KR[o:o + 64, d, p, 0, :],
                                   s_in[o:o + 64, 2 * d + p, :], start=u < 2, stop=False)
                            for u, (d, p, hh) in enumerate(UNITS):
                                hd, c0 = 2 * p + hh, (2 * d + p) * 64
                                last = mm(ps[:, hh, c0:c0 + 64], G[:, u, 0, :],
                                          V[:, tiles[d], 256 + hd * 64:256 + hd * 64 + 64],
                                          start=False, stop=u >= 6)
                            last.then_inc(f_psum.sem, 1)
                        if m == 3:
                            pe.wait_ge(f_ready.sem, f_ready.at(layer, rd + 1))
                            for u, (d, p, hh) in enumerate(UNITS):
                                o, hd, c0 = 64 * hh, 2 * p + hh, (2 * d + p) * P
                                mm(ps[o:o + 64, hh, c0:c0 + P],
                                   V[:, tiles[d], 256 + hd * 64:256 + hd * 64 + 64], G[:, u, 1, :],
                                   start=u < 2, stop=False)
                            for u, (d, p, hh) in enumerate(UNITS):
                                o, c0 = 64 * hh, (2 * d + p) * P
                                mm(ps[o:o + 64, hh, c0:c0 + P], s_in[o:o + 64, 2 * d + p, :],
                                   KR[o:o + 64, d, p, 1, :], start=False, stop=False)
                        if m == LEVELS - 1 and rd < 2:
                            running_sums(rd + 1)
                        for grp in range(2):
                            pe.wait_ge(x_ready.sem, x_ready.at(layer, lev1(rd, m, grp)))
                            for q in range(4):
                                u = 4 * grp + q
                                if m < LEVELS - 1:
                                    mm(ps[:, 4 + grp, q * P:(q + 1) * P], Tt[:, u, :], X[:, u, :],
                                       start=True, stop=True)
                                last = mm(ps[:, 6 + grp, q * P:(q + 1) * P], X[:, u, :], Tt[:, u, :],
                                          start=True, stop=True)
                            last.then_inc(inv_psum.sem, 1)
                    for grp in range(2):
                        pe.wait_ge(t_ready.sem, t_ready.at(layer, lev(rd, LEVELS - 1, grp)))
                        for q in range(4):
                            u = 4 * grp + q
                            last = mm(ps[:, 2 + grp, q * 64:(q + 1) * 64], Tt[:, u, :], Fm[:, u, :],
                                      start=True, stop=True)
                        last.then_inc(u_psum.sem, 1)
                    if rd < 2:
                        for u, (d, p, hh) in enumerate(UNITS):
                            o, hd, c0 = 64 * hh, 2 * p + hh, (2 * d + p) * 64
                            mm(ps[o:o + 64, 7, c0:c0 + 64], KBt[:, d, p * P + o:p * P + o + 64],
                               V[:, tiles[d], 256 + hd * 64:256 + hd * 64 + 64], start=u < 2, stop=False)
                    for grp in range(2):
                        pe.wait_ge(u_ready.sem, u_ready.at(layer, 2 * rd + grp + 1))
                        for u in range(4 * grp, 4 * grp + 4):
                            d, p, hh = UNITS[u]
                            o, c0 = 64 * hh, (2 * d + p) * 64
                            if rd < 2:
                                mm(ps[o:o + 64, 7, c0:c0 + 64],
                                   KBt[:, d, 256 + p * P + o:256 + p * P + o + 64], Um[:, u, :],
                                   start=False, stop=u >= 6)
                            last = mm(ps[o:o + 64, hh, 2 * c0:2 * c0 + P], Um[:, u, :], G[:, u, 3, :],
                                      start=False, stop=u >= 6)
                    last.then_inc(y_psum.sem, 1)
                pe.wait_ge(round_done.sem, round_done.at(layer, 3))
                for j in range(3):
                    for p in range(2):
                        last = nc.tensor.transpose(
                            ps[:, 4 + j // 2, (j % 2 * 2 + p) * P:(j % 2 * 2 + p + 1) * P],
                            oT[2][:, p, j * P:(j + 1) * P], ident)
                last.then_inc(Y_psum.sem, 1)
                for q in range(6):
                    for n in range(4 * q, 4 * q + 4):
                        w = piece_of(layer, PA["gate0"] + n)
                        if n >= 4:
                            pe.wait_ge(proj_done.sem, proj_done.at(layer, 14 + n - 3))
                        tile8(layer, w, 0, KT, hB, ps[:, n % 4, 0:TOK], 16 if n == 0 else None
                              ).then_inc(piece_used.sem, 1)
                    if q == 0:
                        pe.wait_ge(rw_out.sem, rw_out.at(layer, 1))
                        for p in range(2):
                            for j in range(3):
                                last = nc.tensor.transpose(ps[:, 4 + p, j * P:(j + 1) * P],
                                                           Y[:, j, p * P:(p + 1) * P], ident)
                        last.then_inc(br_psum.sem, 1)
                        pe.wait_ge(rwT_ready.sem, rwT_ready.at(layer, 1))
                    w = block_of(layer, AT[f"branch{q}"])
                    for n in range(4 * q, 4 * q + 4):
                        if n >= 4:
                            pe.wait_ge(br_free.sem, br_free.at(layer, n - 3))
                        for z in range(2):
                            last = mm(ps[:, 4 + n % 4, 0:TOK], w[:, (n % 4 * 2 + z) * P:(n % 4 * 2 + z + 1) * P],
                                      oT[(0, 2, 1)[n % 3]][:, z, :], start=z == 0, stop=z == 1)
                        last.then_inc(br_psum.sem, 1)
                for n in range(8):
                    w = piece_of(layer, PA["out"] + n)
                    if n >= 4:
                        pe.wait_ge(out_free.sem, out_free.at(layer, n - 3))
                    for t in range(KT):
                        if n == 0:
                            pe.wait_ge(comb_ready.sem, comb_ready.at(layer, t + 1))
                        last = mm3(ps[:, n % 4, 0:TOK], both(w, ALLP, slice(t * P, (t + 1) * P)),
                                   both(hA, ALLP, t, ALLP), t == 0, t == KT - 1)
                    last.then_inc(piece_used.sem, 1)
                    if n:
                        sumsq(layer, 2, n - 1, sq[:, (n - 1) % 2, :])
                sumsq(layer, 2, KT - 1, sq[:, (KT - 1) % 2, :])
                ffn(layer, 1, 24)

        @blk.scalar
        def _(act):
            A = nc.scalar.activation
            act.wait_ge(const_landed.sem, 16)
            A(C("cond"), C("cond"), ACT.Silu).then_inc(cond_ready.sem, 1)

            def squares(layer, n, wait=None, base=0):
                for t in range(KT):
                    if wait is not None:
                        act.wait_ge(wait.sem, wait.at(layer, base + t + 1))
                    if wait is not None or t >= 2:
                        act.wait_ge(ss_step.sem, ss_step.at(layer, 8 * n + t - 1) if n else t - 1)
                    A(sq[:, t % 2, :], x[:, t, :], ACT.Square).then_inc(sq_ready.sem, 1)
                act.wait_ge(ss_step.sem, ss_step.at(layer, 8 * n + 8))
                A(root, ps[:, 6, 0:TOK], ACT.Sqrt, bias=eps6, scale=1.0 / D).then_inc(root_ready.sem, 1)

            def shift(layer, n, count, dst):
                for t in range(KT):
                    act.wait_ge(h_scaled.sem, h_scaled.at(layer, count + t + 1))
                    for c, s0, s1 in SEGS:
                        last = A(dst[0][:, t, s0:s1], htmp[:, t % 3, s0:s1], ACT.Identity,
                                 bias=modv[:, 3 * n, t, c:c + 1])
                    last.then_inc(h_hi.sem, 1)

            cursor = [0]

            def split_through(layer, n):
                while cursor[0] <= n:
                    m = cursor[0]
                    blk_, c0, c1 = PIECES[m]
                    slot = blk_ % SLOTS
                    act.wait_ge(landed[slot].sem, landed[slot].at(layer, 16 * (blk_ // SLOTS + 1)))
                    act.wait_ge(piece_used.sem, piece_used.at(layer, m - 1))
                    A(w_hi[:, m % 2, 0:c1 - c0], ring[:, slot, c0:c1], ACT.Copy).then_inc(hi_ready.sem, 1)
                    cursor[0] += 1

            def ada_rows(layer, chunk, parity):
                act.wait_ge(ada_psum.sem, layer * ADA + (chunk + 1))
                A(rows[:, parity, :], ps[:, 4 + parity, 0:256], ACT.Copy).then_inc(rows_ready.sem, 1)

            def ffn(layer, f):
                for half in range(2):
                    p0 = PA[f"up{f}{half}"]
                    for t in range(HALF):
                        if f == 0:
                            ada_rows(layer, ADA0 + half * HALF + t, t % 2)
                        split_through(layer, p0 + 2 * t + 3)
                        act.wait_ge(piece_used.sem, piece_used.at(layer, p0 + 2 * t + 2))
                        A(silu[:, t % 2, :], ps[:, t % 2 * 2, 0:TOK], ACT.Silu).then_inc(silu_ready.sem, 1)
                        act.wait_ge(up_free.sem, up_free.at(layer, f * FT + half * HALF + t + 1))
                        A(hid[0][:, t, :], product[:, t % 2, :], ACT.Copy).then_inc(hid_hi.sem, 1)
                    p0 = PA[f"down{f}{half}"]
                    for t in range(KT):
                        split_through(layer, min(p0 + 2 * t + 3, NPIECE - 1))
                        if half == 1:
                            n = 1 + 2 * f
                            act.wait_ge(down_free.sem, down_free.at(layer, 16 * f + 8 + t + 1))
                            act.wait_ge(ss_step.sem, ss_step.at(layer, 8 * n + t - 1))
                            A(sq[:, t % 2, :], x[:, t, :], ACT.Square).then_inc(sq_ready.sem, 1)
                n = 1 + 2 * f
                act.wait_ge(ss_step.sem, ss_step.at(layer, 8 * n + 8))
                A(root, ps[:, 6, 0:TOK], ACT.Sqrt, bias=eps6, scale=1.0 / D).then_inc(root_ready.sem, 1)

            act.wait_ge(x_landed.sem, 16)
            squares(0, 0)
            with act.Fori(0, DEPTH) as layer:
                with act.Fori(0, ADA0 // SLOTS) as i:
                    for c in range(4):
                        ada_rows(layer, i * SLOTS + c, c % 2)
                for c in range(2):
                    ada_rows(layer, ADA0 // SLOTS * SLOTS + c, c)
                split_through(layer, 1)
                shift(layer, 0, 0, hA)
                ffn(layer, 0)
                shift(layer, 1, 8, hA)

                dest = ([qT[:, z, :] for z in range(2)] + [kT[:, z, 0:TOK] for z in range(2)]
                        + [r[:, z, :] for z in range(2)] + [k[:, z, :] for z in range(2)]
                        + [w1t, a1, g1s] + [dq[:, z, :] for z in range(2)] + [ckvT[:, 0:TOK]])
                for t in range(14):
                    split_through(layer, PA["proj"] + t + 2)
                    act.wait_ge(piece_used.sem, piece_used.at(layer, PA["proj"] + t + 1))
                    A(dest[t], ps[:, t % 4, 0:TOK], {8: ACT.Tanh, 10: ACT.Sigmoid}.get(t, ACT.Copy),
                      scale=HD ** -0.5 if t < 2 else 1.0).then_inc(proj_done.sem, 1)
                split_through(layer, PA["gate0"] + 1)
                act.wait_ge(wlog_biased.sem, wlog_biased.at(layer, 1))
                A(sig[:, :, :], sig[:, :, :], ACT.Sigmoid).then_inc(sig_ready.sem, 1)
                act.wait_ge(a_ready.sem, a_ready.at(layer, 1))
                for d in range(2):
                    for p in range(2):
                        last = A(b[:, d, p, :], ps[:, 4 + 2 * d + p, 0:TOK], ACT.Sigmoid,
                                 bias=S("a0")[:, 2 * d + p:2 * d + p + 1])
                last.then_inc(a_done.sem, 1)
                act.wait_ge(g_ready.sem, g_ready.at(layer, 1))
                A(g[:, 0:2, :].rearrange("p a b -> p (a b)"), ps[:, 0, :], ACT.Copy)
                A(g[:, 2, :], ps[:, 1, 0:256], ACT.Copy).then_inc(g_done.sem, 1)
                act.wait_ge(kkmax_ready.sem, kkmax_ready.at(layer, 1))
                A(root2, root2, ACT.Sqrt).then_inc(kkroot_ready.sem, 1)
                act.wait_ge(mla_ss.sem, mla_ss.at(layer, 1))
                act.wait_ge(bonus_psum.sem, bonus_psum.at(layer, 1))
                A(prod[:, 0, :], ps[:, 0, 0:TOK], ACT.Sqrt, bias=eps6, scale=1.0 / 256)
                A(prod[:, 1, :], ps[:, 1, 0:TOK], ACT.Sqrt, bias=eps6, scale=1.0 / P).then_inc(mla_root.sem, 1)
                act.wait_ge(kn_psum.sem, kn_psum.at(layer, 1))
                A(KTm[0:64, :, :], ps[0:64, 4:8, :], ACT.Copy).then_inc(kn_done.sem, 1)
                act.wait_ge(vm_psum.sem, vm_psum.at(layer, 1))
                A(Vm[:, :, :].rearrange("p a b -> p (a b)"), ps[:, 0:2, :].rearrange("p a b -> p (a b)"),
                  ACT.Copy).then_inc(vm_done.sem, 1)
                act.wait_ge(mla_normed.sem, mla_normed.at(layer, 1))
                row = act.snap(layer + 0)
                act.dma_start(k_d[bass.ds(row, 1)].rearrange("a p t n -> (a p) t n"), kT[:, :, 0:SEQ]
                              ).then_inc(kv_stored.sem, 16)
                act.dma_start(v_d[bass.ds(row, 1)].rearrange("a p n -> (a p) n"), V[:, 0, 0:256]
                              ).then_inc(kv_stored.sem, 16)
                act.dma_start(ckv_d[bass.ds(row, 1)].rearrange("a p n -> (a p) n"), ckvT[:, 0:SEQ]
                              ).then_inc(kv_stored.sem, 16)
                act.dma_start(kr_d[bass.ds(row, 1)].rearrange("a p n -> (a p) n"), kr_raw[64:96, :]
                              ).then_inc(kv_stored.sem, 16)

                def exp(n):
                    br, hd, q = JOBS[n]
                    act.wait_ge(maxed.sem, maxed.at(layer, n + 1))
                    if n >= 3:
                        act.wait_ge(pT_psum.sem, pT_psum.at(layer, n - 2))
                    width = P if q == 0 else TOK
                    A(prob[:, n % 3, 0:width], ps[:, n % 3, 0:width], ACT.Exp, bias=stat[:, 2 + n % 3:3 + n % 3],
                      accum_out=stat[:, 5 + n % 3:6 + n % 3]).then_inc(exped.sem, 1)

                def copyT(n):
                    _, _, q = JOBS[n]
                    width = P if q == 0 else TOK
                    act.wait_ge(pT_psum.sem, pT_psum.at(layer, n + 1))
                    if n >= 2:
                        act.wait_ge(o_psum.sem, o_psum.at(layer, n - 1))
                    A(probT[:, n % 2, 0:width], ps[:, 3 + n % 2, 0:width], ACT.Copy).then_inc(pT_ready.sem, 1)

                for n in range(NJ + 2):
                    if n < NJ:
                        exp(n)
                    if n >= 2:
                        copyT(n - 2)

                act.wait_ge(kv_stored.sem, kv_stored.at(layer, 64))

                def decays(rd):
                    act.wait_ge(cum_ready.sem, cum_ready.at(layer, rd + 1))
                    for d in range(2):
                        cs = ps[:, 4 + d, :].rearrange("p (a b c) -> p a b c", a=2, b=2)
                        A(E1[:, d].rearrange("p a b c -> p (a b c)"), ps[:, 4 + d, :], ACT.Exp, scale=-DECAY)
                        A(E2[:, d], cs[:, :, 0, :], ACT.Exp, scale=DECAY)
                        first = 0 if d == 0 else P - 1
                        last = A(pmid[:, 2 * d:2 * d + 2], cs[:, :, 1, first], ACT.Exp, scale=DECAY)
                    last.then_inc(exps_ready.sem, 1)

                decays(0)
                for rd in range(3):
                    act.wait_ge(kbt_psum.sem, kbt_psum.at(layer, rd + 1))
                    for d in range(2):
                        A(KBt[:, d, 0:256], ps[:, d, 0:256], ACT.Copy)
                        last = A(KBt[:, d, 256:512], ps[:, d, 256:512], ACT.Copy, scale=-1.0)
                    last.then_inc(kbt_ready.sem, 1)
                    for m in range(1, LEVELS):
                        for grp in range(2):
                            act.wait_ge(inv_psum.sem, inv_psum.at(layer, inv_x(rd, m, grp)))
                            A(X[:, 4 * grp:4 * grp + 4, :], ps[:, 2 + grp, :].rearrange("p (a b) -> p a b", b=P),
                              ACT.Copy).then_inc(x_ready.sem, 1)
                    if rd < 2:
                        decays(rd + 1)
                    if rd == 0:
                        act.wait_ge(round_done.sem, round_done.at(layer, 1))
                        act.dma_start(s_d[bass.ds(row, 1)].rearrange("a p t n -> (a p) t n"), s_out[:, :, :]
                                      ).then_inc(s_stored.sem, 16)
                act.wait_ge(s_stored.sem, s_stored.at(layer, 16))
                act.wait_ge(Y_psum.sem, Y_psum.at(layer, 1))
                A(Y[:, 0:2, :].rearrange("p a b -> p (a b)"), ps[:, 4, :], ACT.Copy)
                A(Y[:, 2, :], ps[:, 5, 0:256], ACT.Copy).then_inc(Y_ready.sem, 1)
                shift(layer, 1, 16, hB)
                for n in range(24):
                    split_through(layer, PA["gate0"] + n + 2)
                    act.wait_ge(piece_used.sem, piece_used.at(layer, PA["gate0"] + n + 1))
                    if n >= 4:
                        act.wait_ge(br_free.sem, br_free.at(layer, n - 3))
                    A(gsig[:, n % 4, :], ps[:, n % 4, 0:TOK], ACT.Sigmoid).then_inc(proj_done.sem, 1)
                    if n == 1:
                        act.wait_ge(gn_var.sem, gn_var.at(layer, 1))
                        A(stat2[:, 0:12], stat[:, 12:24], ACT.Sqrt, bias=epsgn, scale=1.0 / HD
                          ).then_inc(gn_root.sem, 1)
                    if n == 3:
                        act.wait_ge(br_psum.sem, br_psum.at(layer, 1))
                        A(oT[2][:, :, :], ps[:, 4:6, 0:TOK], ACT.Copy).then_inc(rwT_ready.sem, 1)
                    if n % 4 == 3:
                        for t in range(KT):
                            if (3 * t + 2) // 4 == n // 4:
                                act.wait_ge(comb_sum.sem, comb_sum.at(layer, t + 1))
                                A(hA[0][:, t, :], comb[:, t % 2, :], ACT.Copy).then_inc(comb_hi.sem, 1)
                for t in range(KT):
                    split_through(layer, PA["out"] + t + 2)
                    act.wait_ge(out_free.sem, out_free.at(layer, t + 1))
                    act.wait_ge(ss_step.sem, ss_step.at(layer, 16 + t - 1))
                    A(sq[:, t % 2, :], x[:, t, :], ACT.Square).then_inc(sq_ready.sem, 1)
                act.wait_ge(ss_step.sem, ss_step.at(layer, 24))
                A(root, ps[:, 6, 0:TOK], ACT.Sqrt, bias=eps6, scale=1.0 / D).then_inc(root_ready.sem, 1)
                shift(layer, 2, 24, hA)
                ffn(layer, 1)
                cursor[0] = 0

        @blk.vector
        def _(dve):
            v = nc.vector
            dve.sem_inc(up_free.sem, up_free.credit)
            dve.sem_inc(down_free.sem, down_free.credit)
            dve.sem_inc(mod_done.sem, mod_done.credit)
            dve.sem_inc(out_free.sem, out_free.credit)
            dve.wait_ge(const_landed.sem, 16)
            dve.wait_ge(x_landed.sem, 16)

            def inverse_root(layer, n):
                dve.wait_ge(root_ready.sem, root_ready.at(layer, n + 1))
                v.reciprocal(rinv[:, :], root)
                dve.drain()

            def normalise(layer, n, count, dst):
                for t in range(KT + 1):
                    if t < KT:
                        for c, s0, s1 in SEGS:
                            last = v.scalar_tensor_tensor(out=htmp[:, t % 3, s0:s1], in0=x[:, t, s0:s1],
                                                          scalar=scale_c[:, n, t, c:c + 1], in1=rinv[:, s0:s1],
                                                          op0=ALU.mult, op1=ALU.mult)
                        last.then_inc(h_scaled.sem, 1)
                    if t:
                        dve.wait_ge(h_hi.sem, h_hi.at(layer, count + t))
                        for c, s0, s1 in SEGS:
                            last = v.scalar_tensor_tensor(
                                out=dst[1][:, t - 1, s0:s1], in0=htmp[:, (t - 1) % 3, s0:s1],
                                scalar=modv[:, 3 * n, t - 1, c:c + 1], in1=dst[0][:, t - 1, s0:s1],
                                op0=ALU.add, op1=ALU.subtract)
                        last.then_inc(h_ready.sem, 1)
                        dve.drain()

            cursor = [0]

            def split_through(layer, n):
                while cursor[0] <= n:
                    m = cursor[0]
                    blk_, c0, c1 = PIECES[m]
                    slot = blk_ % SLOTS
                    dve.wait_ge(hi_ready.sem, hi_ready.at(layer, m + 1))
                    v.tensor_tensor(w_lo[:, m % 2, 0:c1 - c0], ring[:, slot, c0:c1],
                                    w_hi[:, m % 2, 0:c1 - c0], ALU.subtract).then_inc(split_ready.sem, 1)
                    if c0:
                        dve.drain().then_inc(slot_free[slot].sem, 1)
                    cursor[0] += 1

            def ada_cols(layer, chunk, parity):
                dve.wait_ge(cols_ready.sem, layer * ADA + (chunk + 1))
                cols = slice(chunk * 4, chunk * 4 + 4) if isinstance(chunk, int) else bass.ds(chunk * 4, 4)
                v.tensor_tensor(mod[:, cols], ps[:, 6 + parity, 0:4],
                                ada_b[:, cols], ALU.add
                                ).then_inc(mod_done.sem, 1)

            def coefficients(layer, n):
                v.scalar_tensor_tensor(out=scale_c[:, n].rearrange("p t c -> p (t c)"),
                                       in0=modv[:, 3 * n + 1].rearrange("p t c -> p (t c)"), scalar=1.0,
                                       in1=C("norm_g")[:, bass.ds(layer * 48 + 16 * n, 16)],
                                       op0=ALU.add, op1=ALU.mult)
                if n != 1:
                    v.tensor_scalar(gate_c[:, n // 2], modv[:, 3 * n + 2], 0.5, None, ALU.mult)

            def ffn(layer, f):
                for half in range(2):
                    p0 = PA[f"up{f}{half}"]
                    for t in range(HALF):
                        n = f * FT + half * HALF + t
                        split_through(layer, p0 + 2 * t + 3)
                        dve.wait_ge(silu_ready.sem, silu_ready.at(layer, n + 1))
                        v.tensor_tensor(product[:, t % 2, :], silu[:, t % 2, :],
                                        ps[:, t % 2 * 2 + 1, 0:TOK], ALU.mult).then_inc(up_free.sem, 1)
                        if f == 0:
                            ada_cols(layer, ADA0 + half * HALF + t, t % 2)
                        dve.wait_ge(hid_hi.sem, hid_hi.at(layer, n + 1))
                        v.tensor_tensor(hid[1][:, t, :], product[:, t % 2, :], hid[0][:, t, :], ALU.subtract
                                        ).then_inc(hid_ready.sem, 1)
                    if f == 0 and half == 1:
                        dve.drain()
                        coefficients(layer, 1)
                        coefficients(layer, 2)
                    p0 = PA[f"down{f}{half}"]
                    for t in range(KT):
                        split_through(layer, min(p0 + 2 * t + 3, NPIECE - 1))
                        dve.wait_ge(piece_used.sem, piece_used.at(layer, p0 + 2 * t + 2))
                        for c, s0, s1 in SEGS:
                            last = v.scalar_tensor_tensor(out=x[:, t, s0:s1], in0=ps[:, 4 + t % 2, s0:s1],
                                                          scalar=gate_c[:, f, t, c:c + 1], in1=x[:, t, s0:s1],
                                                          op0=ALU.mult, op1=ALU.add)
                        last.then_inc(down_free.sem, 1)

            with dve.Fori(0, DEPTH) as layer:
                v.tensor_copy(ada_b[:, :], C("ada_b")[:, bass.ds(layer * 144, 144)])
                dve.drain()
                with dve.Fori(0, ADA0 // SLOTS) as i:
                    for c in range(SLOTS):
                        ada_cols(layer, i * SLOTS + c, c % 2)
                for c in range(2):
                    ada_cols(layer, ADA0 // SLOTS * SLOTS + c, c)
                split_through(layer, 1)
                dve.drain()
                coefficients(layer, 0)
                dve.drain()
                inverse_root(layer, 0)
                normalise(layer, 0, 0, hA)
                ffn(layer, 0)
                dve.drain()
                inverse_root(layer, 1)
                normalise(layer, 1, 8, hA)
                split_through(layer, PA["v"] + 3)

                dve.wait_ge(piece_used.sem, piece_used.at(layer, PA["kr"] + 2))
                v.tensor_copy(kr_raw[64:96, :], ps[64:96, 4, 0:SEQ])
                v.tensor_tensor(kpe[64:96, :], ps[64:96, 4, 0:TOK], C("rope")[64:96, :], ALU.mult)
                v.tensor_tensor(ropes[64:96, 0, :], ps[96:128, 4, 0:TOK], C("rope")[96:128, :], ALU.mult)
                dve.wait_ge(proj_done.sem, proj_done.at(layer, 14))
                v.tensor_tensor(sq3[:, 0:2, :], dq, dq, ALU.mult)
                v.tensor_tensor(sq3[:, 2, :], ckvT[:, 0:TOK], ckvT[:, 0:TOK], ALU.mult).then_inc(mla_sq.sem, 1)
                dve.drain()
                v.tensor_tensor(kpe[64:96, :], kpe[64:96, :], ropes[64:96, 0, :], ALU.add)
                dve.drain()
                dve.wait_ge(small_landed.sem, small_landed.at(layer, 16))
                for hd in range(HEADS):
                    v.tensor_copy(KTm[64:96, hd, 0:TOK], kpe[64:96, :])
                    v.tensor_copy(KTm[64:96, hd, TOK:KEYS], S("krope")[64:96, :])
                for z in range(2):
                    v.tensor_copy(kT[:, z, TOK:KEYS], S("na_k", P)[:, z, :])
                v.tensor_copy(ckvT[:, TOK:KEYS], S("ckv"))
                dve.wait_ge(piece_used.sem, piece_used.at(layer, PA["v"] + 4))
                for j in range(3):
                    last = v.tensor_copy(V[:, j, :], ps[:, 5 + j, :])
                last.then_inc(v_done.sem, 1)
                for p in range(2):
                    v.tensor_scalar(kk[:, p, :], k[:, p, :], S("kk")[:, p:p + 1], None, ALU.mult)
                dve.drain()
                v.tensor_tensor(kd[:, 0, :, :], kk[:, :, :], kk[:, :, :], ALU.mult).then_inc(kksq_ready.sem, 1)
                split_through(layer, PA["gate0"] + 1)
                dve.wait_ge(wlog_ready.sem, wlog_ready.at(layer, 1))
                for j in range(3):
                    for d in range(2):
                        last = v.tensor_tensor(sig[:, j, d * 256:(d + 1) * 256],
                                               ps[:, 2 * d + j // 2, j % 2 * 256:j % 2 * 256 + 256],
                                               S("w0")[:, d * 256:(d + 1) * 256], ALU.add)
                last.then_inc(wlog_biased.sem, 1)
                dve.wait_ge(kkss_ready.sem, kkss_ready.at(layer, 1))
                v.tensor_scalar(root2, ps[:, 2:4, 0:TOK], 1e-24, None, ALU.max).then_inc(kkmax_ready.sem, 1)
                dve.wait_ge(kkroot_ready.sem, kkroot_ready.at(layer, 1))
                v.reciprocal(root2, root2)
                v.tensor_scalar(stat[:, 0:2], S("ka"), -1.0, 1.0, ALU.mult, ALU.add)
                dve.drain()
                v.tensor_tensor(kk[:, :, :], kk[:, :, :], root2, ALU.mult)
                dve.wait_ge(a_done.sem, a_done.at(layer, 1))
                for d in range(2):
                    for p in range(2):
                        v.tensor_scalar(kd[:, d, p, :], b[:, d, p, :], S("ka")[:, p:p + 1], stat[:, p:p + 1],
                                        ALU.mult, ALU.add)
                dve.drain()
                for d in range(2):
                    v.tensor_tensor(kd[:, d], kd[:, d], k[:, :, :], ALU.mult)
                    v.tensor_tensor(b[:, d], b[:, d], kk[:, :, :], ALU.mult)
                dve.drain()
                v.tensor_tensor(prod, kd[:, 0], kd[:, 1], ALU.add)
                dve.drain()
                for p in range(2):
                    last = v.scalar_tensor_tensor(out=prod[:, p, :], in0=prod[:, p, :],
                                                  scalar=S("rk")[:, p:p + 1], in1=r[:, p, :],
                                                  op0=ALU.mult, op1=ALU.mult)
                last.then_inc(prod_ready.sem, 1)
                dve.wait_ge(bonus_psum.sem, bonus_psum.at(layer, 1))
                v.tensor_copy(bonus[:, :], ps[:, 2, 0:12]).then_inc(bonus_done.sem, 1)
                dve.wait_ge(mla_root.sem, mla_root.at(layer, 1))
                v.reciprocal(prod, prod)
                dve.drain()
                for z in range(2):
                    v.scalar_tensor_tensor(out=dq[:, z, :], in0=dq[:, z, :], scalar=S("qn")[:, z:z + 1],
                                           in1=prod[:, 0, :], op0=ALU.mult, op1=ALU.mult)
                v.scalar_tensor_tensor(out=ckvT[:, 0:TOK], in0=ckvT[:, 0:TOK], scalar=S("kvn"),
                                       in1=prod[:, 1, :], op0=ALU.mult, op1=ALU.mult
                                       ).then_inc(mla_normed.sem, 1)
                dve.wait_ge(q_psum.sem, q_psum.at(layer, 1))
                q_scale = (NOPE + ROPE) ** -0.5
                v.tensor_scalar(qm[0:64, :, :], ps[0:64, 0:4, 0:TOK], q_scale, None, ALU.mult)
                for hd in range(HEADS):
                    for dst, at in ((qm, 64), (ropes, 96)):
                        v.scalar_tensor_tensor(out=dst[64:96, hd, :], in0=ps[at:at + 32, hd, 0:TOK],
                                               scalar=q_scale, in1=C("rope")[at:at + 32, :],
                                               op0=ALU.mult, op1=ALU.mult)
                dve.drain()
                v.tensor_tensor(qm[64:96, :, :], qm[64:96, :, :], ropes[64:96, :, :], ALU.add
                                ).then_inc(q_done.sem, 1)

                def top(n):
                    br, hd, q = JOBS[n]
                    dve.wait_ge(scored.sem, scored.at(layer, n + 1))
                    src = ps[:, n % 3, 0:P if q == 0 else TOK]
                    if br == 0 and q > 0:
                        if n == 1:
                            dve.wait_ge(bias_ready.sem, bias_ready.at(layer, 1))
                        v.tensor_tensor(src, src, S("bias", TOK)[:, (q - 1) * 4 + hd, :], ALU.add)
                        dve.drain()
                    v.tensor_reduce(stat[:, 2 + n % 3:3 + n % 3], src, AX, ALU.max, negate=True
                                    ).then_inc(maxed.sem, 1)

                def share(n):
                    width = P if JOBS[n][2] == 0 else TOK
                    dve.wait_ge(exped.sem, exped.at(layer, n + 1))
                    v.reciprocal(stat[:, 8 + n % 2:9 + n % 2], stat[:, 5 + n % 3:6 + n % 3])
                    dve.drain()
                    v.tensor_scalar(prob[:, n % 3, 0:width], prob[:, n % 3, 0:width],
                                    stat[:, 8 + n % 2:9 + n % 2], None, ALU.mult).then_inc(normed.sem, 1)

                def keep(n):
                    br, hd, q = JOBS[n]
                    o = 64 * (hd % 2)
                    dve.wait_ge(o_psum.sem, o_psum.at(layer, n + 1))
                    v.tensor_copy(oT[br][o:o + 64, hd // 2, q * P:(q + 1) * P], ps[o:o + 64, 5 + n % 2, 0:P]
                                  ).then_inc(o_done.sem, 1)

                for n in range(NJ + 3):
                    if n < NJ:
                        top(n)
                    if 1 <= n <= NJ:
                        share(n - 1)
                    if n >= 3:
                        keep(n - 3)

                def factors(rd):
                    dve.wait_ge(exps_ready.sem, exps_ready.at(layer, rd + 1))
                    for d in range(2):
                        c0, c1 = ROUNDS[rd][d] * P, (ROUNDS[rd][d] + 1) * P
                        at_end = P - 1 if d == 0 else 0
                        v.tensor_tensor(KR[:, d, :, 0, :], kk[:, :, c0:c1], E1[:, d, :, 1, :], ALU.mult)
                        v.tensor_tensor(KR[:, d, :, 1, :], r[:, :, c0:c1], E1[:, d, :, 0, :], ALU.mult)
                        v.tensor_copy(pend[:, rd % 2, d, :], E1[:, d, :, 0, at_end])
                        v.tensor_tensor(KB[:, d, :, 0, :], kd[:, d, :, c0:c1], E2[:, d], ALU.mult)
                        last = v.tensor_tensor(KB[:, d, :, 1, :], b[:, d, :, c0:c1], E2[:, d], ALU.mult)
                    last.then_inc(factors_ready.sem, 1)

                factors(0)
                v.memset(s_in[:, :, :], 0.0).then_inc(state_ready.sem, 1)
                for rd, tiles in enumerate(ROUNDS):
                    for u, (d, p, hh) in enumerate(UNITS):
                        dve.wait_ge(gram_psum.sem, gram_psum.at(layer, 8 * rd + u + 1))
                        v.tensor_tensor(G[:, u].rearrange("p a b -> p (a b)"), ps[:, (u + 2) % 8, :],
                                        C(f"gram{d}"), ALU.mult).then_inc(gram_masked.sem, 1)
                        if u % 4 == 3:
                            dve.drain()
                            v.tensor_tensor(Nm[:, 0, u - 3:u + 1, :], G[:, u - 3:u + 1, 2, :],
                                            bcast(C(f"level{d}", P)[:, 0, :], 4), ALU.mult
                                            ).then_inc(level0_masked.sem, 1)
                    for m in range(LEVELS):
                        for grp in range(2):
                            sl = slice(4 * grp, 4 * grp + 4)
                            pv = lambda bank: ps[:, bank, :].rearrange("p (a b) -> p a b", b=P)
                            if m == 0:
                                eye = bcast(ident, 4)
                                dve.wait_ge(inv_psum.sem, inv_psum.at(layer, inv_x(rd, m, grp)))
                                v.tensor_tensor(T[:, sl, :], pv(2 + grp), eye, ALU.add)
                                v.tensor_tensor(Tt[:, sl, :], Nm[:, 0, sl, :], eye, ALU.add
                                                ).then_inc(t_ready.sem, 1)
                                continue
                            dve.wait_ge(inv_psum.sem, inv_psum.at(layer, inv_tt(rd, m, grp)))
                            if m < LEVELS - 1:
                                v.tensor_tensor(T[:, sl, :], T[:, sl, :], pv(4 + grp), ALU.add)
                            v.tensor_tensor(Tt[:, sl, :], Tt[:, sl, :], pv(6 + grp), ALU.add
                                            ).then_inc(t_ready.sem, 1)
                        if m == 0:
                            dve.drain()
                        if m == 1:
                            dve.wait_ge(f_psum.sem, f_psum.at(layer, rd + 1))
                            for hh in range(2):
                                last = v.tensor_copy(Fm[:, hh::2, :],
                                                     ps[:, hh, 0:256].rearrange("p (a b) -> p a b", b=HD))
                            last.then_inc(f_ready.sem, 1)
                    for grp in range(2):
                        dve.wait_ge(u_psum.sem, u_psum.at(layer, 2 * rd + grp + 1))
                        v.tensor_copy(Um[:, 4 * grp:4 * grp + 4, :].rearrange("p a b -> p (a b)"),
                                      ps[:, 2 + grp, 0:256]).then_inc(u_ready.sem, 1)
                    if rd < 2:
                        factors(rd + 1)
                    dve.drain()
                    dve.wait_ge(y_psum.sem, y_psum.at(layer, rd + 1))
                    if rd < 2:
                        s_new = (s_out, s_mid)[rd]
                        v.tensor_tensor(s_new[:, :, :].rearrange("p a b -> p (a b)"), ps[:, 7, 0:256],
                                        s_in[:, :, :].rearrange("p a b -> p (a b)"), ALU.add)
                    for d in range(2):
                        if d == 1 or rd < 2:
                            dve.drain()
                        for hh in range(2):
                            o = 64 * hh
                            src = ps[o:o + 64, hh, 2 * d * P:2 * (d + 1) * P].rearrange("p (a b) -> p a b", b=P)
                            dst = oT[2][o:o + 64, :, tiles[d] * P:(tiles[d] + 1) * P]
                            if rd == 2 or (rd == 0 and d == 1):
                                v.tensor_tensor(dst, dst, src, ALU.add)
                            else:
                                v.tensor_copy(dst, src)
                    if rd < 2:
                        for z in range(4):
                            last = v.tensor_scalar(s_new[:, z, :], s_new[:, z, :],
                                                   pend[:, rd, z // 2, z % 2:z % 2 + 1], None, ALU.mult)
                        last.then_inc(round_done.sem, 1)
                        dve.drain()
                        for z in range(4):
                            src = S("state", HD)[:, z, :] if rd == 0 else s_mid[:, z, :]
                            last = v.tensor_scalar(s_in[:, z, :], src, pmid[:, z:z + 1], None, ALU.mult)
                        last.then_inc(state_ready.sem, 1)
                    else:
                        dve.drain().then_inc(round_done.sem, 1)

                normalise(layer, 1, 16, hB)
                split_through(layer, PA["gate0"] + 2)
                Yh = Y[:, :, :].rearrange("p a (h c) -> p (a h) c", c=HD)
                sqY, bv = view(tmp, 0, 12, HD), view(tmp, 768, 3, 256)
                dve.wait_ge(Y_ready.sem, Y_ready.at(layer, 1))
                v.tensor_reduce(stat[:, 12:24], Yh, AX, ALU.add)
                dve.drain()
                v.tensor_scalar(stat[:, 12:24], stat[:, 12:24], 1.0 / HD, None, ALU.mult)
                dve.drain()
                v.tensor_tensor(Yh, Yh, spread(stat[:, 12:24], HD), ALU.subtract)
                dve.drain()
                v.tensor_tensor(sqY, Yh, Yh, ALU.mult)
                dve.drain()
                v.tensor_reduce(stat[:, 12:24], sqY, AX, ALU.add).then_inc(gn_var.sem, 1)
                for j in range(3):
                    v.tensor_tensor(bv[:, j, :].rearrange("p (h c) -> p h c", c=HD),
                                    V[:, j, 256:512].rearrange("p (h c) -> p h c", c=HD),
                                    spread(bonus[:, 4 * j:4 * j + 4], HD), ALU.mult)
                split_through(layer, PA["gate0"] + 3)
                dve.wait_ge(gn_root.sem, gn_root.at(layer, 1))
                v.reciprocal(stat2[:, 12:24], stat2[:, 0:12])
                dve.drain()
                v.tensor_tensor(Yh, Yh, spread(stat2[:, 12:24], HD), ALU.mult)
                dve.drain()
                v.tensor_tensor(Y[:, :, :], Y[:, :, :], bcast(S("gnw"), 3), ALU.mult)
                dve.drain()
                split_through(layer, PA["gate0"] + 4)
                v.tensor_tensor(Y[:, :, :], Y[:, :, :], bcast(S("gnb"), 3), ALU.add)
                dve.drain()
                v.tensor_tensor(Y[:, :, :], Y[:, :, :], bv, ALU.add)
                dve.drain()
                v.tensor_tensor(Y[:, :, :], Y[:, :, :], g[:, :, :], ALU.mult).then_inc(rw_out.sem, 1)

                for q in range(6):
                    split_through(layer, PA["gate0"] + 4 * q + 5)
                    for n in range(4 * q, 4 * q + 4):
                        t, br = n // 3, n % 3
                        dve.drain()
                        dve.wait_ge(proj_done.sem, proj_done.at(layer, 14 + n + 1))
                        dve.wait_ge(br_psum.sem, br_psum.at(layer, 1 + n + 1))
                        v.tensor_tensor(comb[:, t % 2, :] if br == 0 else brtmp[:, n % 2, :],
                                        ps[:, 4 + n % 4, 0:TOK], gsig[:, n % 4, :], ALU.mult
                                        ).then_inc(br_free.sem, 1)
                        if n % 4 == 3:
                            dve.drain().then_inc(slot_free[AT[f"branch{q}"] % SLOTS].sem, 1)
                        if br:
                            dve.drain()
                            last = v.tensor_tensor(comb[:, t % 2, :], comb[:, t % 2, :], brtmp[:, n % 2, :],
                                                   ALU.add)
                            if br == 2:
                                last.then_inc(comb_sum.sem, 1)
                    for t in range(KT):
                        if (3 * t + 2) // 4 == q:
                            dve.wait_ge(comb_hi.sem, comb_hi.at(layer, t + 1))
                            v.tensor_tensor(hA[1][:, t, :], comb[:, t % 2, :], hA[0][:, t, :], ALU.subtract
                                            ).then_inc(comb_ready.sem, 1)
                for t in range(KT):
                    split_through(layer, PA["out"] + t + 2)
                    dve.wait_ge(piece_used.sem, piece_used.at(layer, PA["out"] + t + 1))
                    for c, s0, s1 in SEGS:
                        last = v.scalar_tensor_tensor(out=x[:, t, s0:s1], in0=ps[:, t % 4, s0:s1],
                                                      scalar=modv[:, 5, t, c:c + 1], in1=x[:, t, s0:s1],
                                                      op0=ALU.mult, op1=ALU.add)
                    last.then_inc(out_free.sem, 1)
                dve.drain()
                inverse_root(layer, 2)
                normalise(layer, 2, 24, hA)
                ffn(layer, 1)
                cursor[0] = 0
                dve.drain()
            inverse_root(DEPTH, 0)
            for t in range(KT):
                last = v.scalar_tensor_tensor(out=x[:, t, :], in0=x[:, t, :], scalar=C("final_g")[:, t:t + 1],
                                              in1=rinv[:, :], op0=ALU.mult, op1=ALU.mult)
            last.then_inc(y_ready.sem, 1)

        @blk.gpsimd
        def _(pool):
            g_ = nc.gpsimd
            with pool.Fori(0, DEPTH) as layer:
                pool.wait_ge(const_landed.sem, 16)
                pool.wait_ge(small_landed.sem, small_landed.at(layer, 16))
                for n in range(8):
                    tab = S("bias", TOK)[:, n, 0:256].rearrange("p (a b) -> p a b", b=64)
                    last = g_.tensor_tensor(tab, tab, bcast(C("okcol"), 4), ALU.mult)
                pool.drain()
                for n in range(8):
                    tab = S("bias", TOK)[:, n, 0:256].rearrange("p (a b) -> p a b", b=64)
                    last = g_.tensor_tensor(tab, tab, bcast(C("negcol"), 4), ALU.add)
                last.then_inc(bias_ready.sem, 1)
                for rd in range(3):
                    for m in range(1, LEVELS):
                        for grp in range(2):
                            if m == 1:
                                pool.wait_ge(gram_masked.sem, gram_masked.at(layer, 8 * rd + 4 * grp + 4))
                                if rd == 0:
                                    pool.wait_ge(exps_ready.sem, exps_ready.at(layer, 1))
                            if m >= 2:
                                pool.wait_ge(inv_psum.sem, inv_psum.at(layer, inv_x(rd, m - 2, grp)))
                                pool.wait_ge(t_ready.sem, t_ready.at(layer, lev(rd, m - 2, grp)))
                            g_.tensor_tensor(Nm[:, m % 2, 4 * grp:4 * grp + 4, :],
                                             G[:, 4 * grp:4 * grp + 4, 2, :],
                                             bcast(C(f"level{grp}", P)[:, m, :], 4), ALU.mult
                                             ).then_inc(level_masked.sem, 1)


def packed(where, width, lead=()):
    a = np.zeros((*lead, P, width), np.float32)

    def put(name, v):
        lo, hi = where[name]
        v = np.asarray(v)
        v = v.reshape(*v.shape[:len(lead) + 1], -1)
        a[..., lo:lo + v.shape[-1]] = v
        assert v.shape[-1] <= hi - lo
    return a, put


def shape_constants():
    i = np.arange(P)
    s, t = i[:, None], i[None, :]
    out = {"ident": np.eye(P), "ones": np.ones((P, P)), "block": s // 64 == t // 64}
    for d in range(2):
        before = (s < t) if d == 0 else (s > t)
        upto = (s <= t) if d == 0 else (s >= t)
        mid = (s < 64) if d == 0 else (s >= 64)
        out[f"cum{d}"] = np.concatenate([upto * 1.0 - mid, before * 1.0 - mid], 1)
        out[f"gram{d}"] = np.concatenate([before * 1.0, upto * 1.0, before * -1.0, upto * -1.0], 1)
        levels = []
        for lv in range(LEVELS):
            m = 1 << lv
            half_s, half_t = s // m % 2, t // m % 2
            levels.append((s // (2 * m) == t // (2 * m)) & ((half_s == d) & (half_t == 1 - d)))
        out[f"level{d}"] = np.stack(levels, 1)
    heads = np.zeros((P, 2, 4))
    for p in range(2):
        for hh in range(2):
            heads[64 * hh:64 * hh + 64, p, 2 * p + hh] = 1
    out["heads"] = heads
    qc, kc = i % 64, np.arange(64)
    lo = np.clip(qc - 8, 0, 48)[:, None]
    ok = (kc[None] >= lo) & (kc[None] < lo + 16)
    out["okcol"], out["negcol"] = ok, np.where(ok, 0.0, -1e30)
    n_freq = ROPE // 4
    inv = 1.0 / (10000.0 ** (np.arange(n_freq) / n_freq))
    pos = np.arange(DEC)
    ang = np.concatenate([(pos // 64)[:, None] * inv, (pos % 64)[:, None] * inv], -1).T
    rope = np.zeros((P, TOK))
    rope[64:96, 0:SEQ] = 1
    rope[64:96, SEQ:] = np.concatenate([np.cos(ang)] * 2)
    rope[96:112, SEQ:], rope[112:128, SEQ:] = -np.sin(ang), np.sin(ang)
    out["rope"] = rope
    pick = np.zeros((P, 2))
    pick[0::32, 0] = pick[1::32, 1] = 1
    out["pick"] = pick
    out["eps"] = np.tile([1e-6, 64e-5, 0, 0], (P, 1))
    return out


def by_feature(v, lead):
    return np.swapaxes(v.reshape(*v.shape[:lead], -1, P), -1, -2)


def weight_stream(w):
    out = np.zeros((DEPTH * NBLK, P, WIDE), np.float32)
    for layer in range(DEPTH):
        def put(name, i, v):
            v = v.reshape(P, -1)
            out[layer * NBLK + AT[name] + i, :, 0:v.shape[1]] = v

        def tiles(m):
            return m.reshape(m.shape[0] // P, P, m.shape[1] // P, P).transpose(1, 2, 0, 3)

        ada = w["ada_w"][layer].reshape(KT, P, ADA, 256)
        for c in range(ADA):
            half, i = divmod(c - ADA0, HALF)
            put(*(("ada", c) if c < ADA0 else (f"up0{half}", 2 * i)), ada[:, :, c].transpose(1, 0, 2))
        for f in range(2):
            wg, wu = tiles(w["ffn_wg"][layer, f]), tiles(w["ffn_wu"][layer, f])
            wd = tiles(w["ffn_wd"][layer, f])
            for half in range(2):
                for t in range(HALF):
                    n = half * HALF + t
                    put(f"up{f}{half}", 2 * t + 1 if f == 0 else t, np.stack([wg[:, n], wu[:, n]], 1))
                for t in range(KT):
                    put(f"down{f}{half}", t, wd[:, t, HALF * half:HALF * half + HALF])
        w_in = w["w_in"][layer]
        feat = tiles(np.concatenate([w_in[:, 0:512], w_in[:, 768:1280], w_in[:, 1536:2304]], 1))
        for i in range(7):
            put("proj", i, feat[:, 2 * i:2 * i + 2])
        kr = w_in[:, 2304:2336]
        put("kr", 0, tiles(np.concatenate([np.zeros((D, 64), np.float32), kr, swap_halves(kr)], 1)))
        vals = np.concatenate([w_in[:, 512:768], w_in[:, 1280:1536]], 1).reshape(KT, P, 512)
        for half in range(2):
            put("v", half, vals[4 * half:4 * half + 4].transpose(1, 0, 2))
        gates = tiles(w_in[:, 2336:])
        order = [br * KT + t for t in range(KT) for br in range(3)]
        for i in range(12):
            put(f"gate{i}", 0, gates[:, order[2 * i:2 * i + 2]])
        br = np.stack([tiles(w["w_br"][layer, n]) for n in range(3)], 2).reshape(P, 24, 2, P)
        for i in range(6):
            put(f"branch{i}", 0, br[:, 4 * i:4 * i + 4])
        wo = tiles(w["w_o"][layer])
        for i in range(4):
            put("out", i, wo[:, 2 * i:2 * i + 2])
    return out


def swap_halves(a):
    return np.concatenate([a[..., ROPE // 2:], a[..., :ROPE // 2]], -1)


def small_weights(w):
    a, put = packed(SMALL, NSMALL, (DEPTH,))
    L = DEPTH
    put("kk", by_feature(w["rw_kk"], 1))
    put("ka", by_feature(w["rw_ka"], 1))
    put("rk", by_feature(w["rw_rk"].reshape(L, 256), 1))
    put("a0", by_feature(w["rw_a0"].reshape(L, 512), 1))
    put("qn", by_feature(w["mla_qn_g"], 1))
    put("kvn", by_feature(w["mla_kvn_g"], 1))
    put("w2", w["rw_w2"].reshape(L, P, 256))
    put("a2", w["rw_a2"].reshape(L, P, 256))
    put("g2", w["rw_g2"])
    for name, v in (("w0", w["rw_w0"].reshape(L, 1, 512)), ("gnw", w["rw_gn_w"][:, None]),
                    ("gnb", w["rw_gn_b"][:, None])):
        put(name, np.broadcast_to(v, (L, P, v.shape[-1])))
    uq = w["mla_w_uq"].reshape(L, 2, P, 4, NOPE + ROPE)
    put("uq", np.concatenate([uq, swap_halves(uq[..., NOPE:])], -1).transpose(0, 2, 1, 3, 4))
    ukv = w["mla_w_ukv"].reshape(L, P, 4, 2, 64)
    put("ukv_k", ukv[:, :, :, 0])
    put("ukv_v", ukv[:, :, :, 1])
    nk = w["cache_na_k"][0].reshape(L, 2, 2, P, HD)
    put("na_k", nk.transpose(0, 2, 4, 1, 3).reshape(L, P, 256))
    put("na_v", w["cache_na_v"][0].transpose(0, 2, 1, 3).reshape(L, P, 256))
    put("ckv", w["cache_mla_ckv"][0].transpose(0, 2, 1))
    lo = SMALL["krope"][0]
    a[:, 64:96, lo:lo + P] = w["cache_mla_krope"][0].transpose(0, 2, 1)
    st = np.stack([w["state_rwkv_fwd"][0], w["state_rwkv_bwd"][0]], 1).reshape(L, 2, 2, 2, HD, HD)
    put("state", st.transpose(0, 3, 5, 1, 2, 4).reshape(L, P, 256))
    q, n = np.arange(DEC), np.arange(DEC)
    row = n[None] // 64 - q[:, None] // 64 + 7
    col = np.clip(n[None] % 64 - q[:, None] % 64 + 15, 0, 30)
    tab = w["na_rpb"][:, :, row, col].reshape(L, 4, 2, P, DEC)
    full = np.zeros((L, P, 2, 4, TOK), np.float32)
    full[..., 0:DEC] = tab.transpose(0, 3, 2, 1, 4)
    put("bias", full)
    return a


def constants(w):
    a, put = packed(CONST, NCONST)
    for name, v in shape_constants().items():
        put(name, v)
    put("final_g", by_feature(w["final_g"], 0))
    cond = np.zeros((P, KT, 32), np.float32)
    cond[:, :, 0], cond[:, :, 1] = by_feature(w["c_ctx"], 0), by_feature(w["c"][0], 0)
    put("cond", cond)
    put("ada_b", np.repeat(by_feature(w["ada_b"], 1).transpose(1, 0, 2)[..., None], 2, -1))
    put("norm_g", np.repeat(by_feature(w["norm_g"], 2).transpose(2, 0, 1, 3)[..., None], 2, -1))
    return a


_OUTS = [("y", (P, KT, TOK)), ("k", (DEPTH, P, 2, SEQ)), ("v", (DEPTH, P, 256)),
         ("ckv", (DEPTH, P, SEQ)), ("kr", (DEPTH, ROPE, SEQ)), ("s", (DEPTH, P, 4, HD))]


def kernel(**inputs):
    import concourse.bacc as _bacc
    from concourse.bass_utils import run_bass_kernel_spmd as _run

    w = {name: np.asarray(a) for name, a in inputs.items()}
    tokens = np.concatenate([w["x_prompt"][0], w["x_sample"][0]], 0)
    arrays = {
        "wstream": weight_stream(w),
        "small_d": small_weights(w),
        "const_d": constants(w),
        "x_d": np.ascontiguousarray(tokens.T.reshape(KT, P, TOK).transpose(1, 0, 2)),
    }
    nc = _bacc.Bacc("TRN2", target_bir_lowering=False, num_devices=1)
    f32 = mybir.dt.float32
    args = [nc.dram_tensor(n, a.shape, f32, kind="ExternalInput").ap() for n, a in arrays.items()]
    args += [nc.dram_tensor(f"out_{n}", s, f32, kind="ExternalOutput").ap() for n, s in _OUTS]
    hybrid_step(nc, *args)
    res = _run(nc, [arrays], core_ids=[0]).results[0]
    y, k, v, ckv, kr, s = (res[f"out_{n}"] for n, _ in _OUTS)
    y = y.transpose(2, 1, 0).reshape(TOK, D)
    k = k.reshape(DEPTH, 2, HD, 2, SEQ).transpose(0, 3, 1, 4, 2).reshape(1, DEPTH, HEADS, SEQ, HD)
    v = v.reshape(DEPTH, SEQ, HEADS, HD).transpose(0, 2, 1, 3)[None]
    s = s.reshape(DEPTH, 2, HD, 2, 2, HD).transpose(3, 0, 4, 1, 5, 2).reshape(2, 1, DEPTH, HEADS, HD, HD)
    return (y[None, 0:SEQ], y[None, SEQ:], k, v, ckv.transpose(0, 2, 1)[None],
            kr.transpose(0, 2, 1)[None], s[0], s[1])
```

```python
from contextlib import ExitStack

import concourse.bass as bass
from concourse import mybir
import numpy as np

P = 128
DEPTH, D, DFF = 2, 1024, 2816
SEQ, DEC = 128, 256
TOK = SEQ + DEC
KEYS = TOK + 128
KT, FT = D // P, DFF // P
HEADS, HD, ROPE, NOPE = 4, 64, 32, 64
NMOD = 9
CHUNK = 128
LEVELS = 7
SEGS = ((0, 0, SEQ), (1, SEQ, TOK))
DECAY = float(np.exp(-0.5))
Q_SCALE = (NOPE + ROPE) ** -0.5

WIDE, NARROW = 16 * P, 11 * P
ADA, ADA0, HALF = 36, 16, FT // 2
ADAL = (DEPTH * ADA - ADA0) // DEPTH
NEXT = ADAL - FT
FFN0 = [("up00", 2 * HALF), ("down00", KT), ("up01", 2 * HALF), ("down01", KT)]
FFN1 = [("up10", HALF), ("down10", KT), ("up11", HALF), ("down11", KT)]
MIX = [(name, 1) for q in range(6) for name in (f"gate{2 * q}", f"gate{2 * q + 1}", f"branch{q}")]
STAGES = (FFN0 + [("proj", 7), ("kr", 1), ("v", 2)] + MIX[:1] + [("ada_next", NEXT)] + MIX[1:]
          + [("out", 4)] + FFN1)
AT, NBLK = {}, 0
for _name, _n in STAGES:
    AT[_name] = NBLK
    NBLK += _n
SLOTS = 4
TURN0 = ADA0 // SLOTS
assert NBLK % SLOTS == 0 and ADA0 % SLOTS == 0
assert ADA0 + ADAL >= ADA + 2 * KT // 2

PIECES = []


def _pieces(name, n, step=1, first=0, cols=(0, 8 * P, 16 * P)):
    PA.setdefault(name, len(PIECES))
    for i in range(n):
        for c0, c1 in zip(cols[:-1], cols[1:]):
            PIECES.append((AT[name] + first + step * i, c0, c1))


PA = {}
DOWN_CUT = (0, 6 * P, 11 * P)
for _h in range(2):
    _pieces(f"up0{_h}", HALF, 2, 1)
    _pieces(f"down0{_h}", KT, cols=DOWN_CUT)
_pieces("proj", 7)
_pieces("kr", 1, cols=(0, 4 * P, 8 * P))
_pieces("v", 2)
for _q in range(12):
    _pieces(f"gate{_q}", 1)
_pieces("out", 4)
for _h in range(2):
    _pieces(f"up1{_h}", HALF)
    _pieces(f"down1{_h}", KT, cols=DOWN_CUT)
NPIECE = len(PIECES)
assert NPIECE % 2 == 0 and all(p % 2 == 0 for p in PA.values())


def layout(parts):
    at, where = 0, {}
    for name, n in parts:
        where[name] = (at, at + n)
        at += n
    return where, at


CONST, NCONST = layout([
    ("ident", P), ("ones", P), ("block", P), ("cum0", 2 * P), ("cum1", 2 * P),
    ("level0", LEVELS * P), ("level1", LEVELS * P), ("gram0", 4 * P), ("gram1", 4 * P),
    ("heads", 8), ("okcol", 64), ("negcol", 64), ("rope", TOK), ("pick", 2), ("final_g", KT),
    ("cond", KT * 32), ("eps", 4), ("ada_b", DEPTH * 144), ("norm_g", DEPTH * 48)])
SMALL, NSMALL = layout([
    ("kk", 2), ("ka", 2), ("rk", 2), ("a0", 4), ("qn", 2), ("kvn", 1), ("pad", 3),
    ("w2", 512), ("a2", 512), ("g2", 256), ("w0", 512), ("gnw", 256), ("gnb", 256),
    ("krope", P), ("state", 256),
    ("uq", 1024), ("ukv_k", 256), ("ukv_v", 256), ("na_k", 256), ("na_v", 256), ("ckv", P),
    ("bias", 3072)])

JOBS = [(b, h, q) for b in range(2) for h in range(HEADS) for q in range(3)]
ROUNDS = [(0, 0), (1, 2), (2, 1)]
UNITS = [(d, p, hh) for d in range(2) for p in range(2) for hh in range(2)]


def hybrid_step(nc, wstream, small_d, const_d, x_d, y_d, k_d, v_d, ckv_d, kr_d, s_d):
    F32, F32R = mybir.dt.float32, mybir.dt.float32r
    ALU, ACT, AX = mybir.AluOpType, mybir.ActivationFunctionType, mybir.AxisListType.X

    with ExitStack() as ctx:
        def sb(name, *shape):
            return ctx.enter_context(nc.sbuf_tensor(name, [P, *shape], F32))

        const = sb("const", NCONST)
        small = sb("small", NSMALL)
        ring = sb("ring", SLOTS, WIDE)
        x = sb("x", KT, TOK)
        w_hi = ctx.enter_context(nc.sbuf_tensor("w_hi", [P, 2, 8 * P], F32R))
        w_lo = ctx.enter_context(nc.sbuf_tensor("w_lo", [P, 2, 8 * P], F32R))
        tmp = sb("tmp", 2432)
        rinv = sb("rinv", TOK)
        mod_all = sb("mod_all", DEPTH * NMOD * KT * 2)
        mod = sb("mod", NMOD * KT * 2)
        scale_c = sb("scale_c", 3, KT, 2)
        gate_c = sb("gate_c", 2, KT, 2)
        bonus = sb("bonus", 12)
        s_out = sb("s_out", 4, HD)
        s_mid = sb("s_mid", 4, HD)
        s_in = sb("s_in", 4, HD)
        pmid = sb("pmid", 4)
        pend = sb("pend", 2, 2, 2)
        stat = sb("stat", 32)
        stat2 = sb("stat2", 32)
        sqrt_scratch = sb("sqrt_scratch", 1)
        with ExitStack() as region:
            def mx(name, *shape):
                return region.enter_context(nc.sbuf_tensor(name, [P, *shape], F32))
            sig = mx("sig", 3, 512)
            b = mx("b", 2, 2, TOK)
            kd = mx("kd", 2, 2, TOK)
            g = mx("g", 3, 256)
            kk = mx("kk", 2, TOK)
            V = mx("V", 3, 512)
            r = mx("r", 2, TOK)
            k = mx("k", 2, TOK)
            Y = mx("Y", 3, 256)
            oT = [mx(f"oT{i}", 2, TOK) for i in range(2)] + [k]
            big = mx("big", 24 * TOK)
        with ExitStack() as region:
            def mr(name, *shape):
                return region.enter_context(nc.sbuf_tensor(name, [P, *shape], F32R))
            hA = mr("hA_hi", KT, TOK), mr("hA_lo", KT, TOK)
            mr("gap_a", 5376)
            hid = mr("hid_hi", HALF, TOK), mr("hid_lo", HALF, TOK)
        with ExitStack() as region:
            mr("gap_b", 6144 + 5376)
            hB = mr("hB_hi", KT, TOK), mr("hB_lo", KT, TOK)
        ps = ctx.enter_context(nc.psum_tensor("ps", [P, 8, 512], F32))

        def C(name, *dims):
            a, e = CONST[name]
            v = const[:, a:e]
            return v.rearrange("p (a b) -> p a b", b=dims[0]) if dims else v

        def S(name, b_=None):
            a, e = SMALL[name]
            v = small[:, a:e]
            return v.rearrange("p (a b) -> p a b", b=b_) if b_ else v

        def bcast(ap, times):
            return ap.unsqueeze(1).broadcast_to([ap.shape[0], times, ap.shape[1]])

        def spread(ap, width):
            return ap.unsqueeze(2).broadcast_to([ap.shape[0], ap.shape[1], width])

        def view(t, at, *dims):
            n = 1
            for d_ in dims:
                n *= d_
            v = t[:, at:at + n]
            if len(dims) == 2:
                return v.rearrange("p (a b) -> p a b", b=dims[1])
            if len(dims) == 3:
                return v.rearrange("p (a b c) -> p a b c", b=dims[1], c=dims[2])
            if len(dims) == 4:
                return v.rearrange("p (a b c d) -> p a b c d", b=dims[1], c=dims[2], d=dims[3])
            return v

        root, rows = view(tmp, 0, TOK), view(tmp, TOK, 2, 256)
        rows_next = view(tmp, 5 * TOK, 256)
        htmp = view(tmp, 896, 3, TOK)
        silu, product = view(tmp, 896, 2, TOK), view(tmp, 896 + 2 * TOK, 2, TOK)
        sq, sq_sum = view(tmp, 896, 2, TOK), view(tmp, 896 + 2 * TOK, TOK)
        root2 = view(tmp, 0, 2, TOK)
        prod = view(tmp, 2 * TOK, 2, TOK)
        ropes = view(tmp, 0, 4, TOK)
        prob, probT = view(tmp, 0, 3, TOK), view(tmp, 3 * TOK, 2, TOK)
        KBt = view(tmp, 0, 2, 512)
        Fm, Um = view(tmp, 1024, 8, HD), view(tmp, 1536, 8, HD)
        gsig, brtmp, comb = (view(big, 6144, 4, TOK), view(big, 6144 + 4 * TOK, 2, TOK),
                             view(big, 6144 + 6 * TOK, 2, TOK))
        KTm = view(big, 0, 4, KEYS)
        kT = view(big, 2048, 2, KEYS)
        qT = view(big, 3072, 2, TOK)
        qm = view(big, 3840, 4, TOK)
        Vm = view(big, 5376, 4, 256)
        ckvT = view(big, 6400, KEYS)
        dq = view(big, 6912, 2, TOK)
        kpe = view(big, 7680, TOK)
        sq3 = view(big, 8064, 3, TOK)
        G = view(big, 0, 8, 4, P)
        T, Tt, X = (view(big, 4096 + 1024 * i, 8, P) for i in range(3))
        Nm = view(big, 7168, 2, 8, P)
        b0 = SMALL["uq"][0]
        E1 = view(small, b0, 2, 2, 2, P)
        E2 = view(small, b0 + 1024, 2, 2, P)
        Ft = view(small, b0 + 1536, 4, P)
        KB = view(small, b0 + 2048, 2, 2, 2, P)
        KR = view(small, b0 + 3072, 4, 2, 2, P)
        assert b0 + 3072 + 2048 <= NSMALL
        kr_raw = S("krope")
        w1t, a1 = oT[1][:, 0, :], oT[1][:, 1, :]
        bonus_in = oT[1]
        g1s = view(Y[:, :, :].rearrange("p a b -> p (a b)"), 0, TOK)
        ident, ones, block = C("ident"), C("ones"), C("block")
        eps6, epsgn = C("eps")[:, 0:1], C("eps")[:, 1:2]
        modv = mod[:, :].rearrange("p (m t c) -> p m t c", t=KT, c=2)

        class Signal:
            def __init__(self, name, per_layer, credit=0):
                self.sem = ctx.enter_context(nc.semaphore(name))
                self.n, self.credit = per_layer, credit

            def at(self, layer, count):
                return layer * self.n + (count + self.credit)

        landed = [Signal(f"landed{i}", 16 * NBLK // SLOTS, 16 * TURN0) for i in range(SLOTS)]
        slot_free = [Signal(f"slot_free{i}", NBLK // SLOTS) for i in range(SLOTS)]
        hi_ready, split_ready = Signal("piece_hi_ready", NPIECE), Signal("piece_split", NPIECE)
        piece_used = Signal("piece_used", NPIECE, 2)
        hid_hi, hid_ready = Signal("hid_hi_ready", 2 * FT), Signal("hid_ready", 2 * FT)
        const_landed = Signal("const_landed", 0)
        x_landed = Signal("x_landed", 0)
        small_landed = Signal("small_landed", 16)
        cond_ready = Signal("cond_ready", 0)
        ada_psum, rows_ready, cols_ready = (Signal(n, ADAL) for n in ("ada_psum", "ada_rows_ready", "ada_cols_ready"))
        mod_done = Signal("mod_done", ADAL, 1)
        sq_ready, sq_added, ss_psum = Signal("square_ready", 24), Signal("square_added", 18), Signal("sumsq_psum", 3)
        root_ready = Signal("root_ready", 3)
        h_scaled, h_hi, h_ready = (Signal(n, 32) for n in ("h_scaled", "h_hi_ready", "h_ready"))
        silu_ready = Signal("silu_ready", 2 * FT)
        up_free = Signal("up_banks_free", 2 * FT, 2)
        down_free = Signal("down_banks_free", 32, 2)
        proj_done = Signal("proj_done", 14 + 24)
        v_done = Signal("v_done", 1)
        wlog_ready, wlog_biased, sig_ready = (Signal(n, 1) for n in ("wlog_ready", "wlog_biased", "sig_ready"))
        a_ready, a_done = Signal("a_ready", 1), Signal("a_done", 1)
        g_ready, g_done = Signal("g_ready", 1), Signal("g_done", 1)
        kksq_ready, kkss_ready, kkmax_ready, kkroot_ready = (
            Signal(n, 1) for n in ("kksq_ready", "kkss_ready", "kkmax_ready", "kkroot_ready"))
        prod_ready, bonus_psum, bonus_done = (Signal(n, 1) for n in ("prod_ready", "bonus_psum", "bonus_done"))
        mla_sq, mla_ss, mla_root, mla_normed = (
            Signal(n, 1) for n in ("mla_sq", "mla_ss", "mla_root", "mla_normed"))
        q_psum, q_done, q_turned, kn_psum, kn_done, vm_psum, vm_done = (
            Signal(n, 1) for n in ("q_psum", "q_done", "q_turned", "kn_psum", "kn_done", "vm_psum", "vm_done"))
        bias_ready = Signal("bias_ready", 1)
        NJ = len(JOBS)
        scored, maxed, exped, normed, pT_psum, pT_ready, o_psum, o_done = (
            Signal(n, NJ) for n in ("scored", "maxed", "exped", "normed", "pT_psum", "pT_ready", "o_psum", "o_done"))
        cum_ready, exps_ready, factors_ready = (Signal(n, 3) for n in ("cum_ready", "exps_ready", "factors_ready"))
        gram_psum, gram_masked = Signal("gram_psum", 24), Signal("gram_masked", 24)
        kbt_psum, kbt_ready = Signal("kbt_psum", 3), Signal("kbt_ready", 3)
        level0_masked, level_masked = Signal("level0_masked", 6), Signal("level_masked", 3 * (LEVELS - 1) * 2)
        t_ready = Signal("inv_t_ready", 3 * LEVELS * 2)
        x_ready = Signal("inv_x_ready", 3 * (LEVELS - 1) * 2)
        inv_psum = Signal("inv_psum", 3 * (4 * LEVELS - 2))
        f_psum, ft_ready, ft_psum, f_ready, y_psum, round_done, state_ready = (
            Signal(n, 3) for n in ("f_psum", "ft_ready", "ft_psum", "f_ready", "y_psum", "round_done", "state_ready"))
        u_psum, u_ready = Signal("u_psum", 6), Signal("u_ready", 6)
        Y_psum, Y_ready, gn_var, gn_root, rw_out, rwT_ready = (
            Signal(n, 1) for n in ("rw_tokens_psum", "rw_tokens_ready", "gn_var", "gn_root", "rw_out", "rwT_ready"))
        br_psum, br_free = Signal("br_psum", 25), Signal("br_free", 24)
        comb_sum, comb_hi, comb_ready = (Signal(n, 8) for n in ("comb_sum", "comb_hi_ready", "comb_ready"))
        out_free = Signal("out_free", 8, 8)
        kv_stored, s_stored = Signal("kv_stored", 64), Signal("s_stored", 16)
        y_ready, y_stored = Signal("y_ready", 0), Signal("y_stored", 0)

        def chunk_of(layer, j, i=0):
            return layer * ADAL + (i + (ADA0 + j))

        def lev(rd, m, grp):
            return (rd * LEVELS + m) * 2 + grp + 1

        def lev1(rd, m, grp):
            return (rd * (LEVELS - 1) + m - 1) * 2 + grp + 1

        def inv_x(rd, m, grp):
            return rd * (4 * LEVELS - 2) + (4 * m - 2 if m else 0) + grp + 1

        def inv_tt(rd, m, grp):
            return inv_x(rd, m, grp) + 2

        blk = ctx.enter_context(nc.Block())

        @blk.sync
        def _(sp):
            sp.dma_start(const[:, :], const_d).then_inc(const_landed.sem, 16)
            sp.dma_start(x[:, :, :], x_d).then_inc(x_landed.sem, 16)

            def load(row, slot, cols, turn):
                row, turn = sp.snap(row), sp.snap(turn)
                sp.wait_ge(slot_free[slot].sem, turn)
                sp.dma_start(ring[:, slot, 0:cols],
                             wstream[bass.ds(row, 1), :, 0:cols].rearrange("a p n -> (a p) n")
                             ).then_inc(landed[slot].sem, 16)

            with sp.Fori(0, TURN0) as i:
                for j in range(SLOTS):
                    load(i * SLOTS + j, j, WIDE, i + 1)
            with sp.Fori(0, DEPTH) as layer:
                for name, n in STAGES:
                    cols = NARROW if name.startswith("down") else WIDE
                    off = AT[name]
                    if n >= 2 * SLOTS:
                        with sp.Fori(0, n // SLOTS) as i:
                            for j in range(SLOTS):
                                load(layer * NBLK + (i * SLOTS + (ADA0 + off + j)), (off + j) % SLOTS, cols,
                                     layer * (NBLK // SLOTS) + (i + (TURN0 + (off + j) // SLOTS + 1)))
                    for j in range(n if n < 2 * SLOTS else n % SLOTS):
                        at = off + (0 if n < 2 * SLOTS else n // SLOTS * SLOTS) + j
                        load(layer * NBLK + (ADA0 + at), at % SLOTS, cols,
                             layer * (NBLK // SLOTS) + (TURN0 + at // SLOTS + 1))
                    if name == "down01":
                        row = sp.snap(layer + 0)
                        sp.wait_ge(out_free.sem, out_free.at(layer, 0))
                        sp.dma_start(small[:, :], small_d[bass.ds(row, 1)].rearrange("a p n -> (a p) n")
                                     ).then_inc(small_landed.sem, 16)
            sp.wait_ge(y_ready.sem, 1)
            sp.dma_start(y_d, x[:, :, :]).then_inc(y_stored.sem, 16)
            sp.wait_ge(y_stored.sem, 16)

        @blk.tensor
        def _(pe):
            mm = nc.tensor.matmul
            for s_ in slot_free:
                pe.sem_inc(s_.sem, 1)
            pe.sem_inc(piece_used.sem, 2)
            pe.wait_ge(const_landed.sem, 16)

            def block_of(layer, off, i=0):
                slot = off % SLOTS
                pe.wait_ge(landed[slot].sem,
                           layer * (16 * NBLK // SLOTS) + (i * 16 + 16 * (TURN0 + off // SLOTS + 1)))
                return ring[:, slot, :]

            def sumsq(layer, n):
                pe.wait_ge(sq_added.sem, sq_added.at(layer, 6 * n + KT - 2))
                mm(ps[:, 6, 0:TOK], ones, sq_sum, start=True, stop=False)
                pe.wait_ge(sq_ready.sem, sq_ready.at(layer, 8 * n + KT))
                mm(ps[:, 6, 0:TOK], ones, sq[:, (KT - 1) % 2, :], start=False, stop=True).then_inc(ss_psum.sem, 1)

            def piece_of(layer, n, shift=0):
                pe.wait_ge(split_ready.sem, layer * NPIECE + (shift + (n + 1)))
                return w_hi[:, n % 2, :], w_lo[:, n % 2, :]

            def mm3(out, stat_, mov, start, stop):
                mm(out, stat_[0], mov[0], start=start, stop=False)
                mm(out, stat_[0], mov[1], start=False, stop=False)
                return mm(out, stat_[1], mov[0], start=False, stop=stop)

            def both(pair, *at):
                return pair[0][at], pair[1][at]

            ALLP = slice(None)

            def tile8(w, h, out):
                for t in range(KT):
                    last = mm3(out, both(w, ALLP, slice(t * P, (t + 1) * P)), both(h, ALLP, t, ALLP),
                               t == 0, t == KT - 1)
                return last

            def first_tiles(layer, piece, h, hcount, outs):
                w = [piece_of(layer, piece + z) for z in range(2)]
                for t in range(KT):
                    pe.wait_ge(h_ready.sem, h_ready.at(layer, hcount + t + 1))
                    for z in range(2):
                        last = mm3(outs[z], both(w[z], ALLP, slice(t * P, (t + 1) * P)), both(h, ALLP, t, ALLP),
                                   t == 0, t == KT - 1)
                        if t == KT - 1:
                            last.then_inc(piece_used.sem, 1)

            def up(layer, f, half, i, tile, parity, off, hcount):
                pe.wait_ge(up_free.sem, layer * up_free.n + (tile + (f * FT + half * HALF + 1)))
                outs = [ps[:, parity * 2 + z, 0:TOK] for z in range(2)]
                if hcount is not None:
                    first_tiles(layer, off, hA, hcount, outs)
                    return
                for z in range(2):
                    tile8(piece_of(layer, off + z, i * 4), hA, outs[z]).then_inc(piece_used.sem, 1)

            def ada_rows(w, out):
                for t in range(KT):
                    q = t % 4
                    last = mm(out[32 * q:32 * q + 32, :], C("cond", 32)[:, t, :],
                              w[:, t * 256:(t + 1) * 256], start=t < 4, stop=t >= 4)
                last.then_inc(ada_psum.sem, 1)

            def ada_cols(chunk, src, out, slot):
                pe.wait_ge(rows_ready.sem, chunk + 1)
                pe.wait_ge(mod_done.sem, chunk + 1)
                for j in range(2):
                    last = mm(out[:, 2 * j:2 * j + 2], src[:, j * P:(j + 1) * P],
                              C("pick"), start=True, stop=True)
                    last.then_inc(*((slot_free[slot].sem, 1) if j == 0 else (cols_ready.sem, 1)))

            def down_tile(layer, f, half, i, dd, off, poff):
                for z in range(2):
                    w = piece_of(layer, poff + z, i * 8)
                    if z == 0:
                        pe.wait_ge(down_free.sem, layer * down_free.n + (i * 4 + (16 * f + 8 * half + dd + 1)))
                    n0, n1 = DOWN_CUT[z] // P, DOWN_CUT[z + 1] // P
                    for t in range(n0, n1):
                        if dd % 4 == 0:
                            pe.wait_ge(hid_ready.sem, hid_ready.at(layer, f * FT + half * HALF + t + 1))
                        last = mm3(ps[:, 4 + dd % 2, 0:TOK], both(w, ALLP, slice((t - n0) * P, (t - n0 + 1) * P)),
                                   both(hid, ALLP, t, ALLP), t == 0, t == HALF - 1)
                    last.then_inc(piece_used.sem, 1)

            def ffn(layer, f, hcount):
                for half in range(2):
                    name = f"up{f}{half}"
                    off, poff = AT[name], PA[name]

                    def pair(i, c, count=None):
                        if f == 0:
                            pe.wait_ge(down_free.sem, down_free.at(layer, 8 * half))
                            ada_rows(block_of(layer, off + 2 * c, i), ps[:, 4 + c % 2, 0:256])
                        up(layer, f, half, i, i * 2 + c, c % 2, poff + 2 * c, count)
                        if f == 0:
                            ada_cols(chunk_of(layer, half * HALF + c, i * 2), rows[:, c % 2, :],
                                     ps[:, 6 + c % 2, 0:4], (off + 2 * c) % SLOTS)

                    if half == 0:
                        pair(0, 0, hcount)
                        pair(0, 1)
                    with pe.Fori(1 - half, HALF // 2) as i:
                        pair(i, 0)
                        pair(i, 1)
                    c = HALF - 1
                    if f == 0:
                        ada_rows(block_of(layer, off + 2 * c), ps[:, 4, 0:256])
                    up(layer, f, half, 0, c, 0, poff + 2 * c, None)
                    if f == 0:
                        ada_cols(chunk_of(layer, half * HALF + c), rows[:, 0, :], ps[:, 6, 0:4],
                                 (off + 2 * c) % SLOTS)
                    off, poff = AT[f"down{f}{half}"], PA[f"down{f}{half}"]
                    if half == 0:
                        with pe.Fori(0, 2) as i:
                            for dd in range(4):
                                down_tile(layer, f, half, i, dd, off + dd, poff + 2 * dd)
                    else:
                        for dd in range(KT):
                            down_tile(layer, f, half, 0, dd, off + dd, poff + 2 * dd)
                        sumsq(layer, 1 + 2 * f)

            sumsq(0, 0)
            pe.wait_ge(cond_ready.sem, 1)
            with pe.Fori(0, TURN0) as i:
                for pair_ in range(2):
                    for c in range(2):
                        slot = 2 * pair_ + c
                        pe.wait_ge(landed[slot].sem, i * 16 + 16)
                        ada_rows(ring[:, slot, :], ps[:, 4 + c, 0:256])
                    for c in range(2):
                        slot = 2 * pair_ + c
                        ada_cols(i * SLOTS + slot, rows[:, c, :], ps[:, 6 + c, 0:4], slot)
            with pe.Fori(0, DEPTH) as layer:
                ffn(layer, 0, 0)

                first_tiles(layer, PA["proj"], hA, 8, [ps[:, z, 0:TOK] for z in range(2)])
                for t in range(2, 14):
                    w = piece_of(layer, PA["proj"] + t)
                    if t >= 4:
                        pe.wait_ge(proj_done.sem, proj_done.at(layer, t - 3))
                    tile8(w, hA, ps[:, t % 4, 0:TOK]).then_inc(piece_used.sem, 1)
                for z in range(2):
                    w = piece_of(layer, PA["kr"] + z)
                    for t in range(4):
                        last = mm3(ps[:, 4, 0:TOK], both(w, ALLP, slice(t * P, (t + 1) * P)),
                                   both(hA, ALLP, 4 * z + t, ALLP), z == 0 and t == 0, z == 1 and t == 3)
                    last.then_inc(piece_used.sem, 1)
                for q in range(4):
                    w = piece_of(layer, PA["v"] + q)
                    for j in range(3):
                        for z in range(2):
                            last = mm3(ps[:, 5 + j, :], both(hA, ALLP, 2 * q + z, slice(j * P, (j + 1) * P)),
                                       both(w, ALLP, slice(z * 512, (z + 1) * 512)),
                                       q == 0 and z == 0, q == 3 and z == 1)
                    last.then_inc(piece_used.sem, 1)
                    if q == 1:
                        pe.wait_ge(mla_sq.sem, mla_sq.at(layer, 1))
                        for z in range(2):
                            mm(ps[:, 0, 0:TOK], ones, sq3[:, z, :], start=z == 0, stop=z == 1)
                        mm(ps[:, 1, 0:TOK], ones, sq3[:, 2, :], start=True, stop=True).then_inc(mla_ss.sem, 1)
                pe.wait_ge(small_landed.sem, small_landed.at(layer, 16))

                pe.wait_ge(proj_done.sem, proj_done.at(layer, 14))
                pe.wait_ge(mla_normed.sem, mla_normed.at(layer, 1))
                for hd in range(HEADS):
                    for z in range(2):
                        last = mm(ps[:, hd, 0:TOK], S("uq")[:, (z * 4 + hd) * P:(z * 4 + hd + 1) * P],
                                  dq[:, z, :], start=z == 0, stop=z == 1)
                last.then_inc(q_psum.sem, 1)
                pe.wait_ge(v_done.sem, v_done.at(layer, 1))
                for i_ in range(4):
                    last = mm(ps[:, 4 + i_, 0:TOK], S("a2")[:, i_ * P:(i_ + 1) * P], a1, start=True, stop=True)
                last.then_inc(a_ready.sem, 1)
                pe.wait_ge(q_done.sem, q_done.at(layer, 1))
                pe.wait_ge(q_turned.sem, q_turned.at(layer, 1))
                for j in range(3):
                    last = mm(ps[:, j, :], w1t[:, j * P:(j + 1) * P], S("w2"), start=True, stop=True)
                last.then_inc(wlog_ready.sem, 1)
                pe.wait_ge(kksq_ready.sem, kksq_ready.at(layer, 1))
                pe.wait_ge(wlog_biased.sem, wlog_biased.at(layer, 1))
                for p in range(2):
                    last = mm(ps[:, 2 + p, 0:TOK], block, oT[0][:, p, :], start=True, stop=True)
                last.then_inc(kkss_ready.sem, 1)
                for j in range(3):
                    last = mm(ps[:, j // 2, j % 2 * 256:j % 2 * 256 + 256],
                              g1s[:, j * P:(j + 1) * P], S("g2"), start=True, stop=True)
                last.then_inc(g_ready.sem, 1)
                pe.wait_ge(a_done.sem, a_done.at(layer, 1))
                for hd in range(HEADS):
                    last = mm(ps[0:64, 4 + hd, :], S("ukv_k")[:, hd * 64:(hd + 1) * 64], ckvT,
                              start=True, stop=True)
                last.then_inc(kn_psum.sem, 1)
                pe.wait_ge(g_done.sem, g_done.at(layer, 1))
                for t in range(4):
                    last = mm(ps[:, t // 2, t % 2 * 256:t % 2 * 256 + 256], ckvT[:, t * P:(t + 1) * P],
                              S("ukv_v"), start=True, stop=True)
                last.then_inc(vm_psum.sem, 1)
                pe.wait_ge(kn_done.sem, kn_done.at(layer, 1))
                pe.wait_ge(vm_done.sem, vm_done.at(layer, 1))
                pe.wait_ge(kkmax_ready.sem, kkmax_ready.at(layer, 1))

                def scores(n):
                    br, hd, q = JOBS[n]
                    k0, k1 = (0, P) if q == 0 else (P, KEYS)
                    if n >= 3:
                        pe.wait_ge(exped.sem, exped.at(layer, n - 2))
                    if br == 0:
                        o, p = 64 * (hd % 2), hd // 2
                        ins = mm(ps[:, n % 3, 0:k1 - k0], qT[o:o + 64, p, q * P:(q + 1) * P],
                                 kT[o:o + 64, p, k0:k1], start=True, stop=True)
                    else:
                        ins = mm(ps[:, n % 3, 0:k1 - k0], qm[0:96, hd, q * P:(q + 1) * P],
                                 KTm[0:96, hd, k0:k1], start=True, stop=True)
                    ins.then_inc(scored.sem, 1)

                def turn(n):
                    _, _, q = JOBS[n]
                    pe.wait_ge(normed.sem, normed.at(layer, n + 1))
                    if n >= 2:
                        pe.wait_ge(pT_ready.sem, pT_ready.at(layer, n - 1))
                    for t in range(1 if q == 0 else 3):
                        last = nc.tensor.transpose(ps[:, 3 + n % 2, t * P:(t + 1) * P],
                                                   prob[:, n % 3, t * P:(t + 1) * P], ident)
                    last.then_inc(pT_psum.sem, 1)

                def weigh(n):
                    br, hd, q = JOBS[n]
                    o = 64 * (hd % 2)
                    pe.wait_ge(pT_ready.sem, pT_ready.at(layer, n + 1))
                    if n >= 2:
                        pe.wait_ge(o_done.sem, o_done.at(layer, n - 1))
                    tiles = (0,) if q == 0 else (1, 2, 3)
                    for i_, t in enumerate(tiles):
                        if br == 1:
                            v_ = Vm[:, t, hd * 64:(hd + 1) * 64]
                        elif t == 3:
                            v_ = S("na_v")[:, hd * 64:(hd + 1) * 64]
                        else:
                            v_ = V[:, t, hd * 64:(hd + 1) * 64]
                        last = mm(ps[o:o + 64, 5 + n % 2, 0:P], v_, probT[:, n % 2, i_ * P:(i_ + 1) * P],
                                  start=i_ == 0, stop=i_ == len(tiles) - 1)
                    last.then_inc(o_psum.sem, 1)

                for n in range(NJ + 3):
                    if n < NJ:
                        scores(n)
                        if n == 0:
                            pe.wait_ge(prod_ready.sem, prod_ready.at(layer, 1))
                            for j in range(3):
                                for p in range(2):
                                    last = mm(ps[:, 7, 4 * j:4 * j + 4], bonus_in[:, p, j * P:(j + 1) * P],
                                              C("heads", 4)[:, p, :], start=p == 0, stop=p == 1)
                            last.then_inc(bonus_psum.sem, 1)
                        j, step = divmod(n, 4)
                        if n == 1:
                            pe.wait_ge(bonus_done.sem, bonus_done.at(layer, 1))
                        if step == 1:
                            pe.wait_ge(mod_done.sem, chunk_of(layer, FT + j) + 1)
                            ada_rows(block_of(layer, AT["ada_next"] + j), ps[:, 7, 0:256])
                        if step == 3:
                            ada_cols(chunk_of(layer, FT + j), rows_next, ps[:, 7, 256:260],
                                     (AT["ada_next"] + j) % SLOTS)
                    if 2 <= n <= NJ + 1:
                        turn(n - 2)
                    if n >= 3:
                        weigh(n - 3)

                pe.wait_ge(o_done.sem, o_done.at(layer, NJ))
                pe.wait_ge(sig_ready.sem, sig_ready.at(layer, 1))
                def running_sums(rd):
                    for d in range(2):
                        for p in range(2):
                            last = mm(ps[:, 4 + d, p * 256:(p + 1) * 256],
                                      sig[:, ROUNDS[rd][d], d * 256 + p * P:d * 256 + (p + 1) * P],
                                      C(f"cum{d}"), start=True, stop=True)
                    last.then_inc(cum_ready.sem, 1)

                running_sums(0)
                for rd, tiles in enumerate(ROUNDS):
                    pe.wait_ge(factors_ready.sem, factors_ready.at(layer, rd + 1))
                    for n, (d, p, z) in enumerate(UNITS):
                        if rd and n == 5:
                            pe.wait_ge(round_done.sem, round_done.at(layer, rd))
                        mm(ps[:, (n + 2) % 8, :], KB[:, d, p, z, :],
                           KR[:, 2 * d + p].rearrange("p h z t -> p (h z t)"), start=True, stop=True
                           ).then_inc(gram_psum.sem, 1)
                    for m in range(LEVELS):
                        for grp in range(2):
                            if m == 0:
                                pe.wait_ge(level0_masked.sem, level0_masked.at(layer, 2 * rd + grp + 1))
                            else:
                                pe.wait_ge(level_masked.sem, level_masked.at(layer, lev1(rd, m, grp)))
                                pe.wait_ge(t_ready.sem, t_ready.at(layer, lev(rd, m - 1, grp)))
                            for q in range(4):
                                u = 4 * grp + q
                                last = mm(ps[:, 2 + grp, q * P:(q + 1) * P], Nm[:, m % 2, u, :],
                                          T[:, u, :] if m else ident, start=True, stop=True)
                            last.then_inc(inv_psum.sem, 1)
                        if m == 0:
                            pe.wait_ge(gram_masked.sem, gram_masked.at(layer, 8 * rd + 8))
                            for d in range(2):
                                for z in range(2):
                                    for p in range(2):
                                        last = nc.tensor.transpose(
                                            ps[:, d, (2 * z + p) * P:(2 * z + p + 1) * P],
                                            KB[:, d, p, z, :], ident)
                            last.then_inc(kbt_psum.sem, 1)
                            continue
                        if m == 1:
                            pe.wait_ge(kbt_ready.sem, kbt_ready.at(layer, rd + 1))
                            pe.wait_ge(state_ready.sem, state_ready.at(layer, rd + 1))
                            for u, (d, p, hh) in enumerate(UNITS):
                                o, c0 = 64 * hh, (2 * d + p) * P
                                mm(ps[o:o + 64, 0, c0:c0 + P], s_in[:, 2 * d + p, :],
                                   KR[:, 2 * d + p, hh, 0, :], start=u < 2, stop=False)
                            for u, (d, p, hh) in enumerate(UNITS):
                                o, hd, c0 = 64 * hh, 2 * p + hh, (2 * d + p) * P
                                last = mm(ps[o:o + 64, 0, c0:c0 + P],
                                          V[:, tiles[d], 256 + hd * 64:256 + hd * 64 + 64],
                                          G[:, u, 0, :], start=False, stop=u >= 6)
                            last.then_inc(f_psum.sem, 1)
                        if m == 2:
                            pe.wait_ge(ft_ready.sem, ft_ready.at(layer, rd + 1))
                            for i_ in range(4):
                                last = nc.tensor.transpose(ps[:, 1, i_ * P:(i_ + 1) * P], Ft[:, i_, :], ident)
                            last.then_inc(ft_psum.sem, 1)
                        if m == 3:
                            pe.wait_ge(f_ready.sem, f_ready.at(layer, rd + 1))
                            for u, (d, p, hh) in enumerate(UNITS):
                                o, hd, c0 = 64 * hh, 2 * p + hh, (2 * d + p) * P
                                mm(ps[o:o + 64, 0, c0:c0 + P],
                                   V[:, tiles[d], 256 + hd * 64:256 + hd * 64 + 64], G[:, u, 1, :],
                                   start=u < 2, stop=False)
                            for u, (d, p, hh) in enumerate(UNITS):
                                o, c0 = 64 * hh, (2 * d + p) * P
                                mm(ps[o:o + 64, 0, c0:c0 + P], s_in[:, 2 * d + p, :],
                                   KR[:, 2 * d + p, hh, 1, :], start=False, stop=False)
                        if m == LEVELS - 1 and rd < 2:
                            running_sums(rd + 1)
                        for grp in range(2):
                            pe.wait_ge(x_ready.sem, x_ready.at(layer, lev1(rd, m, grp)))
                            for q in range(4):
                                u = 4 * grp + q
                                if m < LEVELS - 1:
                                    mm(ps[:, 4 + grp, q * P:(q + 1) * P], Tt[:, u, :], X[:, u, :],
                                       start=True, stop=True)
                                last = mm(ps[:, 6 + grp, q * P:(q + 1) * P], X[:, u, :], Tt[:, u, :],
                                          start=True, stop=True)
                            last.then_inc(inv_psum.sem, 1)
                    for grp in range(2):
                        pe.wait_ge(t_ready.sem, t_ready.at(layer, lev(rd, LEVELS - 1, grp)))
                        for q in range(4):
                            u = 4 * grp + q
                            last = mm(ps[:, 2 + grp, q * 64:(q + 1) * 64], Tt[:, u, :], Fm[:, u, :],
                                      start=True, stop=True)
                        last.then_inc(u_psum.sem, 1)
                    if rd < 2:
                        for u, (d, p, hh) in enumerate(UNITS):
                            o, hd, c0 = 64 * hh, 2 * p + hh, (2 * d + p) * 64
                            mm(ps[o:o + 64, 7, c0:c0 + 64], KBt[:, d, p * P + o:p * P + o + 64],
                               V[:, tiles[d], 256 + hd * 64:256 + hd * 64 + 64], start=u < 2, stop=False)
                    for grp in range(2):
                        pe.wait_ge(u_ready.sem, u_ready.at(layer, 2 * rd + grp + 1))
                        for u in range(4 * grp, 4 * grp + 4):
                            d, p, hh = UNITS[u]
                            o, c0 = 64 * hh, (2 * d + p) * 64
                            if rd < 2:
                                mm(ps[o:o + 64, 7, c0:c0 + 64],
                                   KBt[:, d, 256 + p * P + o:256 + p * P + o + 64], Um[:, u, :],
                                   start=False, stop=u >= 6)
                            last = mm(ps[o:o + 64, 0, 2 * c0:2 * c0 + P], Um[:, u, :], G[:, u, 3, :],
                                      start=False, stop=u >= 6)
                    last.then_inc(y_psum.sem, 1)
                pe.wait_ge(round_done.sem, round_done.at(layer, 3))
                for j in range(3):
                    for p in range(2):
                        last = nc.tensor.transpose(
                            ps[:, 4 + j // 2, (j % 2 * 2 + p) * P:(j % 2 * 2 + p + 1) * P],
                            oT[2][:, p, j * P:(j + 1) * P], ident)
                last.then_inc(Y_psum.sem, 1)
                first_tiles(layer, PA["gate0"], hB, 16, [ps[:, z, 0:TOK] for z in range(2)])
                for q in range(6):
                    for n in range(max(4 * q, 2), 4 * q + 4):
                        w = piece_of(layer, PA["gate0"] + n)
                        if n >= 4:
                            pe.wait_ge(proj_done.sem, proj_done.at(layer, 14 + n - 3))
                        tile8(w, hB, ps[:, n % 4, 0:TOK]).then_inc(piece_used.sem, 1)
                    if q == 0:
                        pe.wait_ge(rw_out.sem, rw_out.at(layer, 1))
                        for p in range(2):
                            for j in range(3):
                                last = nc.tensor.transpose(ps[:, 4 + p, j * P:(j + 1) * P],
                                                           Y[:, j, p * P:(p + 1) * P], ident)
                        last.then_inc(br_psum.sem, 1)
                        pe.wait_ge(rwT_ready.sem, rwT_ready.at(layer, 1))
                    w = block_of(layer, AT[f"branch{q}"])
                    for n in range(4 * q, 4 * q + 4):
                        if n >= 4:
                            pe.wait_ge(br_free.sem, br_free.at(layer, n - 3))
                        for z in range(2):
                            last = mm(ps[:, 4 + n % 4, 0:TOK], w[:, (n % 4 * 2 + z) * P:(n % 4 * 2 + z + 1) * P],
                                      oT[(0, 2, 1)[n % 3]][:, z, :], start=z == 0, stop=z == 1)
                        last.then_inc(br_psum.sem, 1)
                for n in range(8):
                    w = piece_of(layer, PA["out"] + n)
                    if n >= 4:
                        pe.wait_ge(out_free.sem, out_free.at(layer, n - 3))
                    for t in range(KT):
                        if n == 0:
                            pe.wait_ge(comb_ready.sem, comb_ready.at(layer, t + 1))
                        last = mm3(ps[:, n % 4, 0:TOK], both(w, ALLP, slice(t * P, (t + 1) * P)),
                                   both(hA, ALLP, t, ALLP), t == 0, t == KT - 1)
                    last.then_inc(piece_used.sem, 1)
                sumsq(layer, 2)
                ffn(layer, 1, 24)

        @blk.scalar
        def _(act):
            A = nc.scalar.activation
            act.wait_ge(const_landed.sem, 16)
            A(C("cond"), C("cond"), ACT.Silu).then_inc(cond_ready.sem, 1)

            def load_sqrt():
                A(sqrt_scratch[:, :], eps6, ACT.Sqrt)

            def square(layer, n, t):
                if t >= 2:
                    act.wait_ge(sq_added.sem, sq_added.at(layer, 6 * n + max(t - 2, 1)))
                A(sq[:, t % 2, :], x[:, t, :], ACT.Square).then_inc(sq_ready.sem, 1)

            def take_root(layer, n):
                act.wait_ge(ss_psum.sem, ss_psum.at(layer, n + 1))
                A(root, ps[:, 6, 0:TOK], ACT.Sqrt, bias=eps6, scale=1.0 / D).then_inc(root_ready.sem, 1)

            def shift(layer, n, count, dst):
                for t in range(KT):
                    act.wait_ge(h_scaled.sem, h_scaled.at(layer, count + t + 1))
                    for c, s0, s1 in SEGS:
                        last = A(htmp[:, t % 3, s0:s1], htmp[:, t % 3, s0:s1], ACT.Identity,
                                 bias=modv[:, 3 * n, t, c:c + 1], scale=scale_c[:, n, t, c:c + 1])
                    if t % 2:
                        last.then_inc(h_hi.sem, 1)
                        continue
                    act.drain()
                    A(dst[0][:, t, :], htmp[:, t % 3, :], ACT.Copy).then_inc(h_hi.sem, 1)

            cursor = [0]

            def split_through(layer, n):
                while cursor[0] <= n:
                    m = cursor[0]
                    blk_, c0, c1 = PIECES[m]
                    slot = blk_ % SLOTS
                    act.wait_ge(landed[slot].sem, landed[slot].at(layer, 16 * (blk_ // SLOTS + 1)))
                    act.wait_ge(piece_used.sem, piece_used.at(layer, m - 1))
                    A(w_hi[:, m % 2, 0:c1 - c0], ring[:, slot, c0:c1], ACT.Copy).then_inc(hi_ready.sem, 1)
                    cursor[0] += 1

            def ada_rows(chunk, dst, src):
                act.wait_ge(ada_psum.sem, chunk + 1)
                A(dst, src, ACT.Copy).then_inc(rows_ready.sem, 1)

            def ffn(layer, f):
                for half in range(2):
                    p0 = PA[f"up{f}{half}"]
                    for t in range(HALF):
                        if f == 0:
                            ada_rows(chunk_of(layer, half * HALF + t), rows[:, t % 2, :], ps[:, 4 + t % 2, 0:256])
                        split_through(layer, p0 + 2 * t + 3)
                        act.wait_ge(piece_used.sem, piece_used.at(layer, p0 + 2 * t + 2))
                        A(silu[:, t % 2, :], ps[:, t % 2 * 2, 0:TOK], ACT.Silu).then_inc(silu_ready.sem, 1)
                        act.wait_ge(up_free.sem, up_free.at(layer, f * FT + half * HALF + t + 1))
                        A(hid[0][:, t, :], product[:, t % 2, :], ACT.Copy).then_inc(hid_hi.sem, 1)
                    p0 = PA[f"down{f}{half}"]
                    for t in range(KT):
                        split_through(layer, min(p0 + 2 * t + 3, p0 + 2 * KT, NPIECE - 1))
                        if half == 1:
                            n = 1 + 2 * f
                            if t == KT - 1:
                                load_sqrt()
                            act.wait_ge(down_free.sem, down_free.at(layer, 16 * f + 8 + t + 1))
                            square(layer, n, t)
                    split_through(layer, min(p0 + 2 * KT + 1, NPIECE - 1))
                take_root(layer, 1 + 2 * f)

            act.wait_ge(x_landed.sem, 16)
            for t in range(KT):
                square(0, 0, t)
            take_root(0, 0)
            with act.Fori(0, TURN0) as i:
                for c in range(SLOTS):
                    ada_rows(i * SLOTS + c, rows[:, c % 2, :], ps[:, 4 + c % 2, 0:256])
            with act.Fori(0, DEPTH) as layer:
                split_through(layer, 1)
                shift(layer, 0, 0, hA)
                ffn(layer, 0)
                shift(layer, 1, 8, hA)

                dest = ([qT[:, z, :] for z in range(2)] + [kT[:, z, 0:TOK] for z in range(2)]
                        + [r[:, z, :] for z in range(2)] + [k[:, z, :] for z in range(2)]
                        + [w1t, a1, g1s] + [dq[:, z, :] for z in range(2)] + [ckvT[:, 0:TOK]])
                for t in range(14):
                    split_through(layer, PA["proj"] + t + 2)
                    act.wait_ge(piece_used.sem, piece_used.at(layer, PA["proj"] + t + 1))
                    A(dest[t], ps[:, t % 4, 0:TOK], {8: ACT.Tanh, 10: ACT.Sigmoid}.get(t, ACT.Copy),
                      scale=HD ** -0.5 if t < 2 else 1.0).then_inc(proj_done.sem, 1)
                split_through(layer, PA["v"] + 3)
                act.wait_ge(mla_ss.sem, mla_ss.at(layer, 1))
                A(prod[:, 0, :], ps[:, 0, 0:TOK], ACT.Sqrt, bias=eps6, scale=1.0 / 256)
                A(prod[:, 1, :], ps[:, 1, 0:TOK], ACT.Sqrt, bias=eps6, scale=1.0 / P).then_inc(mla_root.sem, 1)
                split_through(layer, PA["gate0"] + 1)
                act.wait_ge(q_psum.sem, q_psum.at(layer, 1))
                A(qm[0:64, :, :], ps[0:64, 0:4, 0:TOK], ACT.Copy, scale=Q_SCALE).then_inc(q_done.sem, 1)
                act.wait_ge(a_ready.sem, a_ready.at(layer, 1))
                for d in range(2):
                    for p in range(2):
                        last = A(b[:, d, p, :], ps[:, 4 + 2 * d + p, 0:TOK], ACT.Sigmoid,
                                 bias=S("a0")[:, 2 * d + p:2 * d + p + 1])
                last.then_inc(a_done.sem, 1)
                act.wait_ge(wlog_biased.sem, wlog_biased.at(layer, 1))
                A(sig[:, :, :], sig[:, :, :], ACT.Sigmoid).then_inc(sig_ready.sem, 1)
                act.wait_ge(kkmax_ready.sem, kkmax_ready.at(layer, 1))
                A(root2, root2, ACT.Sqrt).then_inc(kkroot_ready.sem, 1)
                act.wait_ge(g_ready.sem, g_ready.at(layer, 1))
                A(g[:, 0:2, :].rearrange("p a b -> p (a b)"), ps[:, 0, :], ACT.Copy)
                A(g[:, 2, :], ps[:, 1, 0:256], ACT.Copy).then_inc(g_done.sem, 1)
                act.wait_ge(kn_psum.sem, kn_psum.at(layer, 1))
                A(KTm[0:64, :, :], ps[0:64, 4:8, :], ACT.Copy).then_inc(kn_done.sem, 1)
                act.wait_ge(vm_psum.sem, vm_psum.at(layer, 1))
                A(Vm[:, :, :].rearrange("p a b -> p (a b)"), ps[:, 0:2, :].rearrange("p a b -> p (a b)"),
                  ACT.Copy).then_inc(vm_done.sem, 1)
                act.wait_ge(mla_normed.sem, mla_normed.at(layer, 1))
                row = act.snap(layer + 0)
                act.dma_start(k_d[bass.ds(row, 1)].rearrange("a p t n -> (a p) t n"), kT[:, :, 0:SEQ]
                              ).then_inc(kv_stored.sem, 16)
                act.dma_start(v_d[bass.ds(row, 1)].rearrange("a p n -> (a p) n"), V[:, 0, 0:256]
                              ).then_inc(kv_stored.sem, 16)
                act.dma_start(ckv_d[bass.ds(row, 1)].rearrange("a p n -> (a p) n"), ckvT[:, 0:SEQ]
                              ).then_inc(kv_stored.sem, 16)
                act.dma_start(kr_d[bass.ds(row, 1)].rearrange("a p n -> (a p) n"), kr_raw[64:96, :]
                              ).then_inc(kv_stored.sem, 16)

                def exp(n):
                    br, hd, q = JOBS[n]
                    act.wait_ge(maxed.sem, maxed.at(layer, n + 1))
                    if n >= 3:
                        act.wait_ge(pT_psum.sem, pT_psum.at(layer, n - 2))
                    width = P if q == 0 else TOK
                    A(prob[:, n % 3, 0:width], ps[:, n % 3, 0:width], ACT.Exp, bias=stat[:, 2 + n % 3:3 + n % 3],
                      accum_out=stat[:, 5 + n % 3:6 + n % 3]).then_inc(exped.sem, 1)

                def copyT(n):
                    _, _, q = JOBS[n]
                    width = P if q == 0 else TOK
                    act.wait_ge(pT_psum.sem, pT_psum.at(layer, n + 1))
                    if n >= 2:
                        act.wait_ge(o_psum.sem, o_psum.at(layer, n - 1))
                    A(probT[:, n % 2, 0:width], ps[:, 3 + n % 2, 0:width], ACT.Copy).then_inc(pT_ready.sem, 1)

                for n in range(NJ + 2):
                    if n < NJ:
                        exp(n)
                        if n % 4 == 1:
                            ada_rows(chunk_of(layer, FT + n // 4), rows_next, ps[:, 7, 0:256])
                    if n >= 2:
                        copyT(n - 2)

                act.wait_ge(kv_stored.sem, kv_stored.at(layer, 64))

                def decays(rd):
                    act.wait_ge(cum_ready.sem, cum_ready.at(layer, rd + 1))
                    for d in range(2):
                        cs = ps[:, 4 + d, :].rearrange("p (a b c) -> p a b c", a=2, b=2)
                        A(E1[:, d].rearrange("p a b c -> p (a b c)"), ps[:, 4 + d, :], ACT.Exp, scale=-DECAY)
                        A(E2[:, d], cs[:, :, 0, :], ACT.Exp, scale=DECAY)
                        first = 0 if d == 0 else P - 1
                        last = A(pmid[:, 2 * d:2 * d + 2], cs[:, :, 1, first], ACT.Exp, scale=DECAY)
                    last.then_inc(exps_ready.sem, 1)

                decays(0)
                for rd in range(3):
                    act.wait_ge(kbt_psum.sem, kbt_psum.at(layer, rd + 1))
                    for d in range(2):
                        A(KBt[:, d, 0:256], ps[:, d, 0:256], ACT.Copy)
                        last = A(KBt[:, d, 256:512], ps[:, d, 256:512], ACT.Copy, scale=-1.0)
                    last.then_inc(kbt_ready.sem, 1)
                    for m in range(1, LEVELS):
                        for grp in range(2):
                            act.wait_ge(inv_psum.sem, inv_psum.at(layer, inv_x(rd, m, grp)))
                            A(X[:, 4 * grp:4 * grp + 4, :], ps[:, 2 + grp, :].rearrange("p (a b) -> p a b", b=P),
                              ACT.Copy).then_inc(x_ready.sem, 1)
                    if rd < 2:
                        decays(rd + 1)
                    if rd == 0:
                        act.wait_ge(round_done.sem, round_done.at(layer, 1))
                        act.dma_start(s_d[bass.ds(row, 1)].rearrange("a p t n -> (a p) t n"), s_out[:, :, :]
                                      ).then_inc(s_stored.sem, 16)
                act.wait_ge(s_stored.sem, s_stored.at(layer, 16))
                act.wait_ge(Y_psum.sem, Y_psum.at(layer, 1))
                A(Y[:, 0:2, :].rearrange("p a b -> p (a b)"), ps[:, 4, :], ACT.Copy)
                A(Y[:, 2, :], ps[:, 5, 0:256], ACT.Copy).then_inc(Y_ready.sem, 1)
                shift(layer, 1, 16, hB)
                for n in range(24):
                    split_through(layer, PA["gate0"] + n + 2)
                    act.wait_ge(piece_used.sem, piece_used.at(layer, PA["gate0"] + n + 1))
                    if n >= 4:
                        act.wait_ge(br_free.sem, br_free.at(layer, n - 3))
                    A(gsig[:, n % 4, :], ps[:, n % 4, 0:TOK], ACT.Sigmoid).then_inc(proj_done.sem, 1)
                    if n == 1:
                        act.wait_ge(gn_var.sem, gn_var.at(layer, 1))
                        A(stat2[:, 0:12], stat[:, 12:24], ACT.Sqrt, bias=epsgn, scale=1.0 / HD
                          ).then_inc(gn_root.sem, 1)
                    if n == 3:
                        act.wait_ge(br_psum.sem, br_psum.at(layer, 1))
                        A(oT[2][:, :, :], ps[:, 4:6, 0:TOK], ACT.Copy).then_inc(rwT_ready.sem, 1)
                    if n % 4 == 3:
                        for t in range(KT):
                            if (3 * t + 2) // 4 == n // 4:
                                act.wait_ge(comb_sum.sem, comb_sum.at(layer, t + 1))
                                A(hA[0][:, t, :], comb[:, t % 2, :], ACT.Copy).then_inc(comb_hi.sem, 1)
                for t in range(KT):
                    split_through(layer, PA["out"] + min(t + 2, KT))
                    if t == KT - 1:
                        load_sqrt()
                    act.wait_ge(out_free.sem, out_free.at(layer, t + 1))
                    square(layer, 2, t)
                split_through(layer, PA["out"] + KT + 1)
                take_root(layer, 2)
                shift(layer, 2, 24, hA)
                ffn(layer, 1)
                cursor[0] = 0

        @blk.vector
        def _(dve):
            v = nc.vector
            dve.sem_inc(up_free.sem, up_free.credit)
            dve.sem_inc(down_free.sem, down_free.credit)
            dve.sem_inc(mod_done.sem, mod_done.credit)
            dve.sem_inc(out_free.sem, out_free.credit)
            dve.wait_ge(const_landed.sem, 16)
            dve.wait_ge(x_landed.sem, 16)

            def inverse_root(layer, n):
                dve.wait_ge(root_ready.sem, root_ready.at(layer, n + 1))
                v.reciprocal(rinv[:, :], root)
                dve.drain()

            def normalise(layer, n, count, dst):
                for t in range(KT + 1):
                    if t < KT:
                        v.tensor_tensor(htmp[:, t % 3, :], x[:, t, :], rinv[:, :], ALU.mult
                                        ).then_inc(h_scaled.sem, 1)
                    if t:
                        dve.wait_ge(h_hi.sem, h_hi.at(layer, count + t))
                        if t % 2 == 0:
                            v.tensor_copy(dst[0][:, t - 1, :], htmp[:, (t - 1) % 3, :])
                            dve.drain()
                        v.tensor_tensor(dst[1][:, t - 1, :], htmp[:, (t - 1) % 3, :], dst[0][:, t - 1, :],
                                        ALU.subtract).then_inc(h_ready.sem, 1)
                        dve.drain()

            cursor = [0]

            def split_through(layer, n):
                while cursor[0] <= n:
                    m = cursor[0]
                    blk_, c0, c1 = PIECES[m]
                    slot = blk_ % SLOTS
                    dve.wait_ge(hi_ready.sem, hi_ready.at(layer, m + 1))
                    v.tensor_tensor(w_lo[:, m % 2, 0:c1 - c0], ring[:, slot, c0:c1],
                                    w_hi[:, m % 2, 0:c1 - c0], ALU.subtract).then_inc(split_ready.sem, 1)
                    if c0:
                        dve.drain().then_inc(slot_free[slot].sem, 1)
                    cursor[0] += 1

            def ada_cols(chunk, src):
                dve.wait_ge(cols_ready.sem, chunk + 1)
                v.tensor_tensor(mod_all[:, bass.ds(chunk * 4, 4)], src, C("ada_b")[:, bass.ds(chunk * 4, 4)],
                                ALU.add).then_inc(mod_done.sem, 1)

            def take_mod(layer, first, end):
                dve.drain()
                v.tensor_copy(mod[:, 16 * first:16 * end],
                              mod_all[:, bass.ds(layer * 144 + 16 * first, 16 * (end - first))])
                dve.drain()

            def scale_of(layer, n):
                v.scalar_tensor_tensor(out=scale_c[:, n].rearrange("p t c -> p (t c)"),
                                       in0=modv[:, 3 * n + 1].rearrange("p t c -> p (t c)"), scalar=1.0,
                                       in1=C("norm_g")[:, bass.ds(layer * 48 + 16 * n, 16)],
                                       op0=ALU.add, op1=ALU.mult)

            def gate_of(f):
                v.tensor_scalar(gate_c[:, f], modv[:, 6 * f + 2], 0.5, None, ALU.mult)

            def ffn(layer, f):
                for half in range(2):
                    p0 = PA[f"up{f}{half}"]
                    for t in range(HALF):
                        n = f * FT + half * HALF + t
                        split_through(layer, p0 + 2 * t + 3)
                        dve.wait_ge(silu_ready.sem, silu_ready.at(layer, n + 1))
                        v.tensor_tensor(product[:, t % 2, :], silu[:, t % 2, :],
                                        ps[:, t % 2 * 2 + 1, 0:TOK], ALU.mult).then_inc(up_free.sem, 1)
                        if f == 0:
                            ada_cols(chunk_of(layer, half * HALF + t), ps[:, 6 + t % 2, 0:4])
                        dve.wait_ge(hid_hi.sem, hid_hi.at(layer, n + 1))
                        v.tensor_tensor(hid[1][:, t, :], product[:, t % 2, :], hid[0][:, t, :], ALU.subtract
                                        ).then_inc(hid_ready.sem, 1)
                    if f == 0:
                        take_mod(layer, *((2, 3) if half == 0 else (3, 6)))
                        if half == 0:
                            gate_of(0)
                        else:
                            scale_of(layer, 1)
                        dve.drain()
                    p0 = PA[f"down{f}{half}"]
                    for t in range(KT):
                        split_through(layer, min(p0 + 2 * t + 3, p0 + 2 * KT, NPIECE - 1))
                        dve.wait_ge(piece_used.sem, piece_used.at(layer, p0 + 2 * t + 2))
                        for c, s0, s1 in SEGS:
                            last = v.scalar_tensor_tensor(out=x[:, t, s0:s1], in0=ps[:, 4 + t % 2, s0:s1],
                                                          scalar=gate_c[:, f, t, c:c + 1], in1=x[:, t, s0:s1],
                                                          op0=ALU.mult, op1=ALU.add)
                        last.then_inc(down_free.sem, 1)
                    split_through(layer, min(p0 + 2 * KT + 1, NPIECE - 1))

            with dve.Fori(0, TURN0) as i:
                for c in range(SLOTS):
                    ada_cols(i * SLOTS + c, ps[:, 6 + c % 2, 0:4])
            with dve.Fori(0, DEPTH) as layer:
                split_through(layer, 1)
                take_mod(layer, 0, 2)
                scale_of(layer, 0)
                dve.drain()
                inverse_root(layer, 0)
                normalise(layer, 0, 0, hA)
                ffn(layer, 0)
                dve.drain()
                inverse_root(layer, 1)
                normalise(layer, 1, 8, hA)
                split_through(layer, PA["v"] + 1)
                dve.wait_ge(proj_done.sem, proj_done.at(layer, 14))
                v.tensor_tensor(sq3[:, 0:2, :], dq, dq, ALU.mult)
                v.tensor_tensor(sq3[:, 2, :], ckvT[:, 0:TOK], ckvT[:, 0:TOK], ALU.mult).then_inc(mla_sq.sem, 1)
                split_through(layer, PA["v"] + 3)

                dve.wait_ge(small_landed.sem, small_landed.at(layer, 16))
                dve.wait_ge(mla_root.sem, mla_root.at(layer, 1))
                v.reciprocal(prod, prod)
                dve.drain()
                for z in range(2):
                    v.scalar_tensor_tensor(out=dq[:, z, :], in0=dq[:, z, :], scalar=S("qn")[:, z:z + 1],
                                           in1=prod[:, 0, :], op0=ALU.mult, op1=ALU.mult)
                v.scalar_tensor_tensor(out=ckvT[:, 0:TOK], in0=ckvT[:, 0:TOK], scalar=S("kvn"),
                                       in1=prod[:, 1, :], op0=ALU.mult, op1=ALU.mult
                                       ).then_inc(mla_normed.sem, 1)
                dve.wait_ge(piece_used.sem, piece_used.at(layer, PA["kr"] + 2))
                v.tensor_tensor(kpe[64:96, :], ps[64:96, 4, 0:TOK], C("rope")[64:96, :], ALU.mult)
                v.tensor_tensor(ropes[64:96, 0, :], ps[96:128, 4, 0:TOK], C("rope")[96:128, :], ALU.mult)
                dve.drain()
                v.tensor_tensor(kpe[64:96, :], kpe[64:96, :], ropes[64:96, 0, :], ALU.add)
                dve.drain()
                for hd in range(HEADS):
                    v.tensor_copy(KTm[64:96, hd, 0:TOK], kpe[64:96, :])
                    v.tensor_copy(KTm[64:96, hd, TOK:KEYS], S("krope")[64:96, :])
                dve.drain()
                v.tensor_copy(kr_raw[64:96, :], ps[64:96, 4, 0:SEQ])
                for z in range(2):
                    v.tensor_copy(kT[:, z, TOK:KEYS], S("na_k", P)[:, z, :])
                v.tensor_copy(ckvT[:, TOK:KEYS], S("ckv"))
                dve.wait_ge(piece_used.sem, piece_used.at(layer, PA["v"] + 4))
                for j in range(3):
                    last = v.tensor_copy(V[:, j, :], ps[:, 5 + j, :])
                last.then_inc(v_done.sem, 1)
                for p in range(2):
                    v.tensor_scalar(kk[:, p, :], k[:, p, :], S("kk")[:, p:p + 1], None, ALU.mult)
                dve.drain()
                v.tensor_tensor(oT[0][:, :, :], kk[:, :, :], kk[:, :, :], ALU.mult).then_inc(kksq_ready.sem, 1)
                split_through(layer, PA["gate0"] + 1)
                dve.wait_ge(q_psum.sem, q_psum.at(layer, 1))
                for hd in range(HEADS):
                    for dst, at in ((qm, 64), (ropes, 96)):
                        last = v.scalar_tensor_tensor(out=dst[64:96, hd, :], in0=ps[at:at + 32, hd, 0:TOK],
                                                      scalar=Q_SCALE, in1=C("rope")[at:at + 32, :],
                                                      op0=ALU.mult, op1=ALU.mult)
                last.then_inc(q_turned.sem, 1)
                dve.drain()
                v.tensor_tensor(qm[64:96, :, :], qm[64:96, :, :], ropes[64:96, :, :], ALU.add)
                dve.wait_ge(a_done.sem, a_done.at(layer, 1))
                v.tensor_scalar(stat[:, 0:2], S("ka"), -1.0, 1.0, ALU.mult, ALU.add)
                dve.drain()
                for d in range(2):
                    for p in range(2):
                        v.tensor_scalar(kd[:, d, p, :], b[:, d, p, :], S("ka")[:, p:p + 1], stat[:, p:p + 1],
                                        ALU.mult, ALU.add)
                dve.drain()
                for d in range(2):
                    v.tensor_tensor(kd[:, d], kd[:, d], k[:, :, :], ALU.mult)
                dve.wait_ge(wlog_ready.sem, wlog_ready.at(layer, 1))
                for j in range(3):
                    last = v.tensor_tensor(sig[:, j, :], ps[:, j, :], S("w0"), ALU.add)
                last.then_inc(wlog_biased.sem, 1)
                dve.drain()
                v.tensor_tensor(bonus_in[:, :, :], kd[:, 0], kd[:, 1], ALU.add)
                dve.drain()
                for p in range(2):
                    last = v.scalar_tensor_tensor(out=bonus_in[:, p, :], in0=bonus_in[:, p, :],
                                                  scalar=S("rk")[:, p:p + 1], in1=r[:, p, :],
                                                  op0=ALU.mult, op1=ALU.mult)
                last.then_inc(prod_ready.sem, 1)
                dve.wait_ge(kkss_ready.sem, kkss_ready.at(layer, 1))
                v.tensor_scalar(root2, ps[:, 2:4, 0:TOK], 1e-24, None, ALU.max).then_inc(kkmax_ready.sem, 1)
                dve.wait_ge(kkroot_ready.sem, kkroot_ready.at(layer, 1))
                v.reciprocal(root2, root2)
                dve.drain()
                v.tensor_tensor(kk[:, :, :], kk[:, :, :], root2, ALU.mult)
                dve.drain()
                for d in range(2):
                    v.tensor_tensor(b[:, d], b[:, d], kk[:, :, :], ALU.mult)

                def top(n):
                    br, hd, q = JOBS[n]
                    dve.wait_ge(scored.sem, scored.at(layer, n + 1))
                    src = ps[:, n % 3, 0:P if q == 0 else TOK]
                    if br == 0 and q > 0:
                        if n == 1:
                            dve.wait_ge(bias_ready.sem, bias_ready.at(layer, 1))
                        v.tensor_tensor(src, src, S("bias", TOK)[:, (q - 1) * 4 + hd, :], ALU.add)
                        dve.drain()
                    v.tensor_reduce(stat[:, 2 + n % 3:3 + n % 3], src, AX, ALU.max, negate=True
                                    ).then_inc(maxed.sem, 1)

                def share(n):
                    width = P if JOBS[n][2] == 0 else TOK
                    dve.wait_ge(exped.sem, exped.at(layer, n + 1))
                    v.reciprocal(stat[:, 8 + n % 2:9 + n % 2], stat[:, 5 + n % 3:6 + n % 3])
                    dve.drain()
                    v.tensor_scalar(prob[:, n % 3, 0:width], prob[:, n % 3, 0:width],
                                    stat[:, 8 + n % 2:9 + n % 2], None, ALU.mult).then_inc(normed.sem, 1)

                def keep(n):
                    br, hd, q = JOBS[n]
                    o = 64 * (hd % 2)
                    dve.wait_ge(o_psum.sem, o_psum.at(layer, n + 1))
                    v.tensor_copy(oT[br][o:o + 64, hd // 2, q * P:(q + 1) * P], ps[o:o + 64, 5 + n % 2, 0:P]
                                  ).then_inc(o_done.sem, 1)

                for n in range(NJ + 3):
                    if n < NJ:
                        top(n)
                        if n == 0:
                            dve.wait_ge(bonus_psum.sem, bonus_psum.at(layer, 1))
                            v.tensor_copy(bonus[:, :], ps[:, 7, 0:12]).then_inc(bonus_done.sem, 1)
                    if n and n % 4 == 0:
                        ada_cols(chunk_of(layer, FT + n // 4 - 1), ps[:, 7, 256:260])
                    if 1 <= n <= NJ:
                        share(n - 1)
                    if n >= 3:
                        keep(n - 3)

                def factors(rd):
                    dve.wait_ge(exps_ready.sem, exps_ready.at(layer, rd + 1))
                    for d in range(2):
                        c0, c1 = ROUNDS[rd][d] * P, (ROUNDS[rd][d] + 1) * P
                        at_end = P - 1 if d == 0 else 0
                        for hh in range(2):
                            o, e = 64 * hh, 64 * hh + 64
                            for z, src in enumerate((kk, r)):
                                v.tensor_tensor(KR[o:e, 2 * d:2 * d + 2, hh, z, :], src[o:e, :, c0:c1],
                                                E1[o:e, d, :, 1 - z, :], ALU.mult)
                        v.tensor_copy(pend[:, rd % 2, d, :], E1[:, d, :, 0, at_end])
                        v.tensor_tensor(KB[:, d, :, 0, :], kd[:, d, :, c0:c1], E2[:, d], ALU.mult)
                        last = v.tensor_tensor(KB[:, d, :, 1, :], b[:, d, :, c0:c1], E2[:, d], ALU.mult)
                    last.then_inc(factors_ready.sem, 1)

                for hh in range(2):
                    o = 64 - 64 * hh
                    v.memset(KR[o:o + 64, :, hh].rearrange("p a b c -> p a (b c)"), 0.0)
                factors(0)
                v.memset(s_in[:, :, :], 0.0).then_inc(state_ready.sem, 1)
                for rd, tiles in enumerate(ROUNDS):
                    for u, (d, p, z) in enumerate(UNITS):
                        dve.wait_ge(gram_psum.sem, gram_psum.at(layer, 8 * rd + u + 1))
                        v.tensor_tensor(G[:, 4 * d + 2 * p:4 * d + 2 * p + 2, 2 * z:2 * z + 2, :].rearrange(
                                            "p h a b -> p h (a b)"),
                                        ps[:, (u + 2) % 8, :].rearrange("p (h a) -> p h a", h=2),
                                        bcast(C(f"gram{d}")[:, z * 256:(z + 1) * 256], 2),
                                        ALU.mult).then_inc(gram_masked.sem, 1)
                        if u % 4 == 3:
                            dve.drain()
                            v.tensor_tensor(Nm[:, 0, u - 3:u + 1, :], G[:, u - 3:u + 1, 2, :],
                                            bcast(C(f"level{d}", P)[:, 0, :], 4), ALU.mult
                                            ).then_inc(level0_masked.sem, 1)
                    for m in range(LEVELS):
                        for grp in range(2):
                            sl = slice(4 * grp, 4 * grp + 4)
                            pv = lambda bank: ps[:, bank, :].rearrange("p (a b) -> p a b", b=P)
                            if m == 0:
                                eye = bcast(ident, 4)
                                dve.wait_ge(inv_psum.sem, inv_psum.at(layer, inv_x(rd, m, grp)))
                                v.tensor_tensor(T[:, sl, :], pv(2 + grp), eye, ALU.add)
                                v.tensor_tensor(Tt[:, sl, :], Nm[:, 0, sl, :], eye, ALU.add
                                                ).then_inc(t_ready.sem, 1)
                                continue
                            dve.wait_ge(inv_psum.sem, inv_psum.at(layer, inv_tt(rd, m, grp)))
                            if m < LEVELS - 1:
                                v.tensor_tensor(T[:, sl, :], T[:, sl, :], pv(4 + grp), ALU.add)
                            v.tensor_tensor(Tt[:, sl, :], Tt[:, sl, :], pv(6 + grp), ALU.add
                                            ).then_inc(t_ready.sem, 1)
                        if m == 0:
                            dve.drain()
                        if m == 1:
                            dve.wait_ge(f_psum.sem, f_psum.at(layer, rd + 1))
                            v.tensor_copy(Ft.rearrange("p a b -> p (a b)"), ps[:, 0, :]
                                          ).then_inc(ft_ready.sem, 1)
                        if m == 2:
                            dve.wait_ge(ft_psum.sem, ft_psum.at(layer, rd + 1))
                            v.tensor_copy(Fm.rearrange("p a b -> p (a b)"), ps[:, 1, :]
                                          ).then_inc(f_ready.sem, 1)
                    for grp in range(2):
                        dve.wait_ge(u_psum.sem, u_psum.at(layer, 2 * rd + grp + 1))
                        v.tensor_copy(Um[:, 4 * grp:4 * grp + 4, :].rearrange("p a b -> p (a b)"),
                                      ps[:, 2 + grp, 0:256]).then_inc(u_ready.sem, 1)
                    if rd < 2:
                        factors(rd + 1)
                    dve.drain()
                    dve.wait_ge(y_psum.sem, y_psum.at(layer, rd + 1))
                    if rd < 2:
                        s_new = (s_out, s_mid)[rd]
                        v.tensor_tensor(s_new[:, :, :].rearrange("p a b -> p (a b)"), ps[:, 7, 0:256],
                                        s_in[:, :, :].rearrange("p a b -> p (a b)"), ALU.add)
                    for d in range(2):
                        if d == 1 or rd < 2:
                            dve.drain()
                        src = ps[:, 0, 2 * d * P:2 * (d + 1) * P].rearrange("p (a b) -> p a b", b=P)
                        dst = oT[2][:, :, tiles[d] * P:(tiles[d] + 1) * P]
                        if rd == 2 or (rd == 0 and d == 1):
                            v.tensor_tensor(dst, dst, src, ALU.add)
                        else:
                            v.tensor_copy(dst, src)
                    if rd < 2:
                        for z in range(4):
                            last = v.tensor_scalar(s_new[:, z, :], s_new[:, z, :],
                                                   pend[:, rd, z // 2, z % 2:z % 2 + 1], None, ALU.mult)
                        last.then_inc(round_done.sem, 1)
                        dve.drain()
                        for z in range(4):
                            src = S("state", HD)[:, z, :] if rd == 0 else s_mid[:, z, :]
                            last = v.tensor_scalar(s_in[:, z, :], src, pmid[:, z:z + 1], None, ALU.mult)
                        last.then_inc(state_ready.sem, 1)
                    else:
                        dve.drain().then_inc(round_done.sem, 1)

                normalise(layer, 1, 16, hB)
                split_through(layer, PA["gate0"] + 2)
                Yh = Y[:, :, :].rearrange("p a (h c) -> p (a h) c", c=HD)
                sqY, bv = view(tmp, 0, 12, HD), view(tmp, 768, 3, 256)
                dve.wait_ge(Y_ready.sem, Y_ready.at(layer, 1))
                v.tensor_reduce(stat[:, 12:24], Yh, AX, ALU.add)
                dve.drain()
                v.tensor_scalar(stat[:, 12:24], stat[:, 12:24], 1.0 / HD, None, ALU.mult)
                dve.drain()
                v.tensor_tensor(Yh, Yh, spread(stat[:, 12:24], HD), ALU.subtract)
                dve.drain()
                v.tensor_tensor(sqY, Yh, Yh, ALU.mult)
                dve.drain()
                v.tensor_reduce(stat[:, 12:24], sqY, AX, ALU.add).then_inc(gn_var.sem, 1)
                for j in range(3):
                    v.tensor_tensor(bv[:, j, :].rearrange("p (h c) -> p h c", c=HD),
                                    V[:, j, 256:512].rearrange("p (h c) -> p h c", c=HD),
                                    spread(bonus[:, 4 * j:4 * j + 4], HD), ALU.mult)
                split_through(layer, PA["gate0"] + 3)
                dve.wait_ge(gn_root.sem, gn_root.at(layer, 1))
                v.reciprocal(stat2[:, 12:24], stat2[:, 0:12])
                dve.drain()
                v.tensor_tensor(Yh, Yh, spread(stat2[:, 12:24], HD), ALU.mult)
                dve.drain()
                v.tensor_tensor(Y[:, :, :], Y[:, :, :], bcast(S("gnw"), 3), ALU.mult)
                dve.drain()
                split_through(layer, PA["gate0"] + 4)
                v.tensor_tensor(Y[:, :, :], Y[:, :, :], bcast(S("gnb"), 3), ALU.add)
                dve.drain()
                v.tensor_tensor(Y[:, :, :], Y[:, :, :], bv, ALU.add)
                dve.drain()
                v.tensor_tensor(Y[:, :, :], Y[:, :, :], g[:, :, :], ALU.mult).then_inc(rw_out.sem, 1)

                for q in range(6):
                    split_through(layer, PA["gate0"] + 4 * q + 5)
                    for n in range(4 * q, 4 * q + 4):
                        t, br = n // 3, n % 3
                        dve.drain()
                        dve.wait_ge(proj_done.sem, proj_done.at(layer, 14 + n + 1))
                        dve.wait_ge(br_psum.sem, br_psum.at(layer, 1 + n + 1))
                        v.tensor_tensor(comb[:, t % 2, :] if br == 0 else brtmp[:, n % 2, :],
                                        ps[:, 4 + n % 4, 0:TOK], gsig[:, n % 4, :], ALU.mult
                                        ).then_inc(br_free.sem, 1)
                        if n % 4 == 3:
                            dve.drain().then_inc(slot_free[AT[f"branch{q}"] % SLOTS].sem, 1)
                        if br:
                            dve.drain()
                            last = v.tensor_tensor(comb[:, t % 2, :], comb[:, t % 2, :], brtmp[:, n % 2, :],
                                                   ALU.add)
                            if br == 2:
                                last.then_inc(comb_sum.sem, 1)
                    for t in range(KT):
                        if (3 * t + 2) // 4 == q:
                            dve.wait_ge(comb_hi.sem, comb_hi.at(layer, t + 1))
                            v.tensor_tensor(hA[1][:, t, :], comb[:, t % 2, :], hA[0][:, t, :], ALU.subtract
                                            ).then_inc(comb_ready.sem, 1)
                take_mod(layer, 6, 9)
                scale_of(layer, 2)
                gate_of(1)
                for t in range(KT):
                    split_through(layer, PA["out"] + min(t + 2, KT))
                    dve.wait_ge(piece_used.sem, piece_used.at(layer, PA["out"] + t + 1))
                    for c, s0, s1 in SEGS:
                        last = v.scalar_tensor_tensor(out=x[:, t, s0:s1], in0=ps[:, t % 4, s0:s1],
                                                      scalar=modv[:, 5, t, c:c + 1], in1=x[:, t, s0:s1],
                                                      op0=ALU.mult, op1=ALU.add)
                    last.then_inc(out_free.sem, 1)
                split_through(layer, PA["out"] + KT + 1)
                inverse_root(layer, 2)
                normalise(layer, 2, 24, hA)
                ffn(layer, 1)
                cursor[0] = 0
                dve.drain()
            inverse_root(DEPTH, 0)
            for t in range(KT):
                last = v.scalar_tensor_tensor(out=x[:, t, :], in0=x[:, t, :], scalar=C("final_g")[:, t:t + 1],
                                              in1=rinv[:, :], op0=ALU.mult, op1=ALU.mult)
            last.then_inc(y_ready.sem, 1)

        @blk.gpsimd
        def _(pool):
            g_ = nc.gpsimd

            def add_squares(layer, n):
                for t in range(1, KT - 1):
                    if t > 1:
                        pool.drain()
                    pool.wait_ge(sq_ready.sem, sq_ready.at(layer, 8 * n + t + 1))
                    g_.tensor_tensor(sq_sum, sq_sum if t > 1 else sq[:, 0, :], sq[:, t % 2, :], ALU.add
                                     ).then_inc(sq_added.sem, 1)

            add_squares(0, 0)
            with pool.Fori(0, DEPTH) as layer:
                add_squares(layer, 1)
                pool.wait_ge(const_landed.sem, 16)
                pool.wait_ge(small_landed.sem, small_landed.at(layer, 16))
                for n in range(8):
                    tab = S("bias", TOK)[:, n, 0:256].rearrange("p (a b) -> p a b", b=64)
                    last = g_.tensor_tensor(tab, tab, bcast(C("okcol"), 4), ALU.mult)
                pool.drain()
                for n in range(8):
                    tab = S("bias", TOK)[:, n, 0:256].rearrange("p (a b) -> p a b", b=64)
                    last = g_.tensor_tensor(tab, tab, bcast(C("negcol"), 4), ALU.add)
                last.then_inc(bias_ready.sem, 1)
                for rd in range(3):
                    for m in range(1, LEVELS):
                        for grp in range(2):
                            if m == 1:
                                pool.wait_ge(gram_masked.sem, gram_masked.at(layer, 8 * rd + 4 * grp + 4))
                                if rd == 0:
                                    pool.wait_ge(exps_ready.sem, exps_ready.at(layer, 1))
                            if m >= 2:
                                pool.wait_ge(inv_psum.sem, inv_psum.at(layer, inv_x(rd, m - 2, grp)))
                                pool.wait_ge(t_ready.sem, t_ready.at(layer, lev(rd, m - 2, grp)))
                            g_.tensor_tensor(Nm[:, m % 2, 4 * grp:4 * grp + 4, :],
                                             G[:, 4 * grp:4 * grp + 4, 2, :],
                                             bcast(C(f"level{grp}", P)[:, m, :], 4), ALU.mult
                                             ).then_inc(level_masked.sem, 1)
                add_squares(layer, 2)
                add_squares(layer, 3)


def packed(where, width, lead=()):
    a = np.zeros((*lead, P, width), np.float32)

    def put(name, v):
        lo, hi = where[name]
        v = np.asarray(v)
        v = v.reshape(*v.shape[:len(lead) + 1], -1)
        a[..., lo:lo + v.shape[-1]] = v
        assert v.shape[-1] <= hi - lo
    return a, put


def shape_constants():
    i = np.arange(P)
    s, t = i[:, None], i[None, :]
    out = {"ident": np.eye(P), "ones": np.ones((P, P)), "block": s // 64 == t // 64}
    for d in range(2):
        before = (s < t) if d == 0 else (s > t)
        upto = (s <= t) if d == 0 else (s >= t)
        mid = (s < 64) if d == 0 else (s >= 64)
        out[f"cum{d}"] = np.concatenate([upto * 1.0 - mid, before * 1.0 - mid], 1)
        out[f"gram{d}"] = np.concatenate([before * 1.0, upto * 1.0, before * -1.0, upto * -1.0], 1)
        levels = []
        for lv in range(LEVELS):
            m = 1 << lv
            half_s, half_t = s // m % 2, t // m % 2
            levels.append((s // (2 * m) == t // (2 * m)) & ((half_s == d) & (half_t == 1 - d)))
        out[f"level{d}"] = np.stack(levels, 1)
    heads = np.zeros((P, 2, 4))
    for p in range(2):
        for hh in range(2):
            heads[64 * hh:64 * hh + 64, p, 2 * p + hh] = 1
    out["heads"] = heads
    qc, kc = i % 64, np.arange(64)
    lo = np.clip(qc - 8, 0, 48)[:, None]
    ok = (kc[None] >= lo) & (kc[None] < lo + 16)
    out["okcol"], out["negcol"] = ok, np.where(ok, 0.0, -1e30)
    n_freq = ROPE // 4
    inv = 1.0 / (10000.0 ** (np.arange(n_freq) / n_freq))
    pos = np.arange(DEC)
    ang = np.concatenate([(pos // 64)[:, None] * inv, (pos % 64)[:, None] * inv], -1).T
    rope = np.zeros((P, TOK))
    rope[64:96, 0:SEQ] = 1
    rope[64:96, SEQ:] = np.concatenate([np.cos(ang)] * 2)
    rope[96:112, SEQ:], rope[112:128, SEQ:] = -np.sin(ang), np.sin(ang)
    out["rope"] = rope
    pick = np.zeros((P, 2))
    pick[0::32, 0] = pick[1::32, 1] = 1
    out["pick"] = pick
    out["eps"] = np.tile([1e-6, 64e-5, 0, 0], (P, 1))
    return out


def by_feature(v, lead):
    return np.swapaxes(v.reshape(*v.shape[:lead], -1, P), -1, -2)


def weight_stream(w):
    out = np.zeros((ADA0 + DEPTH * NBLK, P, WIDE), np.float32)
    ada = w["ada_w"].reshape(DEPTH, KT, P, ADA, 256).transpose(0, 3, 2, 1, 4).reshape(DEPTH * ADA, P, WIDE)
    for n in range(DEPTH * ADA):
        layer, j = divmod(n - ADA0, ADAL)
        half, i = divmod(j, HALF)
        at = AT[f"up0{half}"] + 2 * i if half < 2 else AT["ada_next"] + j - FT
        out[n if n < ADA0 else ADA0 + layer * NBLK + at] = ada[n]
    for layer in range(DEPTH):
        def put(name, i, v):
            v = v.reshape(P, -1)
            out[ADA0 + layer * NBLK + AT[name] + i, :, 0:v.shape[1]] = v

        def tiles(m):
            return m.reshape(m.shape[0] // P, P, m.shape[1] // P, P).transpose(1, 2, 0, 3)

        for f in range(2):
            wg, wu = tiles(w["ffn_wg"][layer, f]), tiles(w["ffn_wu"][layer, f])
            wd = tiles(w["ffn_wd"][layer, f])
            for half in range(2):
                for t in range(HALF):
                    n = half * HALF + t
                    put(f"up{f}{half}", 2 * t + 1 if f == 0 else t, np.stack([wg[:, n], wu[:, n]], 1))
                for t in range(KT):
                    put(f"down{f}{half}", t, wd[:, t, HALF * half:HALF * half + HALF])
        w_in = w["w_in"][layer]
        feat = tiles(np.concatenate([w_in[:, 0:512], w_in[:, 768:1280], w_in[:, 1536:2304]], 1))
        for i in range(7):
            put("proj", i, feat[:, 2 * i:2 * i + 2])
        kr = w_in[:, 2304:2336]
        put("kr", 0, tiles(np.concatenate([np.zeros((D, 64), np.float32), kr, swap_halves(kr)], 1)))
        vals = np.concatenate([w_in[:, 512:768], w_in[:, 1280:1536]], 1).reshape(KT, P, 512)
        for half in range(2):
            put("v", half, vals[4 * half:4 * half + 4].transpose(1, 0, 2))
        gates = tiles(w_in[:, 2336:])
        order = [br * KT + t for t in range(KT) for br in range(3)]
        for i in range(12):
            put(f"gate{i}", 0, gates[:, order[2 * i:2 * i + 2]])
        br = np.stack([tiles(w["w_br"][layer, n]) for n in range(3)], 2).reshape(P, 24, 2, P)
        for i in range(6):
            put(f"branch{i}", 0, br[:, 4 * i:4 * i + 4])
        wo = tiles(w["w_o"][layer])
        for i in range(4):
            put("out", i, wo[:, 2 * i:2 * i + 2])
    return out


def swap_halves(a):
    return np.concatenate([a[..., ROPE // 2:], a[..., :ROPE // 2]], -1)


def small_weights(w):
    a, put = packed(SMALL, NSMALL, (DEPTH,))
    L = DEPTH
    put("kk", by_feature(w["rw_kk"], 1))
    put("ka", by_feature(w["rw_ka"], 1))
    put("rk", by_feature(w["rw_rk"].reshape(L, 256), 1))
    put("a0", by_feature(w["rw_a0"].reshape(L, 512), 1))
    put("qn", by_feature(w["mla_qn_g"], 1))
    put("kvn", by_feature(w["mla_kvn_g"], 1))
    for name in ("w2", "a2"):
        both = np.zeros((L, 2, 64, 2, 256), np.float32)
        for d in range(2):
            both[:, d, :, d] = w[f"rw_{name}"].reshape(L, 2, 64, 256)[:, d]
        put(name, both.reshape(L, P, 512))
    put("g2", w["rw_g2"])
    for name, v in (("w0", w["rw_w0"].reshape(L, 1, 512)), ("gnw", w["rw_gn_w"][:, None]),
                    ("gnb", w["rw_gn_b"][:, None])):
        put(name, np.broadcast_to(v, (L, P, v.shape[-1])))
    uq = w["mla_w_uq"].reshape(L, 2, P, 4, NOPE + ROPE)
    put("uq", np.concatenate([uq, swap_halves(uq[..., NOPE:])], -1).transpose(0, 2, 1, 3, 4))
    ukv = w["mla_w_ukv"].reshape(L, P, 4, 2, 64)
    put("ukv_k", ukv[:, :, :, 0])
    put("ukv_v", ukv[:, :, :, 1])
    nk = w["cache_na_k"][0].reshape(L, 2, 2, P, HD)
    put("na_k", nk.transpose(0, 2, 4, 1, 3).reshape(L, P, 256))
    put("na_v", w["cache_na_v"][0].transpose(0, 2, 1, 3).reshape(L, P, 256))
    put("ckv", w["cache_mla_ckv"][0].transpose(0, 2, 1))
    lo = SMALL["krope"][0]
    a[:, 64:96, lo:lo + P] = w["cache_mla_krope"][0].transpose(0, 2, 1)
    st = np.stack([w["state_rwkv_fwd"][0], w["state_rwkv_bwd"][0]], 1).reshape(L, 2, 2, 2, HD, HD)
    put("state", st.transpose(0, 3, 5, 1, 2, 4).reshape(L, P, 256))
    q, n = np.arange(DEC), np.arange(DEC)
    row = n[None] // 64 - q[:, None] // 64 + 7
    col = np.clip(n[None] % 64 - q[:, None] % 64 + 15, 0, 30)
    tab = w["na_rpb"][:, :, row, col].reshape(L, 4, 2, P, DEC)
    full = np.zeros((L, P, 2, 4, TOK), np.float32)
    full[..., 0:DEC] = tab.transpose(0, 3, 2, 1, 4)
    put("bias", full)
    return a


def constants(w):
    a, put = packed(CONST, NCONST)
    for name, v in shape_constants().items():
        put(name, v)
    put("final_g", by_feature(w["final_g"], 0))
    cond = np.zeros((P, KT, 32), np.float32)
    cond[:, :, 0], cond[:, :, 1] = by_feature(w["c_ctx"], 0), by_feature(w["c"][0], 0)
    put("cond", cond)
    put("ada_b", np.repeat(by_feature(w["ada_b"], 1).transpose(1, 0, 2)[..., None], 2, -1))
    put("norm_g", np.repeat(by_feature(w["norm_g"], 2).transpose(2, 0, 1, 3)[..., None], 2, -1))
    return a


_OUTS = [("y", (P, KT, TOK)), ("k", (DEPTH, P, 2, SEQ)), ("v", (DEPTH, P, 256)),
         ("ckv", (DEPTH, P, SEQ)), ("kr", (DEPTH, ROPE, SEQ)), ("s", (DEPTH, P, 4, HD))]


def kernel(**inputs):
    import concourse.bacc as _bacc
    from concourse.bass_utils import run_bass_kernel_spmd as _run

    w = {name: np.asarray(a) for name, a in inputs.items()}
    tokens = np.concatenate([w["x_prompt"][0], w["x_sample"][0]], 0)
    arrays = {
        "wstream": weight_stream(w),
        "small_d": small_weights(w),
        "const_d": constants(w),
        "x_d": np.ascontiguousarray(tokens.T.reshape(KT, P, TOK).transpose(1, 0, 2)),
    }
    nc = _bacc.Bacc("TRN2", target_bir_lowering=False, num_devices=1)
    f32 = mybir.dt.float32
    args = [nc.dram_tensor(n, a.shape, f32, kind="ExternalInput").ap() for n, a in arrays.items()]
    args += [nc.dram_tensor(f"out_{n}", s, f32, kind="ExternalOutput").ap() for n, s in _OUTS]
    hybrid_step(nc, *args)
    res = _run(nc, [arrays], core_ids=[0]).results[0]
    y, k, v, ckv, kr, s = (res[f"out_{n}"] for n, _ in _OUTS)
    y = y.transpose(2, 1, 0).reshape(TOK, D)
    k = k.reshape(DEPTH, 2, HD, 2, SEQ).transpose(0, 3, 1, 4, 2).reshape(1, DEPTH, HEADS, SEQ, HD)
    v = v.reshape(DEPTH, SEQ, HEADS, HD).transpose(0, 2, 1, 3)[None]
    s = s.reshape(DEPTH, 2, HD, 2, 2, HD).transpose(3, 0, 4, 1, 5, 2).reshape(2, 1, DEPTH, HEADS, HD, HD)
    return (y[None, 0:SEQ], y[None, SEQ:], k, v, ckv.transpose(0, 2, 1)[None],
            kr.transpose(0, 2, 1)[None], s[0], s[1])
```
